# Optimizing a Trainium2 kernel written in Bass

```python
import math
import jax
import jax.numpy as jnp
from jax import lax
import numpy as np
import jax, jax.numpy as jnp

D_MODEL = 1024
BATCH = 1
SEQ = 256
DEPTH = 2

GRID_W = 64
CTX_LEN = 256
N_MIXERS = 3
EXPAND = 2
E_WIDTH = EXPAND * D_MODEL
HEAD_DIM = 128
N_Q_HEADS = E_WIDTH // HEAD_DIM
N_KV_HEADS = max(1, N_Q_HEADS // 4)
Q_PER_KV = N_Q_HEADS // N_KV_HEADS
KV_WIDTH = N_KV_HEADS * HEAD_DIM
WINDOW = 128
ATTN_BLOCK = 128
ROPE_THETA = 10000.0
S5_GROUP = 16
S5_GROUPS = E_WIDTH // S5_GROUP
S5_STATE = 64
S5_CHUNK = 128
HG_HEAD_DIM = 128
HG_HEADS = E_WIDTH // HG_HEAD_DIM
HG_CHUNK = 64
ATTN_IN = 2 * E_WIDTH + 2 * KV_WIDTH
S5_IN = 2 * E_WIDTH
HG_IN = 5 * E_WIDTH
NORM_EPS = 1e-5
NEG_INF = -1e30


def layer_norm(x, g, b):
    xf = x.astype(jnp.float32)
    mu = jnp.mean(xf, -1, keepdims=True)
    var = jnp.mean(jnp.square(xf - mu), -1, keepdims=True)
    y = (xf - mu) * lax.rsqrt(var + NORM_EPS) * g.astype(jnp.float32) + b.astype(jnp.float32)
    return y.astype(x.dtype)

def grid_positions(n_tokens):
    rows = n_tokens // GRID_W
    row = jnp.repeat(jnp.arange(rows, dtype=jnp.float32), GRID_W)
    col = jnp.tile(jnp.arange(GRID_W, dtype=jnp.float32), rows)
    return row, col

def rope_2d(x, row, col):
    half = x.shape[-1] // 2
    nf = half // 2
    inv_freq = jnp.power(ROPE_THETA, -jnp.arange(nf, dtype=jnp.float32) / nf)
    xf = x.astype(jnp.float32)

    def rotate(xp, pos):
        ang = pos[:, None] * inv_freq[None, :]
        cos = jnp.cos(ang)[None, :, None, :]
        sin = jnp.sin(ang)[None, :, None, :]
        x1, x2 = xp[..., :nf], xp[..., nf:]
        return jnp.concatenate([x1 * cos - x2 * sin, x2 * cos + x1 * sin], -1)

    return jnp.concatenate([rotate(xf[..., :half], row), rotate(xf[..., half:], col)], -1).astype(x.dtype)

def softmax_with_sink(s, sink):
    sk = jnp.broadcast_to(sink[None, :, :, None, None], s.shape[:-1] + (1,))
    return jax.nn.softmax(jnp.concatenate([s, sk], -1), axis=-1)[..., :-1]

def attention_mixer(p, pc, sink, row, col, ctx_out):
    bsz, n_lat, _ = p.shape
    n_ctx = pc.shape[1]

    def split(t):
        b_, l_ = t.shape[0], t.shape[1]
        q = t[..., :E_WIDTH].reshape(b_, l_, N_Q_HEADS, HEAD_DIM)
        k = t[..., E_WIDTH:E_WIDTH + KV_WIDTH].reshape(b_, l_, N_KV_HEADS, HEAD_DIM)
        v = t[..., E_WIDTH + KV_WIDTH:].reshape(b_, l_, N_KV_HEADS, HEAD_DIM)
        return q, k, v

    q, k, v = split(p)
    qc, kc, vc = split(pc)
    q = rope_2d(q, row, col).reshape(bsz, n_lat, N_KV_HEADS, Q_PER_KV, HEAD_DIM)
    k = rope_2d(k, row, col)
    qc = qc.reshape(bsz, n_ctx, N_KV_HEADS, Q_PER_KV, HEAD_DIM)
    scale = HEAD_DIM ** -0.5
    sink_r = sink.astype(jnp.float32).reshape(N_KV_HEADS, Q_PER_KV)

    n_blk = n_lat // ATTN_BLOCK
    n_key = ATTN_BLOCK + 2 * WINDOW
    qb = q.reshape(bsz, n_blk, ATTN_BLOCK, N_KV_HEADS, Q_PER_KV, HEAD_DIM).swapaxes(0, 1)
    pad = ((0, 0), (WINDOW, WINDOW), (0, 0), (0, 0))
    kp = jnp.pad(k, pad)
    vp = jnp.pad(v, pad)
    q_off = jnp.arange(ATTN_BLOCK)
    k_off = jnp.arange(n_key) - WINDOW

    def block(args):
        j, qj = args
        start = j * ATTN_BLOCK
        kj = lax.dynamic_slice_in_dim(kp, start, n_key, axis=1)
        vj = lax.dynamic_slice_in_dim(vp, start, n_key, axis=1)
        qpos = start + q_off
        kpos = start + k_off
        valid = ((jnp.abs(qpos[:, None] - kpos[None, :]) <= WINDOW)
                 & (kpos >= 0)[None, :] & (kpos < n_lat)[None, :])
        s_win = jnp.einsum('bqhgd,bkhd->bhgqk', qj, kj, preferred_element_type=jnp.float32) * scale
        s_win = jnp.where(valid, s_win, NEG_INF)
        s_ctx = jnp.einsum('bqhgd,bchd->bhgqc', qj, kc, preferred_element_type=jnp.float32) * scale
        pr = softmax_with_sink(jnp.concatenate([s_win, s_ctx], -1), sink_r).astype(vj.dtype)
        return (jnp.einsum('bhgqk,bkhd->bqhgd', pr[..., :n_key], vj)
                + jnp.einsum('bhgqc,bchd->bqhgd', pr[..., n_key:], vc))

    o = lax.map(block, (jnp.arange(n_blk), qb)).swapaxes(0, 1).reshape(bsz, n_lat, E_WIDTH)
    if not ctx_out:
        return o, None
    sc = jnp.einsum('bqhgd,bkhd->bhgqk', qc, kc, preferred_element_type=jnp.float32) * scale
    prc = softmax_with_sink(sc, sink_r).astype(vc.dtype)
    oc = jnp.einsum('bhgqk,bkhd->bqhgd', prc, vc).reshape(bsz, n_ctx, E_WIDTH)
    return o, oc

def flip_seq(t, rev):
    return jnp.flip(t, axis=1) if rev else t

def _linrec_combine(e1, e2):
    a1, b1 = e1
    a2, b2 = e2
    return a1 * a2, a2 * b1 + b2

def s5_discretise(lam_re, lam_im, log_step, b_re, b_im, c_re, c_im):
    lam = lax.complex(lam_re.astype(jnp.float32), lam_im.astype(jnp.float32))
    dt = jnp.exp(log_step.astype(jnp.float32))[:, None]
    abar = jnp.exp(lam * dt)
    bmat = lax.complex(b_re.astype(jnp.float32), b_im.astype(jnp.float32))
    bbar = ((abar - 1.0) / lam)[..., None] * bmat
    cmat = lax.complex(c_re.astype(jnp.float32), c_im.astype(jnp.float32))
    return abar, bbar, cmat

def s5_scan(u, abar, bbar, cmat, h0):
    bsz, n_tok, n_g, n_c = u.shape
    n_chunk = n_tok // S5_CHUNK
    uc = u.reshape(bsz, n_chunk, S5_CHUNK, n_g, n_c).swapaxes(0, 1)

    def step(h, u_blk):
        bu = jnp.einsum('btgn,gpn->btgp', u_blk.astype(jnp.complex64), bbar)
        bu = bu.at[:, 0].add(abar[None] * h)
        a = jnp.broadcast_to(abar, bu.shape)
        _, hs = lax.associative_scan(_linrec_combine, (a, bu), axis=1)
        y = jnp.einsum('btgp,gnp->btgn', hs, cmat).real
        return hs[:, -1], y

    h_last, ys = lax.scan(step, h0, uc)
    return ys.swapaxes(0, 1).reshape(bsz, n_tok, n_g, n_c), h_last

def s5_mixer(p, pc, lam_re, lam_im, log_step, b_re, b_im, c_re, c_im, d_skip, glu_w, glu_b):
    bsz, n_lat, _ = p.shape
    n_ctx = pc.shape[1]
    u = p.astype(jnp.float32).reshape(bsz, n_lat, S5_GROUPS, S5_GROUP)
    uc = pc.astype(jnp.float32).reshape(bsz, n_ctx, S5_GROUPS, S5_GROUP)
    d = d_skip.astype(jnp.float32).reshape(S5_GROUPS, S5_GROUP)
    y = d * u
    yc = d * uc
    for rev in (0, 1):
        abar, bbar, cmat = s5_discretise(lam_re[rev], lam_im[rev], log_step[rev],
                                         b_re[rev], b_im[rev], c_re[rev], c_im[rev])
        h0 = jnp.zeros((bsz, S5_GROUPS, S5_STATE), jnp.complex64)
        yc_dir, h_ctx = s5_scan(flip_seq(uc, rev), abar, bbar, cmat, h0)
        y_dir, _ = s5_scan(flip_seq(u, rev), abar, bbar, cmat, h_ctx)
        y = y + flip_seq(y_dir, rev)
        yc = yc + flip_seq(yc_dir, rev)
    w = glu_w.astype(jnp.float32)
    bias = glu_b.astype(jnp.float32)

    def glu(t, n):
        g = jax.nn.gelu(t.reshape(bsz, n, E_WIDTH))
        return (g * jax.nn.sigmoid(g @ w + bias)).astype(p.dtype)

    return glu(y, n_lat), glu(yc, n_ctx)

def hgrn2_scan(q, k, v, logf, s0):
    bsz, n_tok, n_h, _ = q.shape
    n_chunk = n_tok // HG_CHUNK
    mid = HG_CHUNK // 2
    order_mask = jnp.tril(jnp.ones((HG_CHUNK, HG_CHUNK), dtype=bool))

    def blocks(t):
        return t.reshape(bsz, n_chunk, HG_CHUNK, n_h, t.shape[-1]).transpose(1, 0, 3, 2, 4)

    def step(s, blk):
        qb, kb, vb, gb = blk
        b = jnp.cumsum(gb, axis=2)
        ref = b[:, :, mid:mid + 1]
        att = jnp.einsum('bhtk,bhsk->bhts', qb * jnp.exp(b - ref), kb * jnp.exp(ref - b))
        att = jnp.where(order_mask, att, 0.0)
        o = (jnp.einsum('bhts,bhsv->bhtv', att, vb)
             + jnp.einsum('bhtk,bhkv->bhtv', qb * jnp.exp(b), s))
        b_last = b[:, :, -1:]
        s = (jnp.exp(b_last[:, :, 0])[..., None] * s
             + jnp.einsum('bhsk,bhsv->bhkv', kb * jnp.exp(b_last - b), vb))
        return s, o

    s_last, outs = lax.scan(step, s0, (blocks(q), blocks(k), blocks(v), blocks(logf)))
    return outs.transpose(1, 0, 3, 2, 4).reshape(bsz, n_tok, n_h, v.shape[-1]), s_last

def hgrn2_mixer(p, pc, lb, norm_g):
    bsz, n_lat, _ = p.shape
    n_ctx = pc.shape[1]
    lbh = lb.astype(jnp.float32).reshape(HG_HEADS, HG_HEAD_DIM)

    def heads(t):
        t = t.astype(jnp.float32).reshape(t.shape[0], t.shape[1], 4, HG_HEADS, HG_HEAD_DIM)
        return t[:, :, 0], t[:, :, 1], t[:, :, 2], t[:, :, 3]

    q, f_fw, f_bw, v = heads(p)
    qc, fc_fw, fc_bw, vc = heads(pc)
    outs, outs_c = [], []
    for rev, (fl, flc) in enumerate(((f_fw, fc_fw), (f_bw, fc_bw))):
        f = lbh + (1.0 - lbh) * jax.nn.sigmoid(fl)
        fc = lbh + (1.0 - lbh) * jax.nn.sigmoid(flc)
        s0 = jnp.zeros((bsz, HG_HEADS, HG_HEAD_DIM, HG_HEAD_DIM), jnp.float32)
        oc_dir, s_ctx = hgrn2_scan(flip_seq(qc, rev), flip_seq(1.0 - fc, rev),
                                   flip_seq(vc, rev), flip_seq(jnp.log(fc), rev), s0)
        o_dir, _ = hgrn2_scan(flip_seq(q, rev), flip_seq(1.0 - f, rev),
                              flip_seq(v, rev), flip_seq(jnp.log(f), rev), s_ctx)
        outs.append(flip_seq(o_dir, rev))
        outs_c.append(flip_seq(oc_dir, rev))
    g = norm_g.astype(jnp.float32).reshape(HG_HEADS, HG_HEAD_DIM)

    def head_norm(t, n):
        t = t * lax.rsqrt(jnp.mean(jnp.square(t), -1, keepdims=True) + NORM_EPS) * g
        return t.reshape(bsz, n, E_WIDTH).astype(p.dtype)

    return head_norm(outs[0] + outs[1], n_lat), head_norm(outs_c[0] + outs_c[1], n_ctx)

def first_inputs(seed: int = 0) -> dict:
    key = jax.random.key(seed)
    ks = jax.random.split(key, 25)
    f32 = jnp.float32
    n_attn = len(range(0, DEPTH, N_MIXERS))
    n_s5 = len(range(1, DEPTH, N_MIXERS))
    n_hg = len(range(2, DEPTH, N_MIXERS))
    beta = (8.0 * DEPTH) ** -0.25

    def nrm(k, shape, std):
        return std * jax.random.normal(k, shape, f32)

    s5_shape = (n_s5, 2, S5_GROUPS, S5_STATE)
    lam_im_init = math.pi * jnp.arange(S5_STATE, dtype=f32)
    return {
        'x': nrm(ks[0], (BATCH, SEQ, D_MODEL), 1.0),
        'c': nrm(ks[1], (BATCH, D_MODEL), 1.0),
        'ctx': nrm(ks[2], (BATCH, CTX_LEN, D_MODEL), 1.0),
        'c_ctx': nrm(ks[3], (D_MODEL,), 1.0),
        'ada_w': nrm(ks[4], (DEPTH, D_MODEL, 3 * D_MODEL), 0.5 * D_MODEL ** -0.5),
        'ada_b': nrm(ks[5], (DEPTH, 3 * D_MODEL), 0.02),
        'ln_g': 1.0 + nrm(ks[6], (DEPTH, D_MODEL), 0.02),
        'ln_b': nrm(ks[7], (DEPTH, D_MODEL), 0.02),
        'w_out': nrm(ks[8], (DEPTH, E_WIDTH, D_MODEL), beta * E_WIDTH ** -0.5),
        'attn_w_in': nrm(ks[9], (n_attn, D_MODEL, ATTN_IN), D_MODEL ** -0.5),
        'attn_sink': nrm(ks[10], (n_attn, N_Q_HEADS), 0.5),
        's5_w_in': nrm(ks[11], (n_s5, D_MODEL, S5_IN), D_MODEL ** -0.5),
        's5_lam_re': -0.5 + nrm(ks[12], s5_shape, 0.01),
        's5_lam_im': lam_im_init + nrm(ks[13], s5_shape, 0.01),
        's5_log_step': jax.random.uniform(ks[14], (n_s5, 2, S5_GROUPS), f32, math.log(1e-3), math.log(1e-1)),
        's5_b_re': nrm(ks[15], (n_s5, 2, S5_GROUPS, S5_STATE, S5_GROUP), (2 * S5_GROUP) ** -0.5),
        's5_b_im': nrm(ks[16], (n_s5, 2, S5_GROUPS, S5_STATE, S5_GROUP), (2 * S5_GROUP) ** -0.5),
        's5_c_re': nrm(ks[17], (n_s5, 2, S5_GROUPS, S5_GROUP, S5_STATE), S5_STATE ** -0.5),
        's5_c_im': nrm(ks[18], (n_s5, 2, S5_GROUPS, S5_GROUP, S5_STATE), S5_STATE ** -0.5),
        's5_d': nrm(ks[19], (n_s5, E_WIDTH), 0.5),
        's5_glu_w': nrm(ks[20], (n_s5, E_WIDTH, E_WIDTH), E_WIDTH ** -0.5),
        's5_glu_b': nrm(ks[21], (n_s5, E_WIDTH), 0.02),
        'hg_w_in': nrm(ks[22], (n_hg, D_MODEL, HG_IN), D_MODEL ** -0.5),
        'hg_lb': nrm(ks[23], (DEPTH, E_WIDTH), 0.1),
        'hg_norm_g': 1.0 + nrm(ks[24], (n_hg, E_WIDTH), 0.02),
    }

def first_block(x, c, ctx, c_ctx, ada_w, ada_b, ln_g, ln_b, w_out, attn_w_in, attn_sink,
              s5_w_in, s5_lam_re, s5_lam_im, s5_log_step, s5_b_re, s5_b_im, s5_c_re, s5_c_im,
              s5_d, s5_glu_w, s5_glu_b, hg_w_in, hg_lb, hg_norm_g):
    n_lat = x.shape[1]
    row, col = grid_positions(n_lat)
    alpha = (2.0 * DEPTH) ** 0.25
    lb_w = jax.nn.softmax(hg_lb.astype(jnp.float32), axis=0)
    lb_all = jnp.cumsum(lb_w, axis=0) - lb_w[0:1]
    xc = ctx
    for i in range(DEPTH):
        kind, j = i % N_MIXERS, i // N_MIXERS
        last = i == DEPTH - 1
        mod = jax.nn.silu(c) @ ada_w[i] + ada_b[i]
        mod_c = jax.nn.silu(c_ctx) @ ada_w[i] + ada_b[i]
        shift, scale, gate = jnp.split(mod[:, None, :], 3, axis=-1)
        shift_c, scale_c, gate_c = jnp.split(mod_c, 3, axis=-1)
        h = x * (1.0 + scale) + shift
        hc = xc * (1.0 + scale_c) + shift_c
        w_in = (attn_w_in, s5_w_in, hg_w_in)[kind][j]
        pz = h @ w_in
        pzc = hc @ w_in
        p, z = pz[..., :-E_WIDTH], pz[..., -E_WIDTH:]
        pc, zc = pzc[..., :-E_WIDTH], pzc[..., -E_WIDTH:]
        if kind == 0:
            y, yc = attention_mixer(p, pc, attn_sink[j], row, col, not last)
        elif kind == 1:
            y, yc = s5_mixer(p, pc, s5_lam_re[j], s5_lam_im[j], s5_log_step[j], s5_b_re[j], s5_b_im[j],
                             s5_c_re[j], s5_c_im[j], s5_d[j], s5_glu_w[j], s5_glu_b[j])
        else:
            y, yc = hgrn2_mixer(p, pc, lb_all[i], hg_norm_g[j])
        x = layer_norm(alpha * x + gate * ((y * jax.nn.silu(z)) @ w_out[i]), ln_g[i], ln_b[i])
        if not last:
            xc = layer_norm(alpha * xc + gate_c * ((yc * jax.nn.silu(zc)) @ w_out[i]), ln_g[i], ln_b[i])
    return x


A_GROUPS = 8
A_GROUP_DIM = 64
A_WIDTH = A_GROUPS * A_GROUP_DIM
A_CHUNK = 128
B_HEADS = 8
B_HEAD_DIM = 64
B_WIDTH = B_HEADS * B_HEAD_DIM
B_BRANCHES = ((128, 1), (512, 4), (2048, 16))
B_BLOCK = 128
C_HEADS = 4
C_DK = 128
C_DV = 256
C_GATE_RANK = 16
C_TAU = 16.0
C_CHUNK = 64
D_FF = 2816
CONV_W = 3

EPS = 1e-6
NEG = -1e30
N_EVEN = (DEPTH + 1) // 2
N_ODD = DEPTH // 2
EVEN_IN = 2 * A_WIDTH + 3 * B_WIDTH
ODD_IN = 2 * C_HEADS * C_DK + 2 * C_HEADS * C_DV + C_GATE_RANK


def rms_norm(x, g):
    xf = x.astype(jnp.float32)
    return xf * lax.rsqrt(jnp.mean(xf * xf, -1, keepdims=True) + EPS) * g.astype(jnp.float32)

def layer_norm_2(x, g, b):
    xf = x.astype(jnp.float32)
    mu = jnp.mean(xf, -1, keepdims=True)
    xc = xf - mu
    return xc * lax.rsqrt(jnp.mean(xc * xc, -1, keepdims=True) + EPS) * g + b

def causal_dwconv(h, w, b):
    S = h.shape[1]
    hp = jnp.pad(h, ((0, 0), (CONV_W - 1, 0), (0, 0)))
    out = b
    for k in range(CONV_W):
        out = out + hp[:, k:k + S] * w[k]
    return out

def chunked_gmlp(u, v, ln_g, ln_b, w_s, b_s):
    Bn, S, _ = u.shape
    nc = S // A_CHUNK
    vn = layer_norm_2(v, ln_g, ln_b).reshape(Bn, nc, A_CHUNK, A_GROUPS, A_GROUP_DIM)
    causal = jnp.tril(jnp.ones((A_CHUNK, A_CHUNK), dtype=bool))
    ws = jnp.where(causal[None], w_s.astype(jnp.float32), 0.0)
    mixed = jnp.einsum('gts,bnsgc->bntgc', ws, vn) + b_s.astype(jnp.float32).T[:, :, None]
    return u.astype(jnp.float32) * mixed.reshape(Bn, S, A_WIDTH)

def dilated_branch(q, k, v, window, dilation):
    Bn, H, S, hd = q.shape
    span = dilation * B_BLOCK
    Sp = -(-S // span) * span
    M = Sp // dilation
    nb = M // B_BLOCK
    n_back = window // dilation

    def to_blocks(t):
        t = jnp.pad(t, ((0, 0), (0, 0), (0, Sp - S), (0, 0)))
        t = t.reshape(Bn, H, M, dilation, hd)
        t = jnp.moveaxis(t, 3, 2)
        return t.reshape(Bn, H, dilation, nb, B_BLOCK, hd)

    def band(t):
        tp = jnp.pad(t, ((0, 0), (0, 0), (0, 0), (1, 0), (0, 0), (0, 0)))
        return jnp.concatenate([tp[:, :, :, :-1], tp[:, :, :, 1:]], axis=4)

    qb = to_blocks(q)
    kk = band(to_blocks(k))
    vv = band(to_blocks(v))

    i = jnp.arange(B_BLOCK)[:, None]
    j = jnp.arange(2 * B_BLOCK)[None, :]
    dist = B_BLOCK + i - j
    in_band = (dist >= 0) & (dist <= n_back)
    valid = in_band[None] & ((jnp.arange(nb) > 0)[:, None, None] | (j >= B_BLOCK)[None])

    s = jnp.einsum('bhrnic,bhrnjc->bhrnij', qb, kk) * (hd ** -0.5)
    s = jnp.where(valid, s, NEG)
    m = jnp.max(s, -1, keepdims=True)
    p = jnp.exp(s - m)
    den = jnp.sum(p, -1)
    o = jnp.einsum('bhrnij,bhrnjc->bhrnic', p, vv) / den[..., None]
    lse = m[..., 0] + jnp.log(den)

    def from_blocks(t):
        tail = t.shape[5:]
        t = t.reshape((Bn, H, dilation, M) + tail)
        t = jnp.moveaxis(t, 2, 3).reshape((Bn, H, Sp) + tail)
        return t[:, :, :S]

    return from_blocks(o), from_blocks(lse)

def even_mixer(h, w_in, a_ln_g, a_ln_b, a_ws, a_bs, q_g, k_g, w_out):
    Bn, S, _ = h.shape
    z = h @ w_in
    u, v, q, k, vb = jnp.split(
        z, [A_WIDTH, 2 * A_WIDTH, 2 * A_WIDTH + B_WIDTH, 2 * A_WIDTH + 2 * B_WIDTH], axis=-1)
    a_out = chunked_gmlp(jax.nn.gelu(u, approximate=False), jax.nn.gelu(v, approximate=False),
                         a_ln_g, a_ln_b, a_ws, a_bs)

    def heads(t):
        return t.reshape(Bn, S, B_HEADS, B_HEAD_DIM).transpose(0, 2, 1, 3)

    qh = rms_norm(heads(q), q_g)
    kh = rms_norm(heads(k), k_g)
    vh = heads(vb).astype(jnp.float32)
    outs, lses = [], []
    for window, dilation in B_BRANCHES:
        o_r, l_r = dilated_branch(qh, kh, vh, window, dilation)
        outs.append(o_r)
        lses.append(l_r)
    wts = jax.nn.softmax(jnp.stack(lses), axis=0)
    o = jnp.einsum('rbhs,rbhsc->bhsc', wts, jnp.stack(outs))
    b_out = o.transpose(0, 2, 1, 3).reshape(Bn, S, B_WIDTH)
    return jnp.concatenate([a_out, b_out], axis=-1).astype(h.dtype) @ w_out

def gla_chunked(q, k, v, log_a):
    Bn, H, S, dk = q.shape
    dv = v.shape[-1]
    nc = S // C_CHUNK

    def rs(t):
        return t.reshape(Bn, H, nc, C_CHUNK, t.shape[-1])

    q, k, v, log_a = rs(q), rs(k), rs(v), rs(log_a)
    b = jnp.cumsum(log_a, axis=3)
    b_last = b[:, :, :, -1:]
    q_t = q * jnp.exp(b)
    k_t = k * jnp.exp(-b)
    k_s = k * jnp.exp(b_last - b)
    causal = jnp.tril(jnp.ones((C_CHUNK, C_CHUNK), dtype=bool))
    attn = jnp.where(causal, jnp.einsum('bhnik,bhnjk->bhnij', q_t, k_t), 0.0)
    o_intra = jnp.einsum('bhnij,bhnjv->bhniv', attn, v)
    kv = jnp.einsum('bhnjk,bhnjv->bhnkv', k_s, v)
    decay = jnp.exp(b_last[:, :, :, 0])

    def step(state, inp):
        kv_n, d_n = inp
        return d_n[..., None] * state + kv_n, state

    init = jnp.zeros((Bn, H, dk, dv), jnp.float32)
    _, states = lax.scan(step, init, (jnp.moveaxis(kv, 2, 0), jnp.moveaxis(decay, 2, 0)))
    states = jnp.moveaxis(states, 0, 2)
    o_inter = jnp.einsum('bhnik,bhnkv->bhniv', q_t, states)
    return (o_intra + o_inter).reshape(Bn, H, S, dv)

def gla_mixer(h, w_in, w_a2, b_a, head_g, w_out):
    Bn, S, _ = h.shape
    hk, hv = C_HEADS * C_DK, C_HEADS * C_DV
    z = h @ w_in
    q, k, v, r, ga = jnp.split(z, [hk, 2 * hk, 2 * hk + hv, 2 * hk + 2 * hv], axis=-1)

    def heads(t, dh):
        return t.reshape(Bn, S, C_HEADS, dh).transpose(0, 2, 1, 3).astype(jnp.float32)

    log_a = jax.nn.log_sigmoid((ga @ w_a2 + b_a).astype(jnp.float32)) / C_TAU
    o = gla_chunked(heads(q, C_DK) * (C_DK ** -0.5), heads(k, C_DK), heads(v, C_DV),
                    heads(log_a, C_DK))
    o = rms_norm(o, head_g)
    o = o.transpose(0, 2, 1, 3).reshape(Bn, S, hv) * jax.nn.silu(r.astype(jnp.float32))
    return o.astype(h.dtype) @ w_out

def conv_ffn(h, w_gate, w_up, conv_w, conv_b, w_down):
    g = causal_dwconv(h @ w_gate, conv_w, conv_b)
    return (jax.nn.silu(g) * (h @ w_up)) @ w_down

def second_inputs(seed: int = 0) -> dict:
    key = jax.random.key(seed)
    ks = iter(jax.random.split(key, 32))

    def nrm(shape, scale):
        return jax.random.normal(next(ks), shape, jnp.float32) * scale

    res = (2 * DEPTH) ** -0.5
    return {
        "x": nrm((BATCH, SEQ, D_MODEL), 1.0),
        "norm_mix_g": 1.0 + nrm((DEPTH, D_MODEL), 0.1),
        "norm_ffn_g": 1.0 + nrm((DEPTH, D_MODEL), 0.1),
        "ev_w_in": nrm((N_EVEN, D_MODEL, EVEN_IN), D_MODEL ** -0.5),
        "ev_a_ln_g": 1.0 + nrm((N_EVEN, A_WIDTH), 0.1),
        "ev_a_ln_b": nrm((N_EVEN, A_WIDTH), 0.02),
        "ev_a_ws": nrm((N_EVEN, A_GROUPS, A_CHUNK, A_CHUNK), A_CHUNK ** -0.5),
        "ev_a_bs": 1.0 + nrm((N_EVEN, A_GROUPS, A_CHUNK), 0.1),
        "ev_q_g": 1.0 + nrm((N_EVEN, B_HEAD_DIM), 0.1),
        "ev_k_g": 1.0 + nrm((N_EVEN, B_HEAD_DIM), 0.1),
        "ev_w_out": nrm((N_EVEN, A_WIDTH + B_WIDTH, D_MODEL), (A_WIDTH + B_WIDTH) ** -0.5 * res),
        "od_w_in": nrm((N_ODD, D_MODEL, ODD_IN), D_MODEL ** -0.5),
        "od_w_a2": nrm((N_ODD, C_GATE_RANK, C_HEADS * C_DK), C_GATE_RANK ** -0.5),
        "od_b_a": nrm((N_ODD, C_HEADS * C_DK), 0.5),
        "od_head_g": 1.0 + nrm((N_ODD, C_DV), 0.1),
        "od_w_out": nrm((N_ODD, C_HEADS * C_DV, D_MODEL), (C_HEADS * C_DV) ** -0.5 * res),
        "ffn_w_gate": nrm((DEPTH, D_MODEL, D_FF), D_MODEL ** -0.5),
        "ffn_w_up": nrm((DEPTH, D_MODEL, D_FF), D_MODEL ** -0.5),
        "ffn_conv_w": nrm((DEPTH, CONV_W, D_FF), CONV_W ** -0.5),
        "ffn_conv_b": nrm((DEPTH, D_FF), 0.02),
        "ffn_w_down": nrm((DEPTH, D_FF, D_MODEL), D_FF ** -0.5 * res),
    }

def second_block(x, norm_mix_g, norm_ffn_g,
              ev_w_in, ev_a_ln_g, ev_a_ln_b, ev_a_ws, ev_a_bs, ev_q_g, ev_k_g, ev_w_out,
              od_w_in, od_w_a2, od_b_a, od_head_g, od_w_out,
              ffn_w_gate, ffn_w_up, ffn_conv_w, ffn_conv_b, ffn_w_down):
    for layer in range(DEPTH):
        h = rms_norm(x, norm_mix_g[layer]).astype(x.dtype)
        if layer % 2 == 0:
            e = layer // 2
            mix = even_mixer(h, ev_w_in[e], ev_a_ln_g[e], ev_a_ln_b[e], ev_a_ws[e], ev_a_bs[e],
                             ev_q_g[e], ev_k_g[e], ev_w_out[e])
        else:
            o = layer // 2
            mix = gla_mixer(h, od_w_in[o], od_w_a2[o], od_b_a[o], od_head_g[o], od_w_out[o])
        x = x + mix.astype(x.dtype)
        h = rms_norm(x, norm_ffn_g[layer]).astype(x.dtype)
        x = x + conv_ffn(h, ffn_w_gate[layer], ffn_w_up[layer], ffn_conv_w[layer],
                         ffn_conv_b[layer], ffn_w_down[layer]).astype(x.dtype)
    return x


def setup_inputs(seed=0):
    out = dict(first_inputs(seed))
    for name, value in second_inputs(seed + 1).items():
        if name != "x":
            out[name + "_2"] = value
    return out


def reference(
    x, c, ctx, c_ctx, ada_w, ada_b, ln_g, ln_b, w_out, attn_w_in, attn_sink, s5_w_in, s5_lam_re,
    s5_lam_im, s5_log_step, s5_b_re, s5_b_im, s5_c_re, s5_c_im, s5_d, s5_glu_w, s5_glu_b,
    hg_w_in, hg_lb, hg_norm_g, norm_mix_g_2, norm_ffn_g_2, ev_w_in_2, ev_a_ln_g_2, ev_a_ln_b_2,
    ev_a_ws_2, ev_a_bs_2, ev_q_g_2, ev_k_g_2, ev_w_out_2, od_w_in_2, od_w_a2_2, od_b_a_2,
    od_head_g_2, od_w_out_2, ffn_w_gate_2, ffn_w_up_2, ffn_conv_w_2, ffn_conv_b_2, ffn_w_down_2,
):
    x = first_block(
        x, c, ctx, c_ctx, ada_w, ada_b, ln_g, ln_b, w_out, attn_w_in, attn_sink, s5_w_in,
        s5_lam_re, s5_lam_im, s5_log_step, s5_b_re, s5_b_im, s5_c_re, s5_c_im, s5_d, s5_glu_w,
        s5_glu_b, hg_w_in, hg_lb, hg_norm_g,
    )
    return second_block(
        x, norm_mix_g_2, norm_ffn_g_2, ev_w_in_2, ev_a_ln_g_2, ev_a_ln_b_2, ev_a_ws_2,
        ev_a_bs_2, ev_q_g_2, ev_k_g_2, ev_w_out_2, od_w_in_2, od_w_a2_2, od_b_a_2, od_head_g_2,
        od_w_out_2, ffn_w_gate_2, ffn_w_up_2, ffn_conv_w_2, ffn_conv_b_2, ffn_w_down_2,
    )


_drawn_inputs = setup_inputs


def setup_inputs(seed=0):
    import zlib

    import numpy as np

    out = dict(_drawn_inputs(seed))
    spreads = {}
    factors = {'ctx': 8.0,
     'c_ctx': 4.273,
     'ada_b': 8.0,
     'attn_sink': 8.0,
     's5_w_in': 3.814,
     's5_lam_re': 64.0,
     's5_lam_im': 64.0,
     's5_log_step': 64.0,
     's5_b_re': 64.0,
     's5_b_im': 64.0,
     's5_c_re': 64.0,
     's5_c_im': 64.0,
     's5_d': 4.176,
     's5_glu_w': 8.0,
     's5_glu_b': 8.0,
     'ev_a_ln_g_2': 3.061,
     'ev_a_ln_b_2': 8.0,
     'ev_q_g_2': 7.619,
     'ev_k_g_2': 7.746,
     'ffn_conv_b_2': 6.837}
    for name, (base, spread) in spreads.items():
        noise = np.random.default_rng([zlib.crc32(name.encode()), seed]).standard_normal(out[name].shape)
        drawn = base * np.exp(spread * noise) if base else spread * noise
        out[name] = jnp.asarray(drawn.astype(out[name].dtype))
    for name, factor in factors.items():
        out[name] = (out[name] * factor).astype(out[name].dtype)
    return out
```

```python
from contextlib import ExitStack, contextmanager

import numpy as np
import concourse.bass as bass
from concourse import mybir

F32 = mybir.dt.float32
I32 = mybir.dt.int32
ALU = mybir.AluOpType
ACT = mybir.ActivationFunctionType
AX = mybir.AxisListType.X

P = 128
DM = 1024
KT = DM // P
NL = 256
NC = 256
LT = NL // P
TT = (NL + NC) // P
NTOK = NL + NC
E = 2048
ET = E // P
HD = 128
NH = E // HD
KVH = NH // 4
KVW = KVH * HD
NW = 512
ALPHA = (2.0 * 2) ** 0.25
LN_EPS = 1e-5
RMS_EPS = 1e-6
NEG = -1e30


class Chain:

    def __init__(self, eng, sem):
        self.eng, self.sem, self.base, self.k = eng, sem, 0, 0

    def run(self, ins):
        ins.then_inc(self.sem, 1)
        self.k += 1
        self.eng.wait_ge(self.sem, self.base + self.k)

    @contextmanager
    def loop(self, trips, per):
        start = self.base + self.k
        with self.eng.Fori(0, trips) as i:
            self.base, self.k = i * per + start, 0
            yield i
            assert self.k == per, (self.k, per)
        self.base, self.k = start + trips * per, 0


class Core:

    def __init__(self, nc, ctx, d):
        self.nc, self.d = nc, d
        sb = lambda name, shape: ctx.enter_context(nc.sbuf_tensor(f"resident_{name}", shape, F32))
        self.ring = sb("ring", [P, 2, KT * NW])
        self.x = sb("x", [P, LT, DM])
        self.ident = sb("ident", [P, P])
        self.modT = sb("modT", [P, 2, 16, 2])
        self.eps = sb("eps", [P, 2])
        self.landed = [ctx.enter_context(nc.semaphore(f"weights_landed{s}")) for s in range(2)]
        self.spent = []
        self.used = [0, 0]

    def load(self, eng, slot, src):
        eng.dma_start(self.ring[:, slot, :], src).then_inc(self.landed[slot], 16)

    def tile(self, slot):
        return self.ring[:, slot, :].rearrange("p (k n) -> p k n", k=KT)


def phase(core, name):
    nc = core.nc

    class Ph:
        def __enter__(s):
            s.ctx, s.sems = ExitStack(), []
            return s

        def __exit__(s, *e):
            core.spent += s.sems
            if len(core.spent) > 110:
                nc.clear_and_free_semaphores(core.spent)
                nc.all_engine_barrier()
                core.spent = []
            return s.ctx.__exit__(*e)

        def sb(s, n, shape, dt=F32):
            return s.ctx.enter_context(nc.sbuf_tensor(f"{name}_{n}", shape, dt))

        def ps(s, n, shape):
            return s.ctx.enter_context(nc.psum_tensor(f"{name}_{n}", shape, F32))

        def sem(s, n):
            s.sems.append(nc.alloc_semaphore(name=f"{name}_{n}"))
            return s.sems[-1]

        def block(s):
            return nc.Block()

    return Ph()



def prefetch(core, eng, units):
    for s in range(2):
        core.load(eng, s, units[s])


def stream_loads(core, sp, tiles, groups, halves, ntt, mm_done, half_used):
    if halves == 2:
        with sp.Fori(0, groups - 1) as i:
            sp.wait_ge(half_used, i + 1)
            core.load(sp, 0, tiles[i * 2 + 2])
            sp.wait_ge(mm_done, i * ntt + ntt)
            core.load(sp, 1, tiles[i * 2 + 3])
        return
    if groups > 3:
        with sp.Fori(0, (groups - 2) // 2) as i:
            for s in range(2):
                sp.wait_ge(mm_done, i * (2 * ntt) + (s + 1) * ntt)
                core.load(sp, s, tiles[i * 2 + 2 + s])
    for u in range(2 + (groups - 2) // 2 * 2, groups):
        sp.wait_ge(mm_done, (u - 1) * ntt)
        core.load(sp, u % 2, tiles[u])


def stream_products(core, pe, groups, halves, ntt, lhs, bank, mm_done, half_used, free, rows=P, after=None):
    def group(g, parity):
        for sem, n in free:
            pe.wait_ge(sem, g * n + 1)
        for h in range(halves):
            ub = parity * halves + h
            slot = ub % 2
            nth = (g * halves + h - slot) // 2 if isinstance(g, int) else None
            if nth is None:
                turn_tiles = halves
                pe.wait_ge(core.landed[slot], turn * (16 * turn_tiles) + 16 * (core.used[slot] + ub // 2 + 1))
            else:
                pe.wait_ge(core.landed[slot], 16 * (core.used[slot] + nth + 1))
            for t in range(ntt):
                for k in range(KT):
                    last = nc.tensor.matmul(bank(parity, t)[0:rows], lhs(h * KT + k, t), core.tile(slot)[:, k, :],
                                            start=h == 0 and k == 0, stop=h == halves - 1 and k == KT - 1)
                if h == halves - 1:
                    last.then_inc(mm_done, 1)
            if h < halves - 1:
                last.then_inc(half_used, 1)

    nc = core.nc
    if groups > 3:
        with pe.Fori(0, groups // 2) as turn:
            for parity in range(2):
                group(turn * 2 + parity, parity)
        for g in range(groups // 2 * 2, groups):
            group(g, g % 2)
    else:
        for g in range(groups):
            group(g, g % 2)
    for s in range(2):
        core.used[s] += (groups * halves + 1 - s) // 2


def stream_turns(eng, groups):
    def run(body):
        if groups > 3:
            with eng.Fori(0, groups // 2) as i:
                for parity in range(2):
                    body(i * 2 + parity, parity)
            for g in range(groups // 2 * 2, groups):
                body(g, g % 2)
        else:
            for g in range(groups):
                body(g, g % 2)
    return run


def prime(eng, sem, n):
    eng.sem_inc(sem, n)


def dve_copy(nc, dst, src):
    return nc.vector.tensor_scalar(dst, src, 1.0, None, ALU.mult)


def modulation(core):
    nc, d = core.nc, core.d
    with phase(core, "ada") as ph:
        ccT = ph.sb("ccT", [P, KT, 2])
        sT = ph.sb("sT", [P, KT, 2])
        mod = ph.sb("mod", [2, 2, 3 * DM])
        bias = ph.sb("bias", [2, 2, 3 * DM])
        ps = [ph.ps(f"ps{s}", [P, 512]) for s in range(2)]
        psT = ph.ps("psT", [P, 64])
        s_in, s_silu, s_const = ph.sem("in"), ph.sem("silu"), ph.sem("const")
        mm_done, mod_done, turned = ph.sem("mm_done"), ph.sem("mod_done"), ph.sem("turned")
        modT_done, stored = ph.sem("modT_done"), ph.sem("stored")
        NT = 2 * 3 * DM // NW

        with ph.block() as block:
            @block.sync
            def _(sp):
                prefetch(core, sp, d["ada_w"])
                stream_loads(core, sp, d["ada_w"], NT, 1, 1, mm_done, None)
                sp.wait_ge(mm_done, NT)
                prefetch(core, sp, d["attn_w_in"])
                sp.wait_ge(mod_done, NT + 2)
                sp.dma_start(d["mod"][:].rearrange("l r n -> r l n"), mod[:]).then_inc(stored, 16)
                sp.wait_ge(stored, 16)

            @block.scalar
            def _(act):
                act.dma_start(ccT[:], d["cc"][:]).then_inc(s_in, 16)
                act.dma_start(core.ident[:], d["ident"][:]).then_inc(s_const, 16)
                for r in range(2):
                    act.dma_start(bias[r:r + 1], d["ada_b"][:].rearrange("(a l) n -> a l n", a=1)).then_inc(s_const, 16)
                for t in range(LT):
                    act.dma_start(core.x[:, t, :], d["x"][t * P:(t + 1) * P, :]).then_inc(s_const, 16)
                act.wait_ge(s_in, 16)
                nc.scalar.activation(sT[:], ccT[:], ACT.Silu).then_inc(s_silu, 1)

            @block.vector
            def _(dve):
                nc.vector.memset(core.eps[:, 0:1], LN_EPS)
                nc.vector.memset(core.eps[:, 1:2], RMS_EPS)
                prime(dve, mod_done, 2)
                dve.wait_ge(s_const, 16 * (3 + LT))
                mv = mod[:].rearrange("r l n -> r (l n)")
                bv = bias[:].rearrange("r l n -> r (l n)")

                def add_bias(g, parity):
                    dve.wait_ge(mm_done, g + 1)
                    cols = bass.ts(g, NW)
                    nc.vector.tensor_tensor(mv[:, cols], ps[parity][0:2, :], bv[:, cols], ALU.add).then_inc(mod_done, 1)
                stream_turns(dve, NT)(add_bias)
                dve.wait_ge(turned, 1)
                nc.vector.tensor_copy(core.modT[:].rearrange("p l b r -> p (l b r)"), psT[:]).then_inc(modT_done, 1)
                dve.wait_ge(modT_done, 1)
                nc.vector.tensor_scalar(core.modT[:, :, 8:16, :], core.modT[:, :, 8:16, :], 1.0, None, ALU.add).then_inc(modT_done, 1)

            @block.tensor
            def _(pe):
                pe.wait_ge(s_silu, 1)
                stream_products(core, pe, NT, 1, 1, lambda k, t: sT[:, k, :], lambda parity, t: ps[parity],
                                mm_done, None, [(mod_done, 1)], rows=2)
                pe.wait_ge(mod_done, NT + 2)
                pe.wait_ge(s_const, 16 * (3 + LT))
                for l in range(2):
                    for b in range(16):
                        c = (l * 16 + b) * 2
                        last = nc.tensor.transpose(psT[:, c:c + 2], mod[:, l, b * P:(b + 1) * P], core.ident[0:2, 0:2])
                last.then_inc(turned, 1)


def modulated_transposes(core, name, layer, hT, xc):
    nc = core.nc
    with phase(core, name) as ph:
        ps = [ph.ps(f"ps{b}", [P, NTOK]) for b in range(4)]
        turned, act_free, dve_free = ph.sem("turned"), ph.sem("act_free"), ph.sem("dve_free")
        halves = ((0, slice(0, NL)), (1, slice(NL, NTOK)))
        with ph.block() as block:
            @block.tensor
            def _(pe):
                for k in range(KT):
                    if k >= 4:
                        pe.wait_ge(dve_free if k % 2 else act_free, (k - 4) // 2 + 1)
                    for t in range(TT):
                        src = (core.x if t < LT else xc)[:, t % LT, k * P:(k + 1) * P]
                        last = nc.tensor.transpose(ps[k % 4][:, t * P:(t + 1) * P], src, core.ident[:])
                    last.then_inc(turned, 1)

            @block.scalar
            def _(act):
                for k in range(0, KT, 2):
                    act.wait_ge(turned, k + 1)
                    for r, cols in halves:
                        last = nc.scalar.activation(hT[:, k, cols], ps[k % 4][:, cols], ACT.Identity, bias=core.modT[:, layer, k, r:r + 1],
                                                    scale=core.modT[:, layer, 8 + k, r:r + 1])
                    last.then_inc(act_free, 1)

            @block.vector
            def _(dve):
                for k in range(1, KT, 2):
                    dve.wait_ge(turned, k + 1)
                    for r, cols in halves:
                        last = nc.vector.tensor_scalar(hT[:, k, cols], ps[k % 4][:, cols], core.modT[:, layer, 8 + k, r:r + 1],
                                                       core.modT[:, layer, k, r:r + 1], ALU.mult, ALU.add)
                    last.then_inc(dve_free, 1)


def attention_projection(core, hT, q, kn, v, z):
    nc, d = core.nc, core.d
    with phase(core, "qkvz") as ph:
        cos = ph.sb("cos", [P, LT, P])
        sin = ph.sb("sin", [P, LT, P])
        straight = ph.sb("straight", [P, LT, NW])
        crossed = ph.sb("crossed", [P, LT, NW])
        ps = [[ph.ps(f"ps{s}{t}", [P, NW]) for t in range(TT)] for s in range(2)]
        mm_done, act_free, dve_free, tables = ph.sem("mm_done"), ph.sem("act_free"), ph.sem("dve_free"), ph.sem("tables")
        steps, silu_done = ph.sem("steps"), ph.sem("silu_done")
        NT = (2 * E + 2 * KVW) // NW
        with ph.block() as block:
            @block.sync
            def _(sp):
                stream_loads(core, sp, d["attn_w_in"], NT, 1, TT, mm_done, None)
                sp.wait_ge(mm_done, NT * TT)
                prefetch(core, sp, d["w_out0"])

            @block.tensor
            def _(pe):
                stream_products(core, pe, NT, 1, TT, lambda k, t: hT[:, k, t * P:(t + 1) * P],
                                lambda s, t: ps[s][t], mm_done, None, [(act_free, 2), (dve_free, 2)])

            @block.scalar
            def _(act):
                act.dma_start(cos[:], d["rope_cos"][:]).then_inc(tables, 16)
                act.dma_start(sin[:], d["rope_sin"][:]).then_inc(tables, 16)
                prime(act, act_free, 3)

                def empty(g, s, dst, tiles, func):
                    for t in tiles:
                        act.wait_ge(mm_done, g * TT + t + 1)
                        nc.scalar.activation(dst(t), ps[s][t][:], func).then_inc(act_free, 1)
                with act.Fori(0, 2) as i:
                    for s in range(2):
                        empty(i * 2 + s, s, lambda t: q[:, t, bass.ts(i * 2 + s, NW)], (2, 3), ACT.Copy)
                empty(4, 0, lambda t: kn[:, t, :], (2, 3), ACT.Copy)
                empty(5, 1, lambda t: v[:, t, :], (2, 3), ACT.Copy)
                with act.Fori(0, 2) as i:
                    for s in range(2):
                        empty(i * 2 + s + 6, s, lambda t: z[:, t, bass.ts(i * 2 + s, NW)], (2, 3), ACT.Silu)
                        for t in range(LT):
                            nc.scalar.activation(z[:, t, bass.ts(i * 2 + s, NW)], ps[s][t][:], ACT.Silu).then_inc(silu_done, 1)

            @block.vector
            def _(dve):
                prime(dve, dve_free, 3)
                dve.wait_ge(tables, 32)
                chain = Chain(dve, steps)

                def rotate(g, s, dst):
                    for t in range(LT):
                        dve.wait_ge(mm_done, g * TT + t + 1)
                        x4 = ps[s][t][:].rearrange("p (h c b w) -> p h c b w", h=4, c=2, b=2)
                        y4 = crossed[:, t, :].rearrange("p (h c b w) -> p h c b w", h=4, c=2, b=2)
                        tb = lambda tab, b: tab[:, t, :].rearrange("p (c b w) -> p c b w", c=2, b=2)[:, :, b, :]
                        nc.vector.tensor_tensor(straight[:, t, :].rearrange("p (h w) -> p h w", h=4), ps[s][t][:].rearrange("p (h w) -> p h w", h=4),
                                                cos[:, t, :].unsqueeze(1).to_broadcast([P, 4, P]), ALU.mult)
                        for b in range(2):
                            last = nc.vector.tensor_tensor(y4[:, :, :, b, :], x4[:, :, :, 1 - b, :],
                                                           tb(sin, b).unsqueeze(1).to_broadcast([P, 4, 2, 32]), ALU.mult)
                        chain.run(last)
                        nc.vector.tensor_tensor(dst(t), straight[:, t, :], crossed[:, t, :], ALU.add).then_inc(dve_free, 1)
                with chain.loop(2, 4) as i:
                    for s in range(2):
                        rotate(i * 2 + s, s, lambda t: q[:, t, bass.ts(i * 2 + s, NW)])
                rotate(4, 0, lambda t: kn[:, t, :])

                def empty(g, s, dst):
                    for t in range(LT):
                        dve.wait_ge(mm_done, g * TT + t + 1)
                        nc.vector.tensor_copy(dst(t), ps[s][t][:]).then_inc(dve_free, 1)
                empty(5, 1, lambda t: v[:, t, :])
                dve.wait_ge(dve_free, 3 + 6 * LT)
                with dve.Fori(0, 2) as i:
                    for s in range(2):
                        dve.wait_ge(silu_done, i * (2 * LT) + (s + 1) * LT)
                        dve.sem_inc(dve_free, LT)


def attention(core, q, kn, v, z, kT, work, yzT):
    nc, d = core.nc, core.d
    SC = HD ** -0.5
    with phase(core, "attn") as ph:
        s_sb = work[:, 0:3, :]
        p_sb = work[:, 3:6, :]
        qs = work[:, 6, :]
        qT = work[:, 7, :]
        pT = ph.sb("pT", [P, 3, NW])
        yz = ph.sb("yz", [P, TT, HD])
        mask = ph.sb("mask", [P, LT, NW])
        sink = ph.sb("sink", [P, NH])
        mx = ph.sb("mx", [P, TT])
        nm = ph.sb("nm", [P, TT])
        sk = ph.sb("sk", [P, TT])
        esk = ph.sb("esk", [P, TT])
        den = ph.sb("den", [P, TT])
        tot = ph.sb("tot", [P, TT])
        rden = ph.sb("rden", [P, TT])
        ps_t = ph.ps("ps_t", [P, NW])
        ps_s = [ph.ps(f"ps_s{b}", [P, NW]) for b in range(3)]
        ps_p = [ph.ps(f"ps_p{b}", [P, NW]) for b in range(3)]
        ps_y = ph.ps("ps_y", [P, TT, HD])
        names = ["qs_ready", "q_turned", "qT_ready", "scores_ready", "max_ready", "exp_ready", "p_turned",
                 "pT_act", "pT_dve", "pv_ready", "yz_ready", "yz_turned", "yzT_ready", "k_turned", "kT_ready",
                 "loads", "steps", "act_steps"]
        (qs_ready, q_turned, qT_ready, scores_ready, max_ready, exp_ready, p_turned, pT_act, pT_dve, pv_ready,
         yz_ready, yz_turned, yzT_ready, k_turned, kT_ready, loads, steps, act_steps) = [ph.sem(n) for n in names]
        ident = core.ident
        head_cols = lambda h: bass.ts(h, HD)
        kv = lambda h: h // 4

        with ph.block() as block:
            @block.gpsimd
            def _(pool):
                nc.gpsimd.tensor_copy(qs.rearrange("p (t w) -> p t w", t=TT), q[:, :, 0:HD]).then_inc(qs_ready, 1)
                with pool.Fori(0, NH - 1) as h:
                    pool.wait_ge(q_turned, h + 1)
                    nc.gpsimd.tensor_copy(qs.rearrange("p (t w) -> p t w", t=TT), q[:, :, head_cols(h + 1)]).then_inc(qs_ready, 1)

            @block.tensor
            def _(pe):
                for g in range(KVH):
                    if g >= 3:
                        pe.wait_ge(kT_ready, g - 2)
                    for t in range(TT):
                        last = nc.tensor.transpose(ps_s[g % 3][:, t * P:(t + 1) * P], kn[:, t, g * HD:(g + 1) * HD], ident[:])
                    last.then_inc(k_turned, 1)

                def turn_queries(h):
                    pe.wait_ge(qs_ready, h + 1)
                    for t in range(TT):
                        last = nc.tensor.transpose(ps_t[:, t * P:(t + 1) * P], qs[:, t * P:(t + 1) * P], ident[:])
                    last.then_inc(q_turned, 1)

                def scores(h, group):
                    pe.wait_ge(qT_ready, h + 1)
                    for t in range(LT):
                        last = nc.tensor.matmul(ps_s[t][:], qT[:, t * P:(t + 1) * P], kT[:, group, :], start=True, stop=True)
                    for t in range(2):
                        last = nc.tensor.matmul(ps_s[2][:, t * NC:(t + 1) * NC], qT[:, (LT + t) * P:(LT + t + 1) * P],
                                                kT[:, group, NL:NTOK], start=True, stop=True)
                    last.then_inc(scores_ready, 1)

                def mix(h, vcols):
                    pe.wait_ge(exp_ready, h + 1)
                    pe.wait_ge(pT_act, h + 1)
                    pe.wait_ge(pT_dve, h * 2 + 1)
                    for b in range(3):
                        for j in range(4):
                            last = nc.tensor.transpose(ps_p[b][:, j * P:(j + 1) * P], p_sb[:, b, j * P:(j + 1) * P], ident[:])
                        last.then_inc(p_turned, 1)
                    pe.wait_ge(pT_act, h + 2)
                    pe.wait_ge(pT_dve, h * 2 + 3)
                    for t in range(LT):
                        for j in range(4):
                            nc.tensor.matmul(ps_y[:, t, :], pT[:, t, j * P:(j + 1) * P], v[:, j, vcols], start=j == 0, stop=j == 3)
                    for t in range(2):
                        for j in range(2):
                            last = nc.tensor.matmul(ps_y[:, LT + t, :], pT[:, 2, (t * 2 + j) * P:(t * 2 + j + 1) * P],
                                                    v[:, LT + j, vcols], start=j == 0, stop=j == 1)
                    last.then_inc(pv_ready, 1)
                    pe.wait_ge(yz_ready, h + 1)
                    for t in range(TT):
                        last = nc.tensor.transpose(ps_t[:, t * P:(t + 1) * P], yz[:, t, :], ident[:])
                    last.then_inc(yz_turned, 1)

                turn_queries(0)
                pe.wait_ge(kT_ready, KVH)
                scores(0, 0)
                for g in range(KVH):
                    turns = 4 if g < KVH - 1 else 3
                    with pe.Fori(0, turns) as j:
                        h = j + 4 * g
                        if g == 0:
                            pe.wait_ge(yzT_ready, h + 1)
                        else:
                            pe.wait_ge(yzT_ready, h + 1)
                        turn_queries(h + 1)
                        pe.wait_ge(max_ready, h + 1)
                        scores(h + 1, (h + 1) // 4)
                        pe.wait_ge(qT_ready, h + 2)
                        mix(h, bass.ts(g, HD))
                mix(NH - 1, bass.ts(KVH - 1, HD))

            @block.scalar
            def _(act):
                act.dma_start(mask[:], d["attn_mask"][:]).then_inc(loads, 16)
                act.dma_start(sink[:], d["attn_sink"][0:1, :].to_broadcast([P, NH])).then_inc(loads, 16)
                prime(act, pT_act, 1)
                prime(act, yzT_ready, 1)
                for g in range(KVH):
                    act.wait_ge(k_turned, g + 1)
                    nc.scalar.activation(kT[:, g, :], ps_s[g % 3][:], ACT.Copy).then_inc(kT_ready, 1)

                def queries(h):
                    act.wait_ge(q_turned, h + 1)
                    nc.scalar.activation(qT[:], ps_t[:], ACT.Copy).then_inc(qT_ready, 1)

                def head(h, chain):
                    act.wait_ge(max_ready, h + 1)
                    act.wait_ge(p_turned, h * 3 + 1)
                    for t in range(TT):
                        src = s_sb[:, t, :] if t < LT else s_sb[:, 2, (t - LT) * NC:(t - LT + 1) * NC]
                        dst = p_sb[:, t, :] if t < LT else p_sb[:, 2, (t - LT) * NC:(t - LT + 1) * NC]
                        nc.scalar.activation(dst, src, ACT.Exp, bias=nm[:, t:t + 1], accum_out=den[:, t:t + 1])
                    nc.scalar.activation(esk[:], sk[:], ACT.Exp).then_inc(exp_ready, 1)
                    act.wait_ge(p_turned, h * 3 + 2)
                    nc.scalar.activation(pT[:, 0, :], ps_p[0][:], ACT.Copy).then_inc(pT_act, 1)
                    act.wait_ge(yz_turned, h + 1)
                    nc.scalar.activation(yzT[:, h, :], ps_t[:], ACT.Copy).then_inc(yzT_ready, 1)
                prime(act, p_turned, 1)
                queries(0)
                with act.Fori(0, NH - 1) as h:
                    queries(h + 1)
                    head(h, None)
                head(NH - 1, None)

            @block.vector
            def _(dve):
                chain = Chain(dve, steps)
                prime(dve, pT_dve, 1)
                dve.wait_ge(loads, 32)

                def maxima(h):
                    dve.wait_ge(scores_ready, h + 1)
                    for t in range(LT):
                        nc.vector.scalar_tensor_tensor(out=s_sb[:, t, :], in0=ps_s[t][:], scalar=SC, in1=mask[:, t, :], op0=ALU.mult, op1=ALU.add)
                    chain.run(nc.vector.tensor_scalar(s_sb[:, 2, :], ps_s[2][:], SC, None, ALU.mult))
                    nc.vector.tensor_reduce(mx[:, 0:LT], s_sb[:, 0:LT, :], AX, ALU.max)
                    chain.run(nc.vector.tensor_reduce(mx[:, LT:TT], s_sb[:, 2, :].rearrange("p (t w) -> p t w", t=2), AX, ALU.max))
                    chain.run(nc.vector.tensor_scalar(nm[:], mx[:], sink[:, bass.ds(h, 1)], -1.0, ALU.max, ALU.mult))
                    nc.vector.tensor_scalar(sk[:], nm[:], sink[:, bass.ds(h, 1)], None, ALU.add).then_inc(max_ready, 1)

                def outputs(h):
                    for b in (1, 2):
                        dve.wait_ge(p_turned, h * 3 + 2 + b)
                        nc.vector.tensor_copy(pT[:, b, :], ps_p[b][:]).then_inc(pT_dve, 1)
                    chain.run(nc.vector.reciprocal(rden[:], tot[:]))
                    dve.wait_ge(pv_ready, h + 1)
                    for t in range(TT):
                        last = nc.vector.scalar_tensor_tensor(out=yz[:, t, :], in0=ps_y[:, t, :], scalar=rden[:, t:t + 1],
                                                              in1=z[:, t, head_cols(h)], op0=ALU.mult, op1=ALU.mult)
                    last.then_inc(yz_ready, 1)

                maxima(0)
                with chain.loop(NH - 1, 5) as h:
                    dve.wait_ge(exp_ready, h + 1)
                    chain.run(nc.vector.tensor_tensor(tot[:], den[:], esk[:], ALU.add))
                    maxima(h + 1)
                    outputs(h)
                dve.wait_ge(exp_ready, NH)
                chain.run(nc.vector.tensor_tensor(tot[:], den[:], esk[:], ALU.add))
                outputs(NH - 1)


def layer_norm_tile(core, chain, act_rstd, t, x, stats, mv, rstd, g_row, b_row):
    nc = core.nc
    for c in range(2):
        last = nc.vector.bn_stats(stats[:, c, :], x[:, c * NW:(c + 1) * NW])
    chain.run(last)
    chain.run(nc.vector.bn_aggr(mv[:], stats[:]))
    act_rstd()
    chain.run(nc.vector.reciprocal(rstd[:], rstd[:]))
    chain.run(nc.vector.tensor_scalar(x, x, mv[:, 0:1], rstd[:, 0:1], ALU.subtract, ALU.mult))
    chain.run(nc.vector.tensor_tensor(x, x, g_row[:], ALU.mult))
    chain.run(nc.vector.tensor_tensor(x, x, b_row[:], ALU.add))


def residual_norm(core, name, layer, weights, tiles, xs, lhsT, following):
    nc, d = core.nc, core.d
    n = len(xs)
    with phase(core, name) as ph:
        rows = sorted({r for _, r in xs})
        gate = ph.sb("gate", [P, 2, DM])
        g_row = ph.sb("g_row", [P, DM])
        b_row = ph.sb("b_row", [P, DM])
        stats = ph.sb("stats", [P, 2, 6])
        mv = ph.sb("mv", [P, 2])
        rstd = ph.sb("rstd", [P, 1])
        tmp = ph.sb("tmp", [P, NW])
        ps = [[ph.ps(f"ps{s}{t}", [P, NW]) for t in range(n)] for s in range(2)]
        names = ["mm_done", "half_used", "rows_ready", "steps", "var_ready", "std_ready", "ready"]
        mm_done, half_used, rows_ready, steps, var_ready, std_ready, ready = [ph.sem(x) for x in names]
        with ph.block() as block:
            @block.sync
            def _(sp):
                stream_loads(core, sp, d[weights], 2, 2, n, mm_done, half_used)
                sp.wait_ge(mm_done, 2 * n)
                if following:
                    prefetch(core, sp, d[following])

            @block.tensor
            def _(pe):
                stream_products(core, pe, 2, 2, n, lhsT, lambda s, t: ps[s][t], mm_done, half_used, [])

            @block.scalar
            def _(act):
                for r in rows:
                    act.dma_start(gate[:, r, :], d["mod"][layer:layer + 1, r, 2 * DM:3 * DM].to_broadcast([P, DM])).then_inc(rows_ready, 16)
                act.dma_start(g_row[:], d["ln_g"][layer:layer + 1, :].to_broadcast([P, DM])).then_inc(rows_ready, 16)
                act.dma_start(b_row[:], d["ln_b"][layer:layer + 1, :].to_broadcast([P, DM])).then_inc(rows_ready, 16)
                for t in range(n):
                    act.wait_ge(var_ready, t + 1)
                    nc.scalar.activation(rstd[:], mv[:, 1:2], ACT.Sqrt, bias=core.eps[:, 0:1]).then_inc(std_ready, 1)

            @block.vector
            def _(dve):
                chain = Chain(dve, steps)
                dve.wait_ge(rows_ready, 16 * (2 + len(rows)))
                for s in range(2):
                    for t in range(n):
                        x, r = xs[t]
                        cols = slice(s * NW, (s + 1) * NW)
                        dve.wait_ge(mm_done, s * n + t + 1)
                        chain.run(nc.vector.tensor_tensor(tmp[:], ps[s][t][:], gate[:, r, cols], ALU.mult))
                        chain.run(nc.vector.scalar_tensor_tensor(out=x[:, cols], in0=x[:, cols], scalar=ALPHA, in1=tmp[:], op0=ALU.mult, op1=ALU.add))
                for t in range(n):
                    def rstd_of(t=t):
                        dve.sem_inc(var_ready, 1)
                        dve.wait_ge(std_ready, t + 1)
                    layer_norm_tile(core, chain, rstd_of, t, xs[t][0], stats, mv, rstd, g_row, b_row)


SG = 16
SN = E // SG
SS = 64
CH = 8
LC, CC = NL // CH, NC // CH
GD = 2 * SN
BG = 4
BD = 2 * BG
NB = SN // BG
TWO_PI = 6.283185307179586
TP1 = 6.28125
TP2 = float(np.float32(np.floor((TWO_PI - TP1) * 2 ** 20) / 2 ** 20))
TP3 = float(TWO_PI - TP1 - TP2)
ROUND = 12582912.0
PI_BELOW = 3.1415925


def s5_projection(core, hT):
    nc, d = core.nc, core.d
    with phase(core, "s5in") as ph:
        u = ph.sb("u", [P, TT, E])
        z = ph.sb("z", [P, LT, E])
        ps = [[ph.ps(f"ps{s}{t}", [P, NW]) for t in range(TT)] for s in range(2)]
        mm_done, act_free, dve_free, stored = [ph.sem(x) for x in ("mm_done", "act_free", "dve_free", "stored")]
        zmm_done, zact_free, zdve_free = [ph.sem(x) for x in ("zmm_done", "zact_free", "zdve_free")]
        G = E // NW
        with ph.block() as block:
            @block.sync
            def _(sp):
                stream_loads(core, sp, d["s5_w_in"][0:G + 2], G + 2, 1, TT, mm_done, None)
                sp.wait_ge(act_free, 3 + 2 * G)
                sp.wait_ge(dve_free, 3 + 2 * G)
                sp.dma_start(d["u"].rearrange("(t p) n -> p t n", p=P), u[:]).then_inc(stored, 16)
                for g in range(2, G):
                    sp.wait_ge(zmm_done, (g - 1) * LT)
                    core.load(sp, g % 2, d["s5_w_in"][G + g])
                sp.wait_ge(zact_free, 3 + 2 * G)
                sp.dma_start(d["z"].rearrange("(t p) n -> p t n", p=P), z[:]).then_inc(stored, 16)
                sp.wait_ge(stored, 32)

            @block.tensor
            def _(pe):
                stream_products(core, pe, G, 1, TT, lambda k, t: hT[:, k, t * P:(t + 1) * P],
                                lambda s, t: ps[s][t], mm_done, None, [(act_free, 2), (dve_free, 2)])
                pe.wait_ge(act_free, 3 + 2 * G)
                pe.wait_ge(dve_free, 3 + 2 * G)
                stream_products(core, pe, G, 1, LT, lambda k, t: hT[:, k, t * P:(t + 1) * P],
                                lambda s, t: ps[s][t], zmm_done, None, [(zact_free, 2)])

            @block.scalar
            def _(act):
                prime(act, act_free, 3)
                prime(act, zact_free, 3)

                def empty(g, s):
                    for t in (2, 3):
                        act.wait_ge(mm_done, g * TT + t + 1)
                        nc.scalar.activation(u[:, t, bass.ts(g, NW)], ps[s][t][:], ACT.Copy).then_inc(act_free, 1)
                stream_turns(act, G)(empty)

                def empty_z(g, s):
                    for t in range(LT):
                        act.wait_ge(zmm_done, g * LT + t + 1)
                        nc.scalar.activation(z[:, t, bass.ts(g, NW)], ps[s][t][:], ACT.Silu).then_inc(zact_free, 1)
                stream_turns(act, G)(empty_z)

            @block.vector
            def _(dve):
                prime(dve, dve_free, 3)

                def empty(g, s):
                    for t in range(LT):
                        dve.wait_ge(mm_done, g * TT + t + 1)
                        dve_copy(nc, u[:, t, bass.ts(g, NW)], ps[s][t][:]).then_inc(dve_free, 1)
                stream_turns(dve, G)(empty)


def s5_tables(core, ptab, qtab, a8):
    nc, d = core.nc, core.d
    with phase(core, "tab") as ph:
        names = "lr li dt er ei k ea r absr co si pr pi nr ni den sr si2 t1 t2 t3 t4".split()
        T = {n: ph.sb(n, [P, GD]) for n in names}
        V = lambda n: T[n][:]
        half_pi = ph.sb("half_pi", [P, 1])
        loads, steps, to_act, from_act = [ph.sem(x) for x in ("loads", "steps", "to_act", "from_act")]
        with ph.block() as block:
            @block.scalar
            def _(act):
                act.dma_start(T["lr"][:], d["s5_lam_re"][:]).then_inc(loads, 16)
                act.dma_start(T["li"][:], d["s5_lam_im"][:]).then_inc(loads, 16)
                act.dma_start(T["dt"][:], d["s5_log_step"][:].to_broadcast([P, GD])).then_inc(loads, 16)
                act.wait_ge(loads, 48)
                nc.scalar.activation(V("dt"), V("dt"), ACT.Exp).then_inc(from_act, 1)
                act.wait_ge(to_act, 1)
                nc.scalar.activation(V("ea"), V("er"), ACT.Exp).then_inc(from_act, 1)
                act.wait_ge(to_act, 2)
                nc.scalar.activation(V("si"), V("r"), ACT.Sin)
                nc.scalar.activation(V("co"), V("absr"), ACT.Sin, scale=-1.0, bias=half_pi[:, 0:1]).then_inc(from_act, 1)

            @block.vector
            def _(dve):
                chain = Chain(dve, steps)
                v = nc.vector
                lo, hi = slice(0, SS), slice(SS, P)

                def mul(o, a, b):
                    chain.run(v.tensor_tensor(o, a, b, ALU.mult))

                def add(o, a, b, op=ALU.add):
                    chain.run(v.tensor_tensor(o, a, b, op))
                chain.run(v.memset(half_pi[:], TWO_PI / 4))
                dve.wait_ge(loads, 48)
                dve.wait_ge(from_act, 1)
                mul(V("er"), V("lr"), V("dt"))
                dve.sem_inc(to_act, 1)
                mul(V("ei"), V("li"), V("dt"))
                chain.run(v.tensor_scalar(V("k"), V("ei"), 1.0 / TWO_PI, ROUND, ALU.mult, ALU.add))
                chain.run(v.tensor_scalar(V("k"), V("k"), -ROUND, None, ALU.add))
                chain.run(v.scalar_tensor_tensor(out=V("r"), in0=V("k"), scalar=-TP1, in1=V("ei"), op0=ALU.mult, op1=ALU.add))
                for part in (TP2, TP3):
                    chain.run(v.scalar_tensor_tensor(out=V("r"), in0=V("k"), scalar=-part, in1=V("r"), op0=ALU.mult, op1=ALU.add))
                chain.run(v.tensor_scalar(V("r"), V("r"), PI_BELOW, -PI_BELOW, ALU.min, ALU.max))
                chain.run(v.tensor_scalar(V("t1"), V("r"), -1.0, None, ALU.mult))
                add(V("absr"), V("r"), V("t1"), ALU.max)
                dve.sem_inc(to_act, 1)
                dve.wait_ge(from_act, 3)
                mul(V("co"), V("co"), V("ea"))
                mul(V("si"), V("si"), V("ea"))
                chain.run(v.tensor_scalar(V("nr"), V("co"), -1.0, None, ALU.add))
                mul(V("t1"), V("lr"), V("lr"))
                mul(V("t2"), V("li"), V("li"))
                add(V("den"), V("t1"), V("t2"))
                chain.run(v.reciprocal(V("den"), V("den")))
                mul(V("t1"), V("nr"), V("lr"))
                mul(V("t2"), V("si"), V("li"))
                add(V("sr"), V("t1"), V("t2"))
                mul(V("sr"), V("sr"), V("den"))
                mul(V("t1"), V("si"), V("lr"))
                mul(V("t2"), V("nr"), V("li"))
                add(V("si2"), V("t1"), V("t2"), ALU.subtract)
                mul(V("si2"), V("si2"), V("den"))
                v.memset(V("pr"), 1.0)
                chain.run(v.memset(V("pi"), 0.0))
                by_dir = lambda ap: ap.rearrange("p (g r) -> p g r", r=2)
                slot = lambda tab, *at: tab[(slice(None), slice(None), *at)].rearrange("p (g r) -> p g r", r=2)
                for n in range(CH + 1):
                    for r in range(2):
                        k = n if r == 0 else CH - n
                        dst_r = ptab[:, :, 0, k].rearrange("p (g r) -> p g r", r=2)[:, :, r]
                        dst_i = ptab[:, :, 1, k].rearrange("p (g r) -> p g r", r=2)[:, :, r]
                        v.tensor_copy(dst_r[lo], by_dir(V("pr"))[lo, :, r])
                        v.tensor_scalar(dst_r[hi], by_dir(V("pr"))[hi, :, r], -1.0, None, ALU.mult)
                        v.tensor_scalar(dst_i, by_dir(V("pi"))[:, :, r], -1.0, None, ALU.mult)
                    if n < CH:
                        v.tensor_tensor(V("t1"), V("pr"), V("sr"), ALU.mult)
                        mul(V("t2"), V("pi"), V("si2"))
                        v.tensor_tensor(V("t1"), V("t1"), V("t2"), ALU.subtract)
                        v.tensor_tensor(V("t3"), V("pr"), V("si2"), ALU.mult)
                        mul(V("t4"), V("pi"), V("sr"))
                        add(V("t3"), V("t3"), V("t4"))
                        for r in range(2):
                            i = CH - 1 - n if r == 0 else n
                            dst_r = qtab[:, :, i].rearrange("p (g r) -> p g r", r=2)[:, :, r]
                            dst_i = qtab[:, :, CH + i].rearrange("p (g r) -> p g r", r=2)[:, :, r]
                            v.tensor_copy(dst_r, by_dir(V("t1"))[:, :, r])
                            v.tensor_scalar(dst_i[lo], by_dir(V("t3"))[lo, :, r], -1.0, None, ALU.mult)
                            last = v.tensor_copy(dst_i[hi], by_dir(V("t3"))[hi, :, r])
                        chain.run(last)
                        v.tensor_tensor(V("t1"), V("pr"), V("co"), ALU.mult)
                        v.tensor_tensor(V("t2"), V("pi"), V("si"), ALU.mult)
                        v.tensor_tensor(V("t3"), V("pr"), V("si"), ALU.mult)
                        mul(V("t4"), V("pi"), V("co"))
                        v.tensor_tensor(V("pr"), V("t1"), V("t2"), ALU.subtract)
                        add(V("pi"), V("t3"), V("t4"))
                v.tensor_copy(a8[:, 0, :], V("pr"))
                v.tensor_copy(a8[lo, 1, :], T["pi"][lo])
                chain.run(v.tensor_scalar(a8[hi, 1, :], T["pi"][hi], -1.0, None, ALU.mult))


def s5_chunk_inputs(core, qtab, S, u8):
    nc, d = core.nc, core.d
    with phase(core, "s5a") as ph:
        ba, bb = ph.sb("ba", [P, BD, SG]), ph.sb("bb", [P, BD, SG])
        uc = ph.sb("uc", [LC + CC, CH, BG * SG])
        uo = ph.sb("uo", [LC + CC, BG, P])
        t1 = ph.sb("t1", [P, BD, P])
        t2 = ph.sb("t2", [P, BD, P])
        w = ph.sb("w", [P, BD, P])
        wT = ph.sb("wT", [P, BD, P])
        ub = ph.sb("ub", [P, BG, LC + CC])
        ps_u = ph.ps("ps_u", [P, BG, LC + CC])
        ps_w = [ph.ps(f"ps_w{i}", [P, BG, P]) for i in range(2)]
        ps_s = ph.ps("ps_s", [P, BD, LC + CC])
        names = "b_landed u_landed t1_made t2_made w_made u_turned w_turned ub_ready wT_ready s_made s_kept u_kept u_ordered".split()
        b_landed, u_landed, t1_made, t2_made, w_made, u_turned, w_turned, ub_ready, wT_ready, s_made, s_kept, u_kept, u_ordered = [ph.sem(n) for n in names]
        cols = lambda b: bass.ts(b, BD)
        ident = core.ident
        spread_q = lambda b, part: qtab[:, cols(b), part * CH:(part + 1) * CH].unsqueeze(3).to_broadcast([P, BD, CH, SG])
        spread_b = lambda m: m[:].unsqueeze(2).to_broadcast([P, BD, CH, SG])
        by_token = lambda m: m[:].rearrange("p g (i m) -> p g i m", i=CH)
        with ph.block() as block:
            @block.sync
            def _(sp):
                def loads(b):
                    sp.dma_start(ba[:], d["s5_ba"][b]).then_inc(b_landed, 16)
                    sp.dma_start(bb[:], d["s5_bb"][b]).then_inc(b_landed, 16)
                    sp.dma_start(uc[:], d["u"].rearrange("(c i) n -> c i n", i=CH)[:, :, bass.ts(b, BG * SG)]).then_inc(u_landed, 16)
                loads(0)
                with sp.Fori(0, NB - 1) as b:
                    sp.wait_ge(t1_made, b + 1)
                    sp.wait_ge(t2_made, b + 1)
                    sp.wait_ge(u_ordered, b + 1)
                    loads(b + 1)

            @block.gpsimd
            def _(pool):
                prime(pool, u_kept, 1)
                with pool.Fori(0, NB) as b:
                    pool.wait_ge(b_landed, b * 32 + 32)
                    pool.wait_ge(w_made, b + 1)
                    nc.gpsimd.tensor_tensor(by_token(t2), spread_q(b, 1), spread_b(bb), ALU.mult).then_inc(t2_made, 1)
                    pool.wait_ge(ub_ready, b + 2)
                    nc.gpsimd.tensor_copy(u8[:, bass.ts(b, BG), :], ub[:, :, 0:LC]).then_inc(u_kept, 1)

            @block.vector
            def _(dve):
                prime(dve, w_made, 1)
                prime(dve, s_kept, 1)
                lat, con = slice(0, LC), slice(LC, LC + CC)
                with dve.Fori(0, NB) as b:
                    dve.wait_ge(b_landed, b * 32 + 32)
                    nc.vector.tensor_tensor(by_token(t1), spread_q(b, 0), spread_b(ba), ALU.mult).then_inc(t1_made, 1)
                    dve.wait_ge(t1_made, b + 1)
                    dve.wait_ge(t2_made, b + 1)
                    dve.wait_ge(w_turned, b + 1)
                    nc.vector.tensor_tensor(w[:], t1[:], t2[:], ALU.add).then_inc(w_made, 1)
                    dve.wait_ge(w_made, b + 2)
                    for r, i in ((0, CH - 1), (1, 0)):
                        dve_copy(nc, qtab[:, cols(b), :].rearrange("p (g r) m -> p g r m", r=2)[:, :, r, :],
                                              w[:].rearrange("p (g r) m -> p g r m", r=2)[:, :, r, i * SG:(i + 1) * SG])
                    dve.wait_ge(s_made, b + 2)
                    by_dir = lambda r, steps: S[:, steps, cols(b)].rearrange("p s (g r) -> p g s r", r=2)[:, :, :, r]
                    of_dir = lambda r, chunks: ps_s[:].rearrange("p (g r) c -> p g r c", r=2)[:, :, r, chunks]
                    dve_copy(nc, by_dir(0, slice(CC, CC + LC)), of_dir(0, lat))
                    nc.vector.tensor_copy(by_dir(0, slice(0, CC)), of_dir(0, con))
                    nc.vector.tensor_copy(by_dir(1, slice(CC, CC + LC)), of_dir(1, lat)[:, :, ::-1])
                    nc.vector.tensor_copy(by_dir(1, slice(0, CC)), of_dir(1, con)[:, :, ::-1]).then_inc(s_kept, 1)

            @block.scalar
            def _(act):
                prime(act, ub_ready, 1)
                prime(act, wT_ready, 1)
                with act.Fori(0, NB) as b:
                    act.wait_ge(u_landed, b * 16 + 16)
                    act.wait_ge(u_turned, b + 1)
                    nc.scalar.activation(uo[:].rearrange("c g (i m) -> c g i m", i=CH), uc[:].rearrange("c i (g m) -> c g i m", g=BG), ACT.Copy).then_inc(u_ordered, 1)
                    act.wait_ge(w_turned, b + 2)
                    act.wait_ge(s_made, b + 1)
                    for i in range(2):
                        last = nc.scalar.activation(wT[:, i * BG:(i + 1) * BG, :], ps_w[i][:], ACT.Copy)
                    last.then_inc(wT_ready, 1)
                    act.wait_ge(u_turned, b + 2)
                    act.wait_ge(u_kept, b + 1)
                    nc.scalar.activation(ub[:], ps_u[:], ACT.Copy).then_inc(ub_ready, 1)

            @block.tensor
            def _(pe):
                prime(pe, s_made, 1)
                prime(pe, u_turned, 1)
                prime(pe, w_turned, 1)
                with pe.Fori(0, NB) as b:
                    pe.wait_ge(u_ordered, b + 1)
                    pe.wait_ge(ub_ready, b + 1)
                    pe.wait_ge(w_made, b + 2)
                    pe.wait_ge(wT_ready, b + 1)
                    for c in range(BD):
                        last = nc.tensor.transpose(ps_w[c // BG][:, c % BG, :], w[:, c, :], ident[:])
                    last.then_inc(w_turned, 1)
                    for g in range(BG):
                        last = nc.tensor.transpose(ps_u[:, g, :], uo[:, g, :], ident[0:LC + CC, 0:LC + CC])
                    last.then_inc(u_turned, 1)
                    pe.wait_ge(wT_ready, b + 2)
                    pe.wait_ge(ub_ready, b + 2)
                    pe.wait_ge(s_kept, b + 1)
                    for c in range(BD):
                        last = nc.tensor.matmul(ps_s[:, c, :], wT[:, c, :], ub[:, c // 2, :], start=True, stop=True)
                    last.then_inc(s_made, 1)


def s5_carry(core, a8, S):
    nc = core.nc
    with phase(core, "s5c") as ph:
        t1, t2 = ph.sb("t1", [P, GD]), ph.sb("t2", [P, GD])
        steps = ph.sem("steps")
        lo, hi = slice(0, SS), slice(SS, P)
        with ph.block() as block:
            @block.vector
            def _(dve):
                chain = Chain(dve, steps)
                with chain.loop(CC + LC - 2, 3) as j:
                    nc.vector.tensor_tensor(t1[:], a8[:, 0, :], S[:, j, :], ALU.mult)
                    nc.vector.tensor_tensor(t2[lo], a8[hi, 1, :], S[hi, j, :], ALU.mult)
                    chain.run(nc.vector.tensor_tensor(t2[hi], a8[lo, 1, :], S[lo, j, :], ALU.mult))
                    chain.run(nc.vector.tensor_tensor(t1[:], t1[:], t2[:], ALU.add))
                    chain.run(nc.vector.tensor_tensor(S[:, j + 1, :], S[:, j + 1, :], t1[:], ALU.add))


def s5_outputs(core, ptab, bbar, S, u8):
    nc, d = core.nc, core.d
    W9 = (CH + 1) * SG
    EW = (2 * CH - 1) * SG
    with phase(core, "s5d") as ph:
        def two(n, shape):
            return [ph.sb(f"{n}{s}", shape) for s in range(2)]
        ca, cb = two("ca", [P, BD, SG]), two("cb", [P, BD, SG])
        v1, v2 = [core.ring[:, s, 0:BD * W9].rearrange("p (g m) -> p g m", g=BD) for s in range(2)]
        V = two("V", [P, BD, W9])
        bs, hs, us = two("bs", [P, BD, SG]), two("hs", [P, BD, LC]), two("us", [P, BG, LC])
        Em = two("Em", [SG, BG, EW])
        T = two("T", [P, BG, P])
        yb = two("yb", [LC, CH, BG * SG])
        ps_f = [ph.ps(f"ps_f{s}", [SG, BG, P]) for s in range(2)]
        ps_b = [ph.ps(f"ps_b{s}", [SG, BG, P]) for s in range(2)]
        ps_y = [ph.ps(f"ps_y{s}", [LC, BG, P]) for s in range(2)]
        names = "v2_made v_steps V_made copied k_made e_back e_made y_made yb_made".split()
        v2_made, v_steps, V_made, copied, k_made, e_back, e_made, y_made, yb_made = [ph.sem(n) for n in names]
        c_landed, T_landed, y_stored = [[ph.sem(f"{n}{s}") for s in range(2)] for n in ("c_landed", "T_landed", "y_stored")]
        cols = lambda b: bass.ts(b, BD)
        grp = lambda b: bass.ts(b, BG)
        HB = NB // 2

        def spread_p(b, part):
            return ptab[:, cols(b), part, :].unsqueeze(3).to_broadcast([P, BD, CH + 1, SG])
        spread_c = lambda m: m[:].unsqueeze(2).to_broadcast([P, BD, CH + 1, SG])
        by_power = lambda m: m.rearrange("p g (i m) -> p g i m", i=CH + 1)
        by_dir = lambda m: m.rearrange("p (g r) m -> p g r m", r=2)

        with ph.block() as block:
            @block.sync
            def _(sp):
                def loads(b, s):
                    sp.dma_start(ca[s][:], d["s5_ca"][b]).then_inc(c_landed[s], 16)
                    sp.dma_start(cb[s][:], d["s5_cb"][b]).then_inc(c_landed[s], 16)

                def windows(b, s):
                    sp.wait_ge(e_made, b + 3)
                    sp.wait_ge(y_made, b + 1)
                    for i in range(CH):
                        at = SG * (CH - 1 - i)
                        sp.dma_start(T[s][i * SG:(i + 1) * SG], Em[s][:, :, at:at + P]).then_inc(T_landed[s], 16)

                def store(b, s):
                    sp.wait_ge(yb_made, b + 3)
                    sp.dma_start(d["y"].rearrange("(c t) n -> c t n", t=CH)[:, :, bass.ts(b, BG * SG)], yb[s][:]).then_inc(y_stored[s], 16)
                for s in range(2):
                    sp.sem_inc(y_stored[s], 16)
                    loads(s, s)
                windows(0, 0)
                with sp.Fori(0, HB - 1) as i:
                    for s in range(2):
                        b = i * 2 + s
                        sp.wait_ge(V_made, b + 2)
                        loads(b + 2, s)
                        windows(b + 1, 1 - s)
                        store(b, s)
                windows(NB - 1, 1)
                for b in (NB - 2, NB - 1):
                    store(b, b % 2)
                for s in range(2):
                    sp.wait_ge(y_stored[s], 16 * (HB + 1))
                prefetch(core, sp, d["s5_glu_w"])

            @block.gpsimd
            def _(pool):
                with pool.Fori(0, HB) as i:
                    for s in range(2):
                        b = i * 2 + s
                        pool.wait_ge(c_landed[s], i * 32 + 32)
                        pool.wait_ge(V_made, b + 1)
                        nc.gpsimd.tensor_tensor(by_power(v2), spread_p(b, 1), spread_c(cb[s]), ALU.mult).then_inc(v2_made, 1)

            @block.vector
            def _(dve):
                prime(dve, V_made, 1)
                prime(dve, e_made, 2)
                with dve.Fori(0, HB) as i:
                    for s in range(2):
                        b = i * 2 + s
                        dve.wait_ge(c_landed[s], i * 32 + 32)
                        nc.vector.tensor_tensor(by_power(v1), spread_p(b, 0), spread_c(ca[s]), ALU.mult).then_inc(v_steps, 1)
                        dve.wait_ge(v_steps, b + 1)
                        dve.wait_ge(v2_made, b + 1)
                        dve.wait_ge(y_made, b + 1)
                        nc.vector.tensor_tensor(V[s][:], v1, v2, ALU.add).then_inc(V_made, 1)
                        dve.wait_ge(k_made, b + 1)
                        dve.wait_ge(e_back, b + 1)
                        mid = Em[s][:, :, EW // 2 - SG // 2:EW // 2 + SG // 2]
                        nc.vector.tensor_tensor(mid, mid, ps_f[s][:, :, 0:SG], ALU.add)
                        nc.vector.tensor_copy(Em[s][:, :, P:EW], ps_f[s][:, :, SG:P]).then_inc(e_made, 1)

            @block.scalar
            def _(act):
                def copies(b, s):
                    act.wait_ge(y_made, b + 1)
                    nc.scalar.activation(bs[s][:], bbar[:, cols(b), :], ACT.Copy)
                    back = S[:, CC - 1:CC + LC - 1, cols(b)].rearrange("p c (g r) -> p g r c", r=2)
                    hd = hs[s][:].rearrange("p (g r) c -> p g r c", r=2)
                    nc.scalar.activation(hd[:, :, 0, :], back[:, :, 0, :], ACT.Copy)
                    nc.scalar.activation(hd[:, :, 1, ::-1], back[:, :, 1, :], ACT.Copy)
                    nc.scalar.activation(us[s][:], u8[:, grp(b), :], ACT.Copy).then_inc(copied, 1)

                def back_lags(b, i, s):
                    act.wait_ge(k_made, b + 1)
                    nc.scalar.activation(Em[s][:, :, 0:P], ps_b[s][:], ACT.Copy).then_inc(e_back, 1)

                def outputs(b, i, s):
                    act.wait_ge(y_made, b + 3)
                    act.wait_ge(y_stored[s], i * 16 + 16)
                    nc.scalar.activation(yb[s][:].rearrange("c t (g n) -> c g t n", g=BG),
                                         ps_y[s][:].rearrange("c g (t n) -> c g t n", t=CH), ACT.Copy).then_inc(yb_made, 1)
                prime(act, yb_made, 2)
                copies(0, 0)
                back_lags(0, 0, 0)
                with act.Fori(0, HB - 1) as i:
                    for s in range(2):
                        b = i * 2 + s
                        copies(b + 1, 1 - s)
                        back_lags(b + 1, i, 1 - s)
                        outputs(b, i, s)
                copies(NB - 1, 1)
                back_lags(NB - 1, HB - 1, 1)
                outputs(NB - 2, HB - 1, 0)
                outputs(NB - 1, HB - 1, 1)

            @block.tensor
            def _(pe):
                prime(pe, y_made, 2)

                def lags(b, s):
                    pe.wait_ge(V_made, b + 2)
                    pe.wait_ge(copied, b + 1)
                    pe.wait_ge(e_made, b + 1)
                    for g in range(BG):
                        nc.tensor.matmul(ps_f[s][:, g, :], bs[s][:, 2 * g, :], V[s][:, 2 * g, 0:P], start=True, stop=True)
                        last = nc.tensor.matmul(ps_b[s][:, g, :], bs[s][:, 2 * g + 1, :], V[s][:, 2 * g + 1, SG:W9], start=True, stop=True)
                    last.then_inc(k_made, 1)

                def outputs(b, i, s):
                    pe.wait_ge(T_landed[s], i * 128 + 128)
                    pe.wait_ge(yb_made, b + 1)
                    for g in range(BG):
                        nc.tensor.matmul(ps_y[s][:, g, :], hs[s][:, 2 * g, :], V[s][:, 2 * g, SG:W9], start=True, stop=False)
                        nc.tensor.matmul(ps_y[s][:, g, :], hs[s][:, 2 * g + 1, :], V[s][:, 2 * g + 1, 0:P], start=False, stop=False)
                        last = nc.tensor.matmul(ps_y[s][:, g, :], us[s][:, g, :], T[s][:, g, :], start=False, stop=True)
                    last.then_inc(y_made, 1)
                lags(0, 0)
                with pe.Fori(0, HB - 1) as i:
                    lags(i * 2 + 1, 1)
                    outputs(i * 2, i, 0)
                    lags(i * 2 + 2, 0)
                    outputs(i * 2 + 1, i, 1)
                lags(NB - 1, 1)
                outputs(NB - 2, HB - 1, 0)
                outputs(NB - 1, HB - 1, 1)


def turn_tiles(pe, nc, src, bank, ident, tiles, turned, freed):
    for f in range(tiles):
        if f >= 2:
            pe.wait_ge(freed, f - 1)
        for t in range(LT):
            last = nc.tensor.transpose(bank(f)[:, t * P:(t + 1) * P], src(t, f), ident)
        last.then_inc(turned, 1)


def s5_gate(core, yzT):
    nc, d = core.nc, core.d
    with phase(core, "glu") as ph:
        y = ph.sb("y", [P, LT, E])
        u = ph.sb("u", [P, LT, E])
        z = ph.sb("z", [P, LT, E])
        row = ph.sb("row", [P, E])
        bias = ph.sb("bias", [P, E])
        gT = ph.sb("gT", [P, ET, NL])
        sg = ph.sb("sg", [P, 2, LT, NW])
        ps = [[ph.ps(f"ps{s}{t}", [P, NW]) for t in range(LT)] for s in range(2)]
        ps_t = [ph.ps(f"ps_t{s}", [P, NL]) for s in range(2)]
        names = "loads y_done g_done g_turned gT_done mm_done half_used biased sig yz_done yz_turned yzT_done steps".split()
        (loads, y_done, g_done, g_turned, gT_done, mm_done, half_used, biased, sig, yz_done, yz_turned,
         yzT_done, steps) = [ph.sem(n) for n in names]
        G = E // NW
        with ph.block() as block:
            @block.sync
            def _(sp):
                sp.dma_start(y[:], d["y"].rearrange("(t p) n -> p t n", p=P)).then_inc(loads, 16)
                sp.dma_start(u[:], d["u"][0:NL].rearrange("(t p) n -> p t n", p=P)).then_inc(loads, 16)
                sp.dma_start(row[:], d["s5_d"].to_broadcast([P, E])).then_inc(loads, 16)
                sp.dma_start(bias[:], d["s5_glu_b"].to_broadcast([P, E])).then_inc(loads, 16)
                sp.dma_start(z[:], d["z"].rearrange("(t p) n -> p t n", p=P)).then_inc(loads, 16)
                stream_loads(core, sp, d["s5_glu_w"], G, 2, LT, mm_done, half_used)
                sp.wait_ge(mm_done, G * LT)
                prefetch(core, sp, d["w_out1"])

            @block.vector
            def _(dve):
                chain = Chain(dve, steps)
                prime(dve, biased, LT + 1)
                dve.wait_ge(loads, 80)
                for t in range(LT):
                    chain.run(nc.vector.tensor_tensor(u[:, t, :], u[:, t, :], row[:], ALU.mult))
                    nc.vector.tensor_tensor(y[:, t, :], y[:, t, :], u[:, t, :], ALU.add).then_inc(y_done, 1)

                def gate(g, s):
                    cols = bass.ts(g, NW)
                    for t in range(LT):
                        dve.wait_ge(mm_done, g * LT + t + 1)
                        nc.vector.tensor_tensor(sg[:, s, t, :], ps[s][t][:], bias[:, cols], ALU.add).then_inc(biased, 1)
                    for t in range(LT):
                        dve.wait_ge(sig, g * LT + t + 1)
                        chain.run(nc.vector.tensor_tensor(sg[:, s, t, :], sg[:, s, t, :], y[:, t, cols], ALU.mult))
                        nc.vector.tensor_tensor(y[:, t, cols], sg[:, s, t, :], z[:, t, cols], ALU.mult).then_inc(yz_done, 1)
                with chain.loop(G // 2, 2 * LT) as i:
                    for s in range(2):
                        gate(i * 2 + s, s)

            @block.scalar
            def _(act):
                for t in range(LT):
                    act.wait_ge(y_done, t + 1)
                    nc.scalar.activation(y[:, t, :], y[:, t, :], ACT.Gelu_apprx_tanh).then_inc(g_done, 1)
                for f in range(ET):
                    act.wait_ge(g_turned, f + 1)
                    nc.scalar.activation(gT[:, f, :], ps_t[f % 2][:], ACT.Copy).then_inc(gT_done, 1)

                def sigmoid(g, s):
                    for t in range(LT):
                        act.wait_ge(biased, g * LT + t + LT + 2)
                        nc.scalar.activation(sg[:, s, t, :], sg[:, s, t, :], ACT.Sigmoid).then_inc(sig, 1)
                stream_turns(act, G)(sigmoid)
                for f in range(ET):
                    act.wait_ge(yz_turned, f + 1)
                    nc.scalar.activation(yzT[:, f, :], ps_t[f % 2][:], ACT.Copy).then_inc(yzT_done, 1)

            @block.tensor
            def _(pe):
                pe.wait_ge(g_done, LT)
                turn_tiles(pe, nc, lambda t, f: y[:, t, f * P:(f + 1) * P], lambda f: ps_t[f % 2], core.ident[:], ET, g_turned, gT_done)
                pe.wait_ge(gT_done, ET)
                stream_products(core, pe, G, 2, LT, lambda k, t: gT[:, k, t * P:(t + 1) * P], lambda s, t: ps[s][t],
                                mm_done, half_used, [(biased, LT)])
                pe.wait_ge(yz_done, G * LT)
                turn_tiles(pe, nc, lambda t, f: y[:, t, f * P:(f + 1) * P], lambda f: ps_t[f % 2], core.ident[:], ET, yz_turned, yzT_done)


AW = 512
AG, AGD = 8, 64
BH, BHD = 8, 64
BW = BH * BHD
EV_IN = 2 * AW + 3 * BW
CHD, CDK, CDV = 4, 128, 256
CR = 16
CTAU = 16.0
CCH = 64
CONV = 3
CK, CV = CHD * CDK, CHD * CDV
FF = 2816
FT = FF // P


def rms_transposes(core, name, g_cols, hT):
    nc, d = core.nc, core.d
    with phase(core, name) as ph:
        xn = ph.sb("xn", [P, LT, DM])
        g = ph.sb("g", [P, KT])
        ms = ph.sb("ms", [P, LT])
        rs = ph.sb("rs", [P, LT])
        ps = [ph.ps(f"ps{b}", [P, NL]) for b in range(4)]
        loaded, squared, std_ready, steps, xn_ready, turned, freed = [ph.sem(n) for n in "loaded squared std_ready steps xn_ready turned freed".split()]
        with ph.block() as block:
            @block.scalar
            def _(act):
                act.dma_start(g[:], g_cols).then_inc(loaded, 16)
                for t in range(LT):
                    last = nc.scalar.activation(xn[:, t, :], core.x[:, t, :], ACT.Square, accum_out=ms[:, t:t + 1])
                last.then_inc(squared, 1)
                act.wait_ge(squared, 1)
                nc.scalar.activation(rs[:], ms[:], ACT.Sqrt, scale=1.0 / DM, bias=core.eps[:, 1:2]).then_inc(std_ready, 1)

            @block.vector
            def _(dve):
                chain = Chain(dve, steps)
                dve.wait_ge(std_ready, 1)
                chain.run(nc.vector.reciprocal(rs[:], rs[:]))
                for t in range(LT):
                    nc.vector.tensor_scalar(xn[:, t, :], core.x[:, t, :], rs[:, t:t + 1], None, ALU.mult).then_inc(xn_ready, 1)
                dve.wait_ge(loaded, 16)
                for k in range(KT):
                    dve.wait_ge(turned, k + 1)
                    nc.vector.tensor_scalar(hT[:, k, :], ps[k % 4][:], g[:, k:k + 1], None, ALU.mult).then_inc(freed, 1)

            @block.tensor
            def _(pe):
                pe.wait_ge(xn_ready, LT)
                for k in range(KT):
                    if k >= 4:
                        pe.wait_ge(freed, k - 3)
                    for t in range(LT):
                        last = nc.tensor.transpose(ps[k % 4][:, t * P:(t + 1) * P], xn[:, t, k * P:(k + 1) * P], core.ident[:])
                    last.then_inc(turned, 1)


def project(core, name, weights, tiles, hT, dst, funcs, following, extra=None):
    nc, d = core.nc, core.d
    with phase(core, name) as ph:
        ps = [[ph.ps(f"ps{s}{t}", [P, NW]) for t in range(LT)] for s in range(2)]
        mm_done, freed = ph.sem("mm_done"), ph.sem("freed")
        if extra:
            xw = ph.sb("xw", [P, KT, CR])
            xl, xd, xm = ph.sem("xl"), ph.sem("xd"), ph.sem("xm")
            ps_x = ph.ps("ps_x", [CR, NL])
        with ph.block() as block:
            @block.sync
            def _(sp):
                if extra:
                    sp.dma_start(xw[:], extra[0]).then_inc(xl, 16)
                stream_loads(core, sp, d[weights], tiles, 1, LT, mm_done, None)
                sp.wait_ge(mm_done, tiles * LT)
                prefetch(core, sp, d[following])

            @block.tensor
            def _(pe):
                stream_products(core, pe, tiles, 1, LT, lambda k, t: hT[:, k, t * P:(t + 1) * P],
                                lambda s, t: ps[s][t], mm_done, None, [(freed, LT)])
                if extra:
                    pe.wait_ge(xl, 16)
                    for k in range(KT):
                        last = nc.tensor.matmul(ps_x[:], xw[:, k, :], hT[:, k, :], start=k == 0, stop=k == KT - 1)
                    last.then_inc(xm, 1)

            @block.scalar
            def _(act):
                prime(act, freed, LT + 1)

                def empty(g, s, func):
                    for t in range(LT):
                        act.wait_ge(mm_done, g * LT + t + 1)
                        nc.scalar.activation(dst[:, t, bass.ts(g, NW)], ps[s][t][:], func).then_inc(freed, 1)
                at = 0
                for func, n in funcs:
                    if n >= 4 and at % 2 == 0 and n % 2 == 0:
                        with act.Fori(0, n // 2) as i:
                            for s in range(2):
                                empty(i * 2 + at + s, s, func)
                    else:
                        for g in range(at, at + n):
                            empty(g, g % 2, func)
                    at += n
                if extra:
                    act.wait_ge(xm, 1)
                    nc.scalar.activation(extra[1][:], ps_x[:], ACT.Copy).then_inc(xd, 1)


def project_residual(core, name, weights, mixT, following):
    nc, d = core.nc, core.d
    with phase(core, name) as ph:
        ps = [[ph.ps(f"ps{s}{t}", [P, NW]) for t in range(LT)] for s in range(2)]
        mm_done, added = ph.sem("mm_done"), ph.sem("added")
        with ph.block() as block:
            @block.sync
            def _(sp):
                sp.wait_ge(mm_done, 2 * LT)
                if following:
                    prefetch(core, sp, d[following])

            @block.tensor
            def _(pe):
                stream_products(core, pe, 2, 1, LT, lambda k, t: mixT[:, k, t * P:(t + 1) * P], lambda s, t: ps[s][t], mm_done, None, [])

            @block.vector
            def _(dve):
                for s in range(2):
                    for t in range(LT):
                        dve.wait_ge(mm_done, s * LT + t + 1)
                        x = core.x[:, t, s * NW:(s + 1) * NW]
                        nc.vector.tensor_tensor(x, x, ps[s][t][:], ALU.add).then_inc(added, 1)


def gated_mlp(core, zz, mixT):
    nc, d = core.nc, core.d
    with phase(core, "mlp") as ph:
        g_row, b_row = ph.sb("g_row", [P, AW]), ph.sb("b_row", [P, AW])
        wsT = ph.sb("wsT", [P, AG, P])
        bsT = ph.sb("bsT", [P, AG])
        stats, mv, rstd = ph.sb("stats", [P, 6]), ph.sb("mv", [P, 2]), ph.sb("rstd", [P, LT])
        tri = ph.sb("tri", [P, P])
        ps = [ph.ps(f"ps{t}", [P, AW]) for t in range(LT)]
        ps_t = [ph.ps(f"ps_t{s}", [P, NL]) for s in range(2)]
        loads, steps, var, std, vn, mixed, a_done, turned, freed, masked = [ph.sem(n) for n in "loads steps var std vn mixed a_done turned freed masked".split()]
        with ph.block() as block:
            @block.sync
            def _(sp):
                sp.dma_start(g_row[:], d["ev_a_ln_g"].to_broadcast([P, AW])).then_inc(loads, 16)
                sp.dma_start(b_row[:], d["ev_a_ln_b"].to_broadcast([P, AW])).then_inc(loads, 16)
                sp.dma_start(wsT[:], d["ev_a_wsT"]).then_inc(loads, 16)
                sp.dma_start(bsT[:], d["ev_a_bsT"]).then_inc(loads, 16)
                sp.dma_start(tri[:], d["causal"]).then_inc(loads, 16)

            @block.gpsimd
            def _(pool):
                pool.wait_ge(loads, 80)
                nc.gpsimd.tensor_tensor(wsT[:], wsT[:], tri[:].unsqueeze(1).to_broadcast([P, AG, P]), ALU.mult).then_inc(masked, 1)

            @block.vector
            def _(dve):
                chain = Chain(dve, steps)
                dve.wait_ge(loads, 80)
                for t in range(LT):
                    v = zz[:, t, AW:2 * AW]
                    chain.run(nc.vector.bn_stats(stats[:], v))
                    chain.run(nc.vector.bn_aggr(mv[:], stats[:]))
                    dve.sem_inc(var, 1)
                    dve.wait_ge(std, t + 1)
                    chain.run(nc.vector.reciprocal(rstd[:, t:t + 1], rstd[:, t:t + 1]))
                    chain.run(nc.vector.tensor_scalar(v, v, mv[:, 0:1], rstd[:, t:t + 1], ALU.subtract, ALU.mult))
                    chain.run(nc.vector.tensor_tensor(v, v, g_row[:], ALU.mult))
                    nc.vector.tensor_tensor(v, v, b_row[:], ALU.add).then_inc(vn, 1)
                for t in range(LT):
                    dve.wait_ge(mixed, t + 1)
                    for g in range(AG):
                        cols = slice(g * AGD, (g + 1) * AGD)
                        last = nc.vector.scalar_tensor_tensor(out=zz[:, t, cols], in0=ps[t][:, cols], scalar=bsT[:, g:g + 1], in1=zz[:, t, cols], op0=ALU.add, op1=ALU.mult)
                    last.then_inc(a_done, 1)

            @block.scalar
            def _(act):
                for t in range(LT):
                    act.wait_ge(var, t + 1)
                    nc.scalar.activation(rstd[:, t:t + 1], mv[:, 1:2], ACT.Sqrt, bias=core.eps[:, 1:2]).then_inc(std, 1)
                for f in range(AW // P):
                    act.wait_ge(turned, f + 1)
                    nc.scalar.activation(mixT[:, f, :], ps_t[f % 2][:], ACT.Copy).then_inc(freed, 1)

            @block.tensor
            def _(pe):
                pe.wait_ge(masked, 1)
                for t in range(LT):
                    pe.wait_ge(vn, t + 1)
                    for g in range(AG):
                        cols = slice(g * AGD, (g + 1) * AGD)
                        last = nc.tensor.matmul(ps[t][:, cols], wsT[:, g, :], zz[:, t, AW + g * AGD:AW + (g + 1) * AGD], start=True, stop=True)
                    last.then_inc(mixed, 1)
                pe.wait_ge(a_done, LT)
                turn_tiles(pe, nc, lambda t, f: zz[:, t, f * P:(f + 1) * P], lambda f: ps_t[f % 2], core.ident[:], AW // P, turned, freed)


def dilated_attention(core, zz, mixT):
    nc, d = core.nc, core.d
    Q0, K0, V0 = 2 * AW, 2 * AW + BW, 2 * AW + 2 * BW
    HP = BH // 2
    with phase(core, "dil") as ph:
        gq, gk = ph.sb("gq", [P, BHD]), ph.sb("gk", [P, BHD])
        sq = ph.sb("sq", [P, LT, 2 * BW])
        ms = ph.sb("ms", [P, LT, 2 * BH])
        rs = ph.sb("rs", [P, LT, 2 * BH])
        count, bar = ph.sb("count", [P, LT, NL]), ph.sb("bar", [P, LT, NL])
        qkT = ph.sb("qkT", [P, 2, HP, NL])
        s_sb, p_sb = ph.sb("s_sb", [P, 2, LT, NL]), ph.sb("p_sb", [P, 2, LT, NL])
        pT = ph.sb("pT", [P, 2, LT, NL])
        mx, den = ph.sb("mx", [P, 2, LT]), ph.sb("den", [P, 2, LT])
        b_out = ph.sb("b_out", [P, LT, BW])
        ps_t = [ph.ps(f"ps_t{i}", [P, 2, NL]) for i in range(2)]
        ps_s = [ph.ps(f"ps_s{i}", [P, LT, NL]) for i in range(2)]
        ps_p = [ph.ps(f"ps_p{i}", [P, LT, NL]) for i in range(2)]
        ps_y = ph.ps("ps_y", [P, LT, 2, BHD])
        names = "loads steps squared std normed turned qkT_done scores smax expd weighed p_turned pT_done y_done b_done b_turned freed".split()
        (loads, steps, squared, std, normed, turned, qkT_done, scores, smax, expd, weighed, p_turned, pT_done, y_done, b_done,
         b_turned, freed) = [ph.sem(n) for n in names]
        SC = BHD ** -0.5
        with ph.block() as block:
            @block.sync
            def _(sp):
                sp.dma_start(gq[:], d["ev_q_g"].to_broadcast([P, BHD])).then_inc(loads, 16)
                sp.dma_start(gk[:], d["ev_k_g"].to_broadcast([P, BHD])).then_inc(loads, 16)
                sp.dma_start(count[:], d["branch_count"]).then_inc(loads, 16)
                sp.dma_start(bar[:], d["branch_bar"]).then_inc(loads, 16)

            @block.vector
            def _(dve):
                chain = Chain(dve, steps)
                dve.wait_ge(loads, 64)
                chain.run(nc.vector.tensor_tensor(sq[:], zz[:, :, Q0:V0], zz[:, :, Q0:V0], ALU.mult))
                chain.run(nc.vector.tensor_reduce(ms[:], sq[:].rearrange("p t (h w) -> p t h w", w=BHD), AX, ALU.add))
                dve.sem_inc(squared, 1)
                dve.wait_ge(std, 1)
                chain.run(nc.vector.reciprocal(rs[:], rs[:]))
                for t in range(LT):
                    for n, (c0, g) in enumerate(((Q0, gq), (K0, gk))):
                        blk = zz[:, t, c0:c0 + BW].rearrange("p (h w) -> p h w", w=BHD)
                        chain.run(nc.vector.tensor_tensor(blk, blk, rs[:, t, n * BH:(n + 1) * BH].unsqueeze(2).to_broadcast([P, BH, BHD]), ALU.mult))
                        nc.vector.tensor_tensor(blk, blk, g[:].unsqueeze(1).to_broadcast([P, BH, BHD]), ALU.mult).then_inc(normed, 1)
                for hp in range(HP):
                    for i in range(2):
                        dve.wait_ge(scores, hp * 2 + i + 1)
                        chain.run(nc.vector.scalar_tensor_tensor(out=s_sb[:, i], in0=ps_s[i][:], scalar=SC, in1=bar[:], op0=ALU.mult, op1=ALU.add))
                        chain.run(nc.vector.tensor_reduce(mx[:, i], s_sb[:, i], AX, ALU.max))
                        nc.vector.tensor_scalar(mx[:, i], mx[:, i], -1.0, None, ALU.mult).then_inc(smax, 1)
                    for i in range(2):
                        dve.wait_ge(expd, hp * 2 + i + 1)
                        chain.run(nc.vector.tensor_tensor(p_sb[:, i], p_sb[:, i], count[:], ALU.mult))
                        dve.sem_inc(weighed, 1)
                        chain.run(nc.vector.tensor_reduce(den[:, i], p_sb[:, i], AX, ALU.add))
                    chain.run(nc.vector.reciprocal(den[:], den[:]))
                    dve.wait_ge(y_done, hp + 1)
                    for i in range(2):
                        for t in range(LT):
                            last = nc.vector.tensor_scalar(b_out[:, t, (2 * hp + i) * BHD:(2 * hp + i + 1) * BHD], ps_y[:, t, i, :], den[:, i, t:t + 1], None, ALU.mult)
                    last.then_inc(b_done, 1)

            @block.scalar
            def _(act):
                act.wait_ge(squared, 1)
                nc.scalar.activation(rs[:], ms[:], ACT.Sqrt, scale=1.0 / BHD, bias=core.eps[:, 1:2]).then_inc(std, 1)
                for n in range(2):
                    for i in range(2):
                        act.wait_ge(turned, n * 2 + i + 1)
                        nc.scalar.activation(qkT[:, n, 2 * i:2 * i + 2, :], ps_t[i][:], ACT.Copy).then_inc(qkT_done, 1)
                for hp in range(HP):
                    for i in range(2):
                        act.wait_ge(smax, hp * 2 + i + 1)
                        if hp:
                            act.wait_ge(p_turned, (hp - 1) * 2 + i + 1)
                        for t in range(LT):
                            last = nc.scalar.activation(p_sb[:, i, t, :], s_sb[:, i, t, :], ACT.Exp, bias=mx[:, i, t:t + 1])
                        last.then_inc(expd, 1)
                    for i in range(2):
                        act.wait_ge(p_turned, hp * 2 + i + 1)
                        if hp:
                            act.wait_ge(y_done, hp)
                        nc.scalar.activation(pT[:, i], ps_p[i][:], ACT.Copy).then_inc(pT_done, 1)
                for f in range(BW // P):
                    act.wait_ge(b_turned, f + 1)
                    nc.scalar.activation(mixT[:, AW // P + f, :], ps_t[f % 2][:, 0, :], ACT.Copy).then_inc(freed, 1)

            @block.tensor
            def _(pe):
                pe.wait_ge(normed, 2 * LT)
                for n, c0 in enumerate((Q0, K0)):
                    for i in range(2):
                        if n:
                            pe.wait_ge(qkT_done, i + 1)
                        for j in range(2):
                            for t in range(LT):
                                hp = 2 * i + j
                                last = nc.tensor.transpose(ps_t[i][:, j, t * P:(t + 1) * P], zz[:, t, c0 + hp * P:c0 + (hp + 1) * P], core.ident[:])
                        last.then_inc(turned, 1)
                pe.wait_ge(qkT_done, 4)

                def make_scores(hp):
                    for i in range(2):
                        half = slice(i * BHD, (i + 1) * BHD)
                        if hp:
                            pe.wait_ge(smax, (hp - 1) * 2 + i + 1)
                        for t in range(LT):
                            last = nc.tensor.matmul(ps_s[i][:, t, :], qkT[half, 0, hp, t * P:(t + 1) * P], qkT[half, 1, hp, :], start=True, stop=True)
                        last.then_inc(scores, 1)
                make_scores(0)
                for hp in range(HP):
                    if hp + 1 < HP:
                        make_scores(hp + 1)
                    for i in range(2):
                        pe.wait_ge(weighed, hp * 2 + i + 1)
                        if hp:
                            pe.wait_ge(pT_done, (hp - 1) * 2 + i + 1)
                        for kt in range(LT):
                            for t in range(LT):
                                last = nc.tensor.transpose(ps_p[i][:, kt, t * P:(t + 1) * P], p_sb[:, i, t, kt * P:(kt + 1) * P], core.ident[:])
                        last.then_inc(p_turned, 1)
                    if hp:
                        pe.wait_ge(b_done, hp)
                    for i in range(2):
                        pe.wait_ge(pT_done, hp * 2 + i + 1)
                        h = 2 * hp + i
                        for t in range(LT):
                            for kt in range(LT):
                                last = nc.tensor.matmul(ps_y[:, t, i, :], pT[:, i, kt, t * P:(t + 1) * P], zz[:, kt, V0 + h * BHD:V0 + (h + 1) * BHD],
                                                        start=kt == 0, stop=kt == LT - 1)
                    last.then_inc(y_done, 1)
                pe.wait_ge(b_done, HP)
                turn_tiles(pe, nc, lambda t, f: b_out[:, t, f * P:(f + 1) * P], lambda f: ps_t[f % 2][:, 0, :], core.ident[:], BW // P, b_turned, freed)


def gla(core, zz, gaT, mixT):
    nc, d = core.nc, core.d
    K0, V0, R0 = CK, 2 * CK, 2 * CK + CV
    with phase(core, "gla") as ph:
        wa2, ba = ph.sb("wa2", [CR, CK]), ph.sb("ba", [P, CK])
        g_row = ph.sb("g_row", [P, CDV])
        sums, block_ones, ends = ph.sb("sums", [P, P]), ph.sb("block_ones", [P, P]), ph.sb("ends", [P, 2])
        la = ph.sb("la", [P, LT, CK])
        ex = ph.sb("ex", [P, LT, CK])
        tmp = ph.sb("tmp", [P, LT, CK])
        qt, kt_, ks = ph.sb("qt", [P, LT, CK]), ph.sb("kt", [P, LT, CK]), ph.sb("ks", [P, LT, CK])
        qT, kT = ph.sb("qT", [P, CHD, NL]), ph.sb("kT", [P, CHD, NL])
        att = ph.sb("att", [P, 2, LT, P])
        dec = ph.sb("dec", [P, CHD, LT, 2])
        st = ph.sb("st", [P, 2, 3, CDV])
        o = ph.sb("o", [P, LT, CV])
        ms, rs = ph.sb("ms", [P, LT, CHD]), ph.sb("rs", [P, LT, CHD])
        ps_b = [ph.ps(f"ps_b{t}", [P, CK]) for t in range(LT)]
        ps_l = [ph.ps(f"ps_l{t}", [P, CK]) for t in range(LT)]
        ps_a = [ph.ps(f"ps_a{t}", [P, LT, P]) for t in range(2)]
        ps_o = [ps_b[t][:, 0:CDV] for t in range(LT)]
        ps_kv = [ps_l[i][:, 0:CDV] for i in range(2)]
        ps_d = ph.ps("ps_d", [P, CHD, LT, 2])
        names = "loads steps asteps ks_done gate_mm xs ex1 la_done cum dec_mm e0 e1 dec_done qk_done turned qkT_done att_mm att_done kv_mm st_done o_mm o_done sq_done std out_done o_turned freed".split()
        S = {n: ph.sem(n) for n in names}
        with ph.block() as block:
            @block.sync
            def _(sp):
                for dst, src in ((wa2[:], d["od_w_a2"]), (ba[:], d["od_b_a"].to_broadcast([P, CK])), (g_row[:], d["od_head_g"].to_broadcast([P, CDV])),
                                 (sums[:], d["chunk_sums"]), (block_ones[:], d["chunk_ones"]), (ends[:], d["chunk_ends"])):
                    sp.dma_start(dst, src).then_inc(S["loads"], 16)

            @block.tensor
            def _(pe):
                pe.wait_ge(S["loads"], 96)
                for t in range(LT):
                    nc.tensor.matmul(ps_b[t][:], gaT[:, t * P:(t + 1) * P], wa2[:], start=True, stop=True).then_inc(S["gate_mm"], 1)
                for t in range(LT):
                    pe.wait_ge(S["la_done"], t + 1)
                    nc.tensor.matmul(ps_b[t][:], sums[:], la[:, t, :], start=True, stop=True)
                    nc.tensor.matmul(ps_l[t][:], block_ones[:], la[:, t, :], start=True, stop=True).then_inc(S["cum"], 1)
                for t in range(LT):
                    for h in range(CHD):
                        last = nc.tensor.matmul(ps_d[:, h, t, :], la[:, t, h * CDK:(h + 1) * CDK], ends[:], start=True, stop=True)
                last.then_inc(S["dec_mm"], 1)
                pe.wait_ge(S["qk_done"], 1)
                for n, (src, bank) in enumerate(((qt, ps_b), (kt_, ps_l))):
                    for i in range(2):
                        for j in range(2):
                            for t in range(LT):
                                last = nc.tensor.transpose(bank[i][:, (j * LT + t) * P:(j * LT + t + 1) * P], src[:, t, (2 * i + j) * P:(2 * i + j + 1) * P], core.ident[:])
                        last.then_inc(S["turned"], 1)
                pe.wait_ge(S["qkT_done"], 4)
                pe.wait_ge(S["ks_done"], 1)
                for h in range(CHD):
                    a = h % 2
                    if h >= 2:
                        pe.wait_ge(S["att_done"], h - 1)
                    for t in range(LT):
                        last = nc.tensor.matmul(ps_a[a][:, t, :], kT[:, h, t * P:(t + 1) * P], qT[:, h, t * P:(t + 1) * P], start=True, stop=True)
                    last.then_inc(S["att_mm"], 1)
                    for c in range(3):
                        t, r = c // 2, slice((c % 2) * CCH, (c % 2 + 1) * CCH)
                        if h * 3 + c >= 2:
                            pe.wait_ge(S["st_done"], h * 3 + c - 1)
                        nc.tensor.matmul(ps_kv[(h * 3 + c) % 2], ks[r, t, h * CDK:(h + 1) * CDK], zz[r, t, V0 + h * CDV:V0 + (h + 1) * CDV],
                                         start=True, stop=True).then_inc(S["kv_mm"], 1)
                    pe.wait_ge(S["att_done"], h + 1)
                    pe.wait_ge(S["st_done"], h * 3 + 3)
                    if h:
                        pe.wait_ge(S["o_done"], h)
                    for t in range(LT):
                        vv = zz[:, t, V0 + h * CDV:V0 + (h + 1) * CDV]
                        last = nc.tensor.matmul(ps_o[t], att[:, a, t, :], vv, start=True, stop=True)
                        if t:
                            nc.tensor.matmul(ps_o[t][0:CCH], qT[:, h, 2 * CCH:3 * CCH], st[:, a, 1, :], start=False, stop=True, skip_group_check=True)
                        last = nc.tensor.matmul(ps_o[t][CCH:P], qT[:, h, (2 * t + 1) * CCH:(2 * t + 2) * CCH], st[:, a, 2 * t, :], start=False, stop=True, skip_group_check=True)
                    last.then_inc(S["o_mm"], 1)
                pe.wait_ge(S["out_done"], 1)
                turn_tiles(pe, nc, lambda t, f: o[:, t, f * P:(f + 1) * P], lambda f: ps_l[f % 2], core.ident[:], KT, S["o_turned"], S["freed"])

            @block.vector
            def _(dve):
                chain = Chain(dve, S["steps"])
                v = nc.vector
                dve.wait_ge(S["loads"], 96)
                for t in range(LT):
                    dve.wait_ge(S["gate_mm"], t + 1)
                    chain.run(v.tensor_tensor(la[:, t, :], ps_b[t][:], ba[:], ALU.add))
                    chain.run(v.tensor_scalar(ex[:, t, :], la[:, t, :], -1.0, None, ALU.mult))
                    chain.run(v.tensor_tensor(ex[:, t, :], ex[:, t, :], la[:, t, :], ALU.max))
                    dve.sem_inc(S["xs"], 1)
                for t in range(LT):
                    dve.wait_ge(S["ex1"], t + 1)
                    chain.run(v.tensor_scalar(la[:, t, :], la[:, t, :], 0.0, None, ALU.min))
                    chain.run(v.tensor_tensor(la[:, t, :], la[:, t, :], ex[:, t, :], ALU.subtract))
                    v.tensor_scalar(la[:, t, :], la[:, t, :], 1.0 / CTAU, None, ALU.mult).then_inc(S["la_done"], 1)
                for t in range(LT):
                    dve.wait_ge(S["e1"], 2 * t + 1)
                    chain.run(v.tensor_tensor(qt[:, t, :], zz[:, t, 0:CK], ex[:, t, :], ALU.mult))
                    chain.run(v.tensor_scalar(qt[:, t, :], qt[:, t, :], float(CDK) ** -0.5, None, ALU.mult))
                    dve.wait_ge(S["e1"], 2 * t + 2)
                    v.tensor_tensor(kt_[:, t, :], zz[:, t, K0:V0], tmp[:, t, :], ALU.mult)
                    chain.run(v.tensor_copy(ks[:, t, :], ps_b[t][:]))
                    chain.run(v.tensor_tensor(ks[:, t, :], ps_l[t][:], ks[:, t, :], ALU.subtract))
                dve.sem_inc(S["qk_done"], 1)
                for t in range(LT):
                    dve.wait_ge(S["asteps"], t + 1)
                    chain.run(v.tensor_tensor(ks[:, t, :], zz[:, t, K0:V0], ks[:, t, :], ALU.mult))
                dve.sem_inc(S["ks_done"], 1)
                dve.wait_ge(S["dec_done"], 1)
                for h in range(CHD):
                    a = h % 2
                    dve.wait_ge(S["att_mm"], h + 1)
                    if h >= 2:
                        dve.wait_ge(S["o_mm"], h - 1)
                    chain.run(v.tensor_scalar(att[:, a], ps_a[a][:], 3.0e38, -3.0e38, ALU.min, ALU.max))
                    v.tensor_tensor(att[:, a], att[:, a], sums[:].unsqueeze(1).to_broadcast([P, LT, P]), ALU.mult).then_inc(S["att_done"], 1)
                    for c in range(3):
                        dve.wait_ge(S["kv_mm"], h * 3 + c + 1)
                        kv = ps_kv[(h * 3 + c) % 2]
                        if c == 0:
                            ins = v.tensor_copy(st[:, a, 0, :], kv)
                        else:
                            ins = v.scalar_tensor_tensor(out=st[:, a, c, :], in0=st[:, a, c - 1, :], scalar=dec[:, h, c // 2, c % 2:c % 2 + 1], in1=kv, op0=ALU.mult, op1=ALU.add)
                        ins.then_inc(S["st_done"], 1)
                        dve.wait_ge(S["st_done"], h * 3 + c + 1)
                    dve.wait_ge(S["o_mm"], h + 1)
                    for t in range(LT):
                        last = v.tensor_copy(o[:, t, h * CDV:(h + 1) * CDV], ps_o[t])
                    last.then_inc(S["o_done"], 1)
                dve.wait_ge(S["o_done"], CHD)
                for t in range(LT):
                    sq = zz[:, t, 0:CV]
                    chain.run(v.tensor_tensor(sq, o[:, t, :], o[:, t, :], ALU.mult))
                    chain.run(v.tensor_reduce(ms[:, t, :], sq.rearrange("p (h w) -> p h w", h=CHD), AX, ALU.add))
                dve.sem_inc(S["sq_done"], 1)
                dve.wait_ge(S["std"], 1)
                chain.run(v.reciprocal(rs[:], rs[:]))
                for t in range(LT):
                    ob = o[:, t, :].rearrange("p (h w) -> p h w", h=CHD)
                    chain.run(v.tensor_tensor(ob, ob, rs[:, t, :].unsqueeze(2).to_broadcast([P, CHD, CDV]), ALU.mult))
                    chain.run(v.tensor_tensor(ob, ob, g_row[:].unsqueeze(1).to_broadcast([P, CHD, CDV]), ALU.mult))
                    chain.run(v.tensor_tensor(o[:, t, :], o[:, t, :], zz[:, t, R0:R0 + CV], ALU.mult))
                dve.sem_inc(S["out_done"], 1)

            @block.scalar
            def _(act):
                sc = nc.scalar
                for t in range(LT):
                    act.wait_ge(S["xs"], t + 1)
                    sc.activation(ex[:, t, :], ex[:, t, :], ACT.Exp, scale=-1.0).then_inc(S["e0"], 1)
                    act.wait_ge(S["e0"], t + 1)
                    sc.activation(ex[:, t, :], ex[:, t, :], ACT.Ln, bias=1.0).then_inc(S["ex1"], 1)
                for t in range(LT):
                    act.wait_ge(S["cum"], t + 1)
                    sc.activation(ex[:, t, :], ps_b[t][:], ACT.Exp).then_inc(S["e1"], 1)
                    sc.activation(tmp[:, t, :], ps_b[t][:], ACT.Exp, scale=-1.0).then_inc(S["e1"], 1)
                act.wait_ge(S["dec_mm"], 1)
                sc.activation(dec[:], ps_d[:], ACT.Exp).then_inc(S["dec_done"], 1)
                act.wait_ge(S["qk_done"], 1)
                for t in range(LT):
                    sc.activation(ks[:, t, :], ks[:, t, :], ACT.Exp).then_inc(S["asteps"], 1)
                for n, (dst, bank) in enumerate(((qT, ps_b), (kT, ps_l))):
                    for i in range(2):
                        act.wait_ge(S["turned"], n * 2 + i + 1)
                        sc.activation(dst[:, 2 * i:2 * i + 2, :], bank[i][:].rearrange("p (j w) -> p j w", j=2), ACT.Copy).then_inc(S["qkT_done"], 1)
                act.wait_ge(S["sq_done"], 1)
                sc.activation(rs[:], ms[:], ACT.Sqrt, scale=1.0 / CDV, bias=core.eps[:, 1:2]).then_inc(S["std"], 1)
                for f in range(KT):
                    act.wait_ge(S["o_turned"], f + 1)
                    sc.activation(mixT[:, f, :], ps_l[f % 2][:, 0:NL], ACT.Copy).then_inc(S["freed"], 1)


def conv_ffn(core, name, layer, hT, following):
    nc, d = core.nc, core.d
    with phase(core, name) as ph:
        wd = [ph.sb(f"wd{s}", [P, 2, DM]) for s in range(2)]
        a = [ph.sb(f"a{s}", [P, 2, NL]) for s in range(2)]
        c = [ph.sb(f"c{s}", [P, 2, NL]) for s in range(2)]
        cw, cb = ph.sb("cw", [P, FT, CONV]), ph.sb("cb", [P, FT])
        ps = [[ph.ps(f"ps{s}{f}", [P, 2, NL]) for f in range(2)] for s in range(2)]
        acc = [[ph.ps(f"acc{t}{n}", [P, NW]) for n in range(2)] for t in range(LT)]
        names = "loads gu_done conv_done silu_done a_made down_done steps added".split()
        loads, gu_done, conv_done, silu_done, a_made, down_done, steps, added = [ph.sem(n) for n in names]
        wd_landed = [ph.sem(f"wd_landed{s}") for s in range(2)]
        NU = FT // 2
        HU = (NU - 3) // 2
        weights = d[f"ffn_gu{layer}"]
        down = d[f"ffn_down{layer}"]
        with ph.block() as block:
            @block.sync
            def _(sp):
                for s in range(2):
                    sp.dma_start(wd[s][:], down[s]).then_inc(wd_landed[s], 16)
                sp.dma_start(cw[:], d["ffn_conv_w"][layer]).then_inc(loads, 16)
                sp.dma_start(cb[:], d["ffn_conv_b"][layer]).then_inc(loads, 16)

                def turn(u, s):
                    sp.wait_ge(gu_done, u + 1)
                    core.load(sp, s, weights[u + 2])
                    sp.wait_ge(down_done, u + 3)
                    sp.dma_start(wd[s][:], down[u + 2]).then_inc(wd_landed[s], 16)
                with sp.Fori(0, (NU - 2) // 2) as i:
                    for s in range(2):
                        turn(i * 2 + s, s)
                for u in range((NU - 2) // 2 * 2, NU - 2):
                    turn(u, u % 2)
                sp.wait_ge(gu_done, NU)
                if following:
                    prefetch(core, sp, d[following])

            @block.tensor
            def _(pe):
                prime(pe, down_done, 2)

                def gate_up(u, turn, s, nth):
                    pe.wait_ge(core.landed[s], turn * 16 + 16 * (core.used[s] + nth + 1))
                    pe.wait_ge(a_made, u + 1)
                    w = core.ring[:, s, :].rearrange("p (m k n) -> p m k n", m=2, k=KT)
                    for f in range(2):
                        for m in range(2):
                            for k in range(KT):
                                last = nc.tensor.matmul(ps[s][f][:, m, :], w[:, m, k, f * P:(f + 1) * P], hT[:, k, :], start=k == 0, stop=k == KT - 1)
                    last.then_inc(gu_done, 1)

                def down_product(u, turn, s, nth, first=False, final=False):
                    pe.wait_ge(a_made, u + 3)
                    pe.wait_ge(wd_landed[s], turn * 16 + 16 * (nth + 1))
                    for f in range(2):
                        for t in range(LT):
                            for n in range(2):
                                last = nc.tensor.matmul(acc[t][n][:], a[s][:, f, t * P:(t + 1) * P], wd[s][:, f, n * NW:(n + 1) * NW],
                                                        start=first and f == 0, stop=final and f == 1)
                    last.then_inc(down_done, 1)
                gate_up(0, 0, 0, 0)
                gate_up(1, 0, 1, 0)
                down_product(0, 0, 0, 0, first=True)
                with pe.Fori(0, HU) as i:
                    gate_up(i * 2 + 2, i, 0, 1)
                    down_product(i * 2 + 1, i, 1, 0)
                    gate_up(i * 2 + 3, i, 1, 1)
                    down_product(i * 2 + 2, i, 0, 1)
                gate_up(NU - 1, 0, 0, HU + 1)
                down_product(NU - 2, 0, 1, HU)
                down_product(NU - 1, 0, 0, HU + 1, final=True)
                core.used[0] += NU // 2 + 1
                core.used[1] += NU // 2

            @block.scalar
            def _(act):
                def silus(u, s):
                    act.wait_ge(conv_done, u * 2 + 1)
                    nc.scalar.activation(c[s][:, 0, :], c[s][:, 0, :], ACT.Silu).then_inc(silu_done, 1)
                    act.wait_ge(conv_done, u * 2 + 2)
                    nc.scalar.activation(c[s][:, 1, :], c[s][:, 1, :], ACT.Silu).then_inc(silu_done, 1)
                with act.Fori(0, NU // 2) as i:
                    for s in range(2):
                        silus(i * 2 + s, s)
                silus(NU - 1, 0)

            @block.vector
            def _(dve):
                chain = Chain(dve, steps)
                v = nc.vector
                prime(dve, a_made, 2)
                dve.wait_ge(loads, 32)

                def unit(u, s):
                    dve.wait_ge(gu_done, u + 1)
                    dve.wait_ge(a_made, u + 1)
                    for f in range(2):
                        g, cf = ps[s][f][:, 0, :], c[s][:, f, :]
                        wk = lambda k: cw[:, bass.ds(u * 2 + f, 1), k]
                        chain.run(v.tensor_scalar(cf, g, wk(2), cb[:, bass.ds(u * 2 + f, 1)], ALU.mult, ALU.add))
                        chain.run(v.scalar_tensor_tensor(out=cf[:, 1:NL], in0=g[:, 0:NL - 1], scalar=wk(1), in1=cf[:, 1:NL], op0=ALU.mult, op1=ALU.add))
                        v.scalar_tensor_tensor(out=cf[:, 2:NL], in0=g[:, 0:NL - 2], scalar=wk(0), in1=cf[:, 2:NL], op0=ALU.mult, op1=ALU.add).then_inc(conv_done, 1)
                    dve.wait_ge(down_done, u + 1)
                    for f in range(2):
                        dve.wait_ge(silu_done, u * 2 + f + 1)
                        last = v.tensor_tensor(a[s][:, f, :], c[s][:, f, :], ps[s][f][:, 1, :], ALU.mult)
                    last.then_inc(a_made, 1)
                with chain.loop(NU // 2, 8) as i:
                    for s in range(2):
                        unit(i * 2 + s, s)
                unit(NU - 1, 0)
                dve.wait_ge(down_done, NU + 2)
                for t in range(LT):
                    for n in range(2):
                        x = core.x[:, t, n * NW:(n + 1) * NW]
                        v.tensor_tensor(x, x, acc[t][n][:], ALU.add).then_inc(added, 1)


def store(core, out):
    nc = core.nc
    with phase(core, "store") as ph:
        stored = ph.sem("stored")
        with ph.block() as block:
            @block.sync
            def _(sp):
                sp.dma_start(out.rearrange("a (t p) n -> p (a t) n", p=P), core.x[:]).then_inc(stored, 16)
                sp.wait_ge(stored, 16)


def load_context(core, xc):
    nc = core.nc
    with phase(core, "ctx") as ph:
        landed = ph.sem("landed")
        with ph.block() as block:
            @block.sync
            def _(sp):
                sp.dma_start(xc[:], core.d["ctx"].rearrange("(t p) n -> p t n", p=P)).then_inc(landed, 16)
                sp.wait_ge(landed, 16)


def build(nc, d, out, start=0):
    for name, shape in (("mod", [2, 2, 3 * DM]), ("u", [NTOK, E]), ("y", [NL, E]), ("z", [NL, E])):
        d[name] = nc.dram_tensor(name + "_scratch", shape, F32, kind="Internal").ap()
    with ExitStack() as ctx:
        core = Core(nc, ctx, d)

        def within(stack, n, shape):
            return stack.enter_context(nc.sbuf_tensor(n, shape, F32))
        latent = [(core.x[:, t, :], 0) for t in range(LT)]
        modulation(core)
        with ExitStack() as first:
            xc = within(first, "xc", [P, LT, DM])
            hT = within(first, "hT", [P, KT, NTOK])
            load_context(core, xc)
            context = [(xc[:, t, :], 1) for t in range(LT)]
            with ExitStack() as mem:
                modulated_transposes(core, "h0", 0, hT, xc)
                q, z = within(mem, "q", [P, TT, E]), within(mem, "z", [P, TT, E])
                kn, v = within(mem, "kn", [P, TT, KVW]), within(mem, "v", [P, TT, KVW])
                attention_projection(core, hT, q, kn, v, z)
                kT, yzT = within(mem, "kT", [P, KVH, NTOK]), within(mem, "yzT", [P, ET, NTOK])
                attention(core, q, kn, v, z, kT, hT, yzT)
                residual_norm(core, "out0", 0, "w_out0", TT, latent + context, lambda k, t: yzT[:, k, t * P:(t + 1) * P], "s5_w_in")
            modulated_transposes(core, "h1", 1, hT, xc)
            s5_projection(core, hT)
        with ExitStack() as second:
            with ExitStack() as mem:
                ptab, qtab = within(mem, "ptab", [P, GD, 2, CH + 1]), within(mem, "qtab", [P, GD, 2 * CH])
                a8 = within(mem, "a8", [P, 2, GD])
                s5_tables(core, ptab, qtab, a8)
                S, u8 = within(mem, "S", [P, LC + CC, GD]), within(mem, "u8", [P, SN, LC])
                s5_chunk_inputs(core, qtab, S, u8)
                s5_carry(core, a8, S)
                s5_outputs(core, ptab, qtab, S, u8)
            yzT = within(second, "yzT1", [P, ET, NL])
            s5_gate(core, yzT)
            residual_norm(core, "out1", 1, "w_out1", LT, latent, lambda k, t: yzT[:, k, t * P:(t + 1) * P], "ev_w_in")
        with ExitStack() as third:
            hT = within(third, "hT2", [P, KT, NL])
            mixT = within(third, "mixT", [P, KT, NL])
            with ExitStack() as mem:
                rms_transposes(core, "hm0", d["norm_mix_g"][0], hT)
                zz = within(mem, "zz0", [P, LT, EV_IN])
                project(core, "evin", "ev_w_in", EV_IN // NW, hT, zz, [(ACT.Gelu, 2), (ACT.Copy, 3)], "ev_w_out")
                gated_mlp(core, zz, mixT)
                dilated_attention(core, zz, mixT)
            project_residual(core, "evout", "ev_w_out", mixT, "ffn_gu0")
            rms_transposes(core, "hf0", d["norm_ffn_g"][0], hT)
            conv_ffn(core, "ffn0", 0, hT, "od_w_in")
            with ExitStack() as mem:
                rms_transposes(core, "hm1", d["norm_mix_g"][1], hT)
                zz, gaT = within(mem, "zz1", [P, LT, 2 * CK + 2 * CV]), within(mem, "gaT", [CR, NL])
                project(core, "odin", "od_w_in", (2 * CK + 2 * CV) // NW, hT, zz, [(ACT.Copy, 4), (ACT.Silu, 2)], "od_w_out",
                        extra=(d["od_w_ga"], gaT))
                gla(core, zz, gaT, mixT)
            project_residual(core, "odout", "od_w_out", mixT, "ffn_gu1")
            rms_transposes(core, "hf1", d["norm_ffn_g"][1], hT)
            conv_ffn(core, "ffn1", 1, hT, None)
            store(core, out)


def tiles_of(w, halves=1):
    k, n = w.shape
    a = w.reshape(halves, KT, P, n // NW, NW).transpose(3, 0, 2, 1, 4)
    return np.ascontiguousarray(a).reshape(n // NW * halves, P, KT * NW)


def constants():
    c = {"ident": np.eye(P, dtype=np.float32)}
    n = np.arange(NL, dtype=np.float32)
    row, col = np.floor(n / 64).astype(np.float32), (n % 64).astype(np.float32)
    inv = np.power(np.float32(10000.0), -np.arange(32, dtype=np.float32) / np.float32(32)).astype(np.float32)
    ar, ac = row[:, None] * inv, col[:, None] * inv
    cos = np.concatenate([np.cos(ar), np.cos(ar), np.cos(ac), np.cos(ac)], 1)
    sin = np.concatenate([-np.sin(ar), np.sin(ar), -np.sin(ac), np.sin(ac)], 1)
    lay = lambda a: np.ascontiguousarray(a.reshape(LT, P, P).transpose(1, 0, 2)).astype(np.float32)
    c["rope_cos"], c["rope_sin"] = lay(cos), lay(sin)
    i = np.arange(NL)
    m = np.zeros((NL, NW), np.float32)
    m[:, :NL] = np.where(np.abs(i[:, None] - i[None, :]) <= 128, 0.0, NEG)
    c["attn_mask"] = np.ascontiguousarray(m.reshape(LT, P, NW).transpose(1, 0, 2))
    t, s = i[:, None], i[None, :]
    seen = ((t - s >= 0) & (t - s <= 128)).astype(np.float32)
    for dilation in (4, 16):
        seen += (t >= s) & ((t - s) % dilation == 0)
    lay2 = lambda m: np.ascontiguousarray(m.reshape(LT, P, NL).transpose(1, 0, 2)).astype(np.float32)
    c["branch_count"], c["branch_bar"] = lay2(seen), lay2(np.where(seen > 0, 0.0, NEG))
    r = np.arange(P)
    c["causal"] = (r[:, None] <= r[None, :]).astype(np.float32)
    same = (r[:, None] // CCH == r[None, :] // CCH).astype(np.float32)
    c["chunk_sums"], c["chunk_ones"] = c["causal"] * same, same
    c["chunk_ends"] = np.ascontiguousarray(same[:, ::CCH])
    return c


def laid_out(i):
    a = {k: np.asarray(v) for k, v in i.items()}
    o = constants()
    o["x"], o["ctx"] = a["x"][0], a["ctx"][0]
    o["cc"] = np.ascontiguousarray(np.stack([a["c"][0], a["c_ctx"]]).reshape(2, KT, P).transpose(2, 1, 0))
    o["ada_w"] = np.concatenate([tiles_of(a["ada_w"][l]) for l in range(2)])
    o["ada_b"], o["ln_g"], o["ln_b"] = a["ada_b"], a["ln_g"], a["ln_b"]
    o["attn_w_in"] = tiles_of(a["attn_w_in"][0])
    o["attn_sink"] = a["attn_sink"]
    o["w_out0"], o["w_out1"] = tiles_of(a["w_out"][0], 2), tiles_of(a["w_out"][1], 2)
    s5 = {k: a["s5_" + k][0] for k in ("lam_re", "lam_im", "log_step", "b_re", "b_im", "c_re", "c_im")}
    o["s5_w_in"] = tiles_of(a["s5_w_in"][0])
    twice = lambda m: np.concatenate([m, m])
    for k in ("lam_re", "lam_im"):
        o["s5_" + k] = twice(s5[k].transpose(2, 1, 0).reshape(SS, GD))
    o["s5_log_step"] = np.ascontiguousarray(s5["log_step"].T).reshape(1, GD)
    batched = lambda m: m.reshape(SS, NB, BD, SG).transpose(1, 0, 2, 3)
    b = {k: batched(s5[k].transpose(2, 1, 0, 3)) for k in ("b_re", "b_im")}
    c = {k: batched(s5[k].transpose(3, 1, 0, 2)) for k in ("c_re", "c_im")}
    o["s5_ba"] = np.concatenate([b["b_re"], b["b_im"]], 1)
    o["s5_bb"] = np.concatenate([b["b_im"], b["b_re"]], 1)
    o["s5_ca"] = np.concatenate([c["c_re"], c["c_im"]], 1)
    o["s5_cb"] = np.concatenate([c["c_im"], c["c_re"]], 1)
    o["s5_d"], o["s5_glu_b"] = a["s5_d"], a["s5_glu_b"]
    o["s5_glu_w"] = tiles_of(a["s5_glu_w"][0], 2)
    cols = lambda m: np.ascontiguousarray(m.reshape(m.shape[0], -1, P).transpose(0, 2, 1))
    o["norm_mix_g"], o["norm_ffn_g"] = cols(a["norm_mix_g_2"]), cols(a["norm_ffn_g_2"])
    o["ev_w_in"], o["ev_w_out"] = tiles_of(a["ev_w_in_2"][0]), tiles_of(a["ev_w_out_2"][0])
    o["ev_a_ln_g"], o["ev_a_ln_b"], o["ev_q_g"], o["ev_k_g"] = (a[f"ev_{k}_2"] for k in ("a_ln_g", "a_ln_b", "q_g", "k_g"))
    o["ev_a_wsT"] = np.ascontiguousarray(a["ev_a_ws_2"][0].transpose(2, 0, 1))
    o["ev_a_bsT"] = np.ascontiguousarray(a["ev_a_bs_2"][0].T)
    w = a["od_w_in_2"][0]
    wide = 2 * CK + 2 * CV
    o["od_w_in"], o["od_w_out"] = tiles_of(w[:, :wide]), tiles_of(a["od_w_out_2"][0])
    o["od_w_ga"] = np.ascontiguousarray(w[:, wide:].reshape(KT, P, CR).transpose(1, 0, 2))
    o["od_w_a2"], o["od_b_a"], o["od_head_g"] = a["od_w_a2_2"][0], a["od_b_a_2"], a["od_head_g_2"]
    for l in range(2):
        gu = np.stack([a["ffn_w_gate_2"][l], a["ffn_w_up_2"][l]])
        gu = gu.reshape(2, KT, P, FT // 2, 2 * P).transpose(3, 2, 0, 1, 4)
        o[f"ffn_gu{l}"] = np.ascontiguousarray(gu).reshape(FT // 2, P, KT * NW)
        o[f"ffn_down{l}"] = np.ascontiguousarray(a["ffn_w_down_2"][l].reshape(FT // 2, 2, P, DM).transpose(0, 2, 1, 3))
    cw = a["ffn_conv_w_2"].reshape(2, CONV, FT, P).transpose(0, 3, 2, 1)
    o["ffn_conv_w"], o["ffn_conv_b"] = np.ascontiguousarray(cw), cols(a["ffn_conv_b_2"])
    return o


def kernel(**inputs):
    import concourse.bacc as bacc
    from concourse.bass_utils import run_bass_kernel_spmd

    nc = bacc.Bacc("TRN2", target_bir_lowering=False, num_devices=1)
    arrays, d = {}, {}
    for name, a in laid_out(inputs).items():
        a = np.ascontiguousarray(a)
        arrays[f"in_{name}"] = a
        d[name] = nc.dram_tensor(f"in_{name}", a.shape, mybir.dt.from_np(a.dtype), kind="ExternalInput").ap()
    out = nc.dram_tensor("out_x", [1, NL, DM], F32, kind="ExternalOutput").ap()
    build(nc, d, out)
    r = run_bass_kernel_spmd(nc, [arrays], core_ids=[0])
    return r.results[0]["out_x"]
```

```python
from contextlib import ExitStack, contextmanager

import numpy as np
import concourse.bass as bass
from concourse import mybir

F32 = mybir.dt.float32
I32 = mybir.dt.int32
ALU = mybir.AluOpType
ACT = mybir.ActivationFunctionType
AX = mybir.AxisListType.X

P = 128
DM = 1024
KT = DM // P
NL = 256
NC = 256
LT = NL // P
TT = (NL + NC) // P
NTOK = NL + NC
E = 2048
ET = E // P
HD = 128
NH = E // HD
KVH = NH // 4
KVW = KVH * HD
NW = 512
ALPHA = (2.0 * 2) ** 0.25
LN_EPS = 1e-5
RMS_EPS = 1e-6
NEG = -1e30


class Chain:

    def __init__(self, eng, sem, passed=None):
        self.eng, self.sem, self.base, self.k, self.passed = eng, sem, 0, 0, passed

    def run(self, ins):
        ins.then_inc(self.sem, 1)
        self.k += 1
        self.eng.wait_ge(self.sem, self.base + self.k)
        if self.passed is not None:
            self.eng.sem_inc(self.passed, 1)

    @contextmanager
    def loop(self, trips, per):
        start = self.base + self.k
        with self.eng.Fori(0, trips) as i:
            self.base, self.k = i * per + start, 0
            yield i
            assert self.k == per, (self.k, per)
        self.base, self.k = start + trips * per, 0


class Core:

    def __init__(self, nc, ctx, d):
        self.nc, self.d = nc, d
        sb = lambda name, shape: ctx.enter_context(nc.sbuf_tensor(f"resident_{name}", shape, F32))
        self.ring = sb("ring", [P, 2, KT * NW])
        self.x = sb("x", [P, LT, DM])
        self.ident = sb("ident", [P, P])
        self.modT = sb("modT", [P, 2, 16, 2])
        self.eps = sb("eps", [P, 2])
        self.landed = [ctx.enter_context(nc.semaphore(f"weights_landed{s}")) for s in range(2)]
        self.spent = []
        self.used = [0, 0]

    def load(self, eng, slot, src):
        eng.dma_start(self.ring[:, slot, :], src).then_inc(self.landed[slot], 16)

    def tile(self, slot):
        return self.ring[:, slot, :].rearrange("p (k n) -> p k n", k=KT)


def phase(core, name):
    nc = core.nc

    class Ph:
        def __enter__(s):
            s.ctx, s.sems = ExitStack(), []
            return s

        def __exit__(s, *e):
            core.spent += s.sems
            if len(core.spent) > 110:
                nc.clear_and_free_semaphores(core.spent)
                nc.all_engine_barrier()
                core.spent = []
            return s.ctx.__exit__(*e)

        def sb(s, n, shape, dt=F32):
            return s.ctx.enter_context(nc.sbuf_tensor(f"{name}_{n}", shape, dt))

        def ps(s, n, shape):
            return s.ctx.enter_context(nc.psum_tensor(f"{name}_{n}", shape, F32))

        def sem(s, n):
            s.sems.append(nc.alloc_semaphore(name=f"{name}_{n}"))
            return s.sems[-1]

        def block(s):
            return nc.Block()

    return Ph()



def prefetch(core, eng, units):
    for s in range(2):
        core.load(eng, s, units[s])


def stream_loads(core, sp, tiles, groups, halves, ntt, mm_done, half_used):
    if halves == 2:
        with sp.Fori(0, groups - 1) as i:
            sp.wait_ge(half_used, i + 1)
            core.load(sp, 0, tiles[i * 2 + 2])
            sp.wait_ge(mm_done, i * ntt + ntt)
            core.load(sp, 1, tiles[i * 2 + 3])
        return
    if groups > 3:
        with sp.Fori(0, (groups - 2) // 2) as i:
            for s in range(2):
                sp.wait_ge(mm_done, i * (2 * ntt) + (s + 1) * ntt)
                core.load(sp, s, tiles[i * 2 + 2 + s])
    for u in range(2 + (groups - 2) // 2 * 2, groups):
        sp.wait_ge(mm_done, (u - 1) * ntt)
        core.load(sp, u % 2, tiles[u])


def stream_products(core, pe, groups, halves, ntt, lhs, bank, mm_done, half_used, free, rows=P, after=None):
    def group(g, parity):
        for sem, n in free:
            pe.wait_ge(sem, g * n + 1)
        for h in range(halves):
            ub = parity * halves + h
            slot = ub % 2
            nth = (g * halves + h - slot) // 2 if isinstance(g, int) else None
            if nth is None:
                turn_tiles = halves
                pe.wait_ge(core.landed[slot], turn * (16 * turn_tiles) + 16 * (core.used[slot] + ub // 2 + 1))
            else:
                pe.wait_ge(core.landed[slot], 16 * (core.used[slot] + nth + 1))
            for t in range(ntt):
                for k in range(KT):
                    last = nc.tensor.matmul(bank(parity, t)[0:rows], lhs(h * KT + k, t), core.tile(slot)[:, k, :],
                                            start=h == 0 and k == 0, stop=h == halves - 1 and k == KT - 1)
                if h == halves - 1:
                    last.then_inc(mm_done, 1)
            if h < halves - 1:
                last.then_inc(half_used, 1)

    nc = core.nc
    if groups > 3:
        with pe.Fori(0, groups // 2) as turn:
            for parity in range(2):
                group(turn * 2 + parity, parity)
        for g in range(groups // 2 * 2, groups):
            group(g, g % 2)
    else:
        for g in range(groups):
            group(g, g % 2)
    for s in range(2):
        core.used[s] += (groups * halves + 1 - s) // 2


def stream_turns(eng, groups):
    def run(body):
        if groups > 3:
            with eng.Fori(0, groups // 2) as i:
                for parity in range(2):
                    body(i * 2 + parity, parity)
            for g in range(groups // 2 * 2, groups):
                body(g, g % 2)
        else:
            for g in range(groups):
                body(g, g % 2)
    return run


def prime(eng, sem, n):
    eng.sem_inc(sem, n)


def dve_copy(nc, dst, src):
    return nc.vector.tensor_scalar(dst, src, 1.0, None, ALU.mult)


def modulation(core):
    nc, d = core.nc, core.d
    with phase(core, "ada") as ph:
        ccT = ph.sb("ccT", [P, KT, 2])
        sT = ph.sb("sT", [P, KT, 2])
        mod = ph.sb("mod", [2, 2, 3 * DM])
        bias = ph.sb("bias", [2, 2, 3 * DM])
        ps = [ph.ps(f"ps{s}", [P, 512]) for s in range(2)]
        psT = ph.ps("psT", [P, 64])
        s_in, s_silu, s_const = ph.sem("in"), ph.sem("silu"), ph.sem("const")
        mm_done, mod_done, turned = ph.sem("mm_done"), ph.sem("mod_done"), ph.sem("turned")
        modT_done, stored, biased = ph.sem("modT_done"), ph.sem("stored"), ph.sem("biased")
        NT = 2 * 3 * DM // NW
        ptab, qtab = ph.sb("ptab", [P, GD, 2, CH + 1]), ph.sb("qtab", [P, GD, 2 * CH])
        a8 = ph.sb("a8", [P, 2, GD])
        tables_done = ph.sem("tables_done")
        tables_on_scalar, tables_on_vector = s5_tables(core, ph, ptab, qtab, a8)

        with ph.block() as block:
            @block.sync
            def _(sp):
                prefetch(core, sp, d["ada_w"])
                stream_loads(core, sp, d["ada_w"], NT, 1, 1, mm_done, None)
                sp.wait_ge(mm_done, NT)
                prefetch(core, sp, d["attn_w_in"])
                sp.wait_ge(tables_done, 1)
                for dst, src in (("ptab", ptab), ("qtab", qtab), ("a8", a8)):
                    sp.dma_start(d[dst], src[:]).then_inc(stored, 16)
                sp.wait_ge(biased, 1)
                sp.dma_start(d["mod"][:].rearrange("l r n -> r l n"), mod[:]).then_inc(stored, 16)
                sp.wait_ge(stored, 64)

            @block.scalar
            def _(act):
                act.dma_start(ccT[:], d["cc"][:]).then_inc(s_in, 16)
                act.dma_start(core.ident[:], d["ident"][:]).then_inc(s_const, 16)
                for r in range(2):
                    act.dma_start(bias[r:r + 1], d["ada_b"][:].rearrange("(a l) n -> a l n", a=1)).then_inc(s_const, 16)
                for t in range(LT):
                    act.dma_start(core.x[:, t, :], d["x"][t * P:(t + 1) * P, :]).then_inc(s_const, 16)
                act.wait_ge(s_in, 16)
                nc.scalar.activation(sT[:], ccT[:], ACT.Silu).then_inc(s_silu, 1)
                tables_on_scalar(act)
                prime(act, mod_done, 2)

                def empty(g, parity):
                    act.wait_ge(mm_done, g + 1)
                    nc.scalar.activation(mod[:].rearrange("r l n -> r (l n)")[:, bass.ts(g, NW)], ps[parity][0:2, :], ACT.Copy).then_inc(mod_done, 1)
                stream_turns(act, NT)(empty)

            @block.vector
            def _(dve):
                nc.vector.memset(core.eps[:, 0:1], LN_EPS)
                nc.vector.memset(core.eps[:, 1:2], RMS_EPS)
                tables_on_vector(dve)
                dve.sem_inc(tables_done, 1)
                dve.wait_ge(s_const, 16 * (3 + LT))
                dve.wait_ge(mod_done, NT + 2)
                nc.vector.tensor_tensor(mod[:], mod[:], bias[:], ALU.add).then_inc(biased, 1)
                dve.wait_ge(turned, 1)
                nc.vector.tensor_copy(core.modT[:].rearrange("p l b r -> p (l b r)"), psT[:]).then_inc(modT_done, 1)
                dve.wait_ge(modT_done, 1)
                nc.vector.tensor_scalar(core.modT[:, :, 8:16, :], core.modT[:, :, 8:16, :], 1.0, None, ALU.add).then_inc(modT_done, 1)

            @block.tensor
            def _(pe):
                pe.wait_ge(s_silu, 1)
                stream_products(core, pe, NT, 1, 1, lambda k, t: sT[:, k, :], lambda parity, t: ps[parity],
                                mm_done, None, [(mod_done, 1)], rows=2)
                pe.wait_ge(biased, 1)
                pe.wait_ge(s_const, 16 * (3 + LT))
                for l in range(2):
                    for b in range(16):
                        c = (l * 16 + b) * 2
                        last = nc.tensor.transpose(psT[:, c:c + 2], mod[:, l, b * P:(b + 1) * P], core.ident[0:2, 0:2])
                last.then_inc(turned, 1)


def modulated_transposes(core, name, layer, hT, xc):
    nc = core.nc
    with phase(core, name) as ph:
        ps = [ph.ps(f"ps{b}", [P, NTOK]) for b in range(4)]
        turned, act_free, dve_free = ph.sem("turned"), ph.sem("act_free"), ph.sem("dve_free")
        halves = ((0, slice(0, NL)), (1, slice(NL, NTOK)))
        with ph.block() as block:
            @block.tensor
            def _(pe):
                for k in range(KT):
                    if k >= 4:
                        pe.wait_ge(dve_free if k % 2 else act_free, (k - 4) // 2 + 1)
                    for t in range(TT):
                        src = (core.x if t < LT else xc)[:, t % LT, k * P:(k + 1) * P]
                        last = nc.tensor.transpose(ps[k % 4][:, t * P:(t + 1) * P], src, core.ident[:])
                    last.then_inc(turned, 1)

            @block.scalar
            def _(act):
                for k in range(0, KT, 2):
                    act.wait_ge(turned, k + 1)
                    for r, cols in halves:
                        last = nc.scalar.activation(hT[:, k, cols], ps[k % 4][:, cols], ACT.Identity, bias=core.modT[:, layer, k, r:r + 1],
                                                    scale=core.modT[:, layer, 8 + k, r:r + 1])
                    last.then_inc(act_free, 1)

            @block.vector
            def _(dve):
                for k in range(1, KT, 2):
                    dve.wait_ge(turned, k + 1)
                    for r, cols in halves:
                        last = nc.vector.tensor_scalar(hT[:, k, cols], ps[k % 4][:, cols], core.modT[:, layer, 8 + k, r:r + 1],
                                                       core.modT[:, layer, k, r:r + 1], ALU.mult, ALU.add)
                    last.then_inc(dve_free, 1)


def attention_projection(core, hT, q, kn, v, z):
    nc, d = core.nc, core.d
    with phase(core, "qkvz") as ph:
        cos = ph.sb("cos", [P, LT, P])
        sin = ph.sb("sin", [P, LT, P])
        straight = ph.sb("straight", [P, LT, NW])
        crossed = ph.sb("crossed", [P, LT, NW])
        ps = [[ph.ps(f"ps{s}{t}", [P, NW]) for t in range(TT)] for s in range(2)]
        mm_done, act_free, dve_free, tables = ph.sem("mm_done"), ph.sem("act_free"), ph.sem("dve_free"), ph.sem("tables")
        steps, silu_done = ph.sem("steps"), ph.sem("silu_done")
        NT = (2 * E + 2 * KVW) // NW
        with ph.block() as block:
            @block.sync
            def _(sp):
                stream_loads(core, sp, d["attn_w_in"], NT, 1, TT, mm_done, None)
                sp.wait_ge(mm_done, NT * TT)
                prefetch(core, sp, d["w_out0"])

            @block.tensor
            def _(pe):
                stream_products(core, pe, NT, 1, TT, lambda k, t: hT[:, k, t * P:(t + 1) * P],
                                lambda s, t: ps[s][t], mm_done, None, [(act_free, 2), (dve_free, 2)])

            @block.scalar
            def _(act):
                act.dma_start(cos[:], d["rope_cos"][:]).then_inc(tables, 16)
                act.dma_start(sin[:], d["rope_sin"][:]).then_inc(tables, 16)
                prime(act, act_free, 3)

                def empty(g, s, dst, tiles, func):
                    for t in tiles:
                        act.wait_ge(mm_done, g * TT + t + 1)
                        nc.scalar.activation(dst(t), ps[s][t][:], func).then_inc(act_free, 1)
                with act.Fori(0, 2) as i:
                    for s in range(2):
                        empty(i * 2 + s, s, lambda t: q[:, t, bass.ts(i * 2 + s, NW)], (2, 3), ACT.Copy)
                empty(4, 0, lambda t: kn[:, t, :], (2, 3), ACT.Copy)
                empty(5, 1, lambda t: v[:, t, :], (2, 3), ACT.Copy)
                with act.Fori(0, 2) as i:
                    for s in range(2):
                        empty(i * 2 + s + 6, s, lambda t: z[:, t, bass.ts(i * 2 + s, NW)], (2, 3), ACT.Silu)
                        for t in range(LT):
                            nc.scalar.activation(z[:, t, bass.ts(i * 2 + s, NW)], ps[s][t][:], ACT.Silu).then_inc(silu_done, 1)

            @block.vector
            def _(dve):
                prime(dve, dve_free, 3)
                dve.wait_ge(tables, 32)
                chain = Chain(dve, steps)

                def rotate(g, s, dst):
                    for t in range(LT):
                        dve.wait_ge(mm_done, g * TT + t + 1)
                        x4 = ps[s][t][:].rearrange("p (h c b w) -> p h c b w", h=4, c=2, b=2)
                        y4 = crossed[:, t, :].rearrange("p (h c b w) -> p h c b w", h=4, c=2, b=2)
                        tb = lambda tab, b: tab[:, t, :].rearrange("p (c b w) -> p c b w", c=2, b=2)[:, :, b, :]
                        nc.vector.tensor_tensor(straight[:, t, :].rearrange("p (h w) -> p h w", h=4), ps[s][t][:].rearrange("p (h w) -> p h w", h=4),
                                                cos[:, t, :].unsqueeze(1).to_broadcast([P, 4, P]), ALU.mult)
                        for b in range(2):
                            last = nc.vector.tensor_tensor(y4[:, :, :, b, :], x4[:, :, :, 1 - b, :],
                                                           tb(sin, b).unsqueeze(1).to_broadcast([P, 4, 2, 32]), ALU.mult)
                        chain.run(last)
                        nc.vector.tensor_tensor(dst(t), straight[:, t, :], crossed[:, t, :], ALU.add).then_inc(dve_free, 1)
                with chain.loop(2, 4) as i:
                    for s in range(2):
                        rotate(i * 2 + s, s, lambda t: q[:, t, bass.ts(i * 2 + s, NW)])
                rotate(4, 0, lambda t: kn[:, t, :])

                def empty(g, s, dst):
                    for t in range(LT):
                        dve.wait_ge(mm_done, g * TT + t + 1)
                        nc.vector.tensor_copy(dst(t), ps[s][t][:]).then_inc(dve_free, 1)
                empty(5, 1, lambda t: v[:, t, :])
                dve.wait_ge(dve_free, 3 + 6 * LT)
                with dve.Fori(0, 2) as i:
                    for s in range(2):
                        dve.wait_ge(silu_done, i * (2 * LT) + (s + 1) * LT)
                        dve.sem_inc(dve_free, LT)


def attention(core, q, kn, v, z, kT, work, yzT):
    nc, d = core.nc, core.d
    SC = HD ** -0.5
    with phase(core, "attn") as ph:
        s_sb = work[:, 0:3, :]
        p_sb = work[:, 3:6, :]
        qs = work[:, 6, :]
        qT = work[:, 7, :]
        pT = [ph.sb(f"pT{s}", [P, 3, NW]) for s in range(2)]
        yz = ph.sb("yz", [P, TT, HD])
        mask = ph.sb("mask", [P, LT, NL])
        sink = ph.sb("sink", [P, NH])
        mx = ph.sb("mx", [P, TT])
        nm = ph.sb("nm", [P, TT])
        sk = ph.sb("sk", [P, TT])
        esk = ph.sb("esk", [P, TT])
        den = ph.sb("den", [P, TT])
        tot = ph.sb("tot", [P, TT])
        rden = [ph.sb(f"rden{s}", [P, TT]) for s in range(2)]
        ps_t = ph.ps("ps_t", [P, NW])
        ps_s = [ph.ps(f"ps_s{b}", [P, NW]) for b in range(3)]
        ps_p = [ph.ps(f"ps_p{b}", [P, NW]) for b in range(3)]
        ps_y = ph.ps("ps_y", [P, TT, HD])
        names = ["qs_ready", "q_turned", "qT_ready", "scores_ready", "max_ready", "exp_ready", "p_turned",
                 "pT_act", "pT_dve", "pv_ready", "yz_ready", "yz_turned", "yzT_ready", "k_turned", "kT_ready",
                 "loads", "steps"]
        (qs_ready, q_turned, qT_ready, scores_ready, max_ready, exp_ready, p_turned, pT_act, pT_dve, pv_ready,
         yz_ready, yz_turned, yzT_ready, k_turned, kT_ready, loads, steps) = [ph.sem(n) for n in names]
        ident = core.ident

        def schedule(eng, chain, per, step):
            for i in (-1, 0, 1):
                step(i, i % 2)
            turns = (NH - 4) // 2
            loop = chain.loop(turns, per) if chain else eng.Fori(0, turns)
            with loop as n:
                for s in range(2):
                    step(n * 2 + 2 + s, s)
            for i in range(2 + 2 * turns, NH + 2):
                step(i, i % 2)

        def exists(i, shift=0):
            return not isinstance(i, int) or 0 <= i + shift < NH

        with ph.block() as block:
            @block.gpsimd
            def _(pool):
                heads = lambda h: nc.gpsimd.tensor_copy(qs.rearrange("p (t w) -> p t w", t=TT), q[:, :, bass.ts(h, HD)]).then_inc(qs_ready, 1)
                heads(0)
                with pool.Fori(0, NH - 1) as h:
                    pool.wait_ge(q_turned, h + 1)
                    heads(h + 1)

            @block.tensor
            def _(pe):
                for g in range(KVH):
                    if g >= 3:
                        pe.wait_ge(kT_ready, g - 2)
                    for t in range(TT):
                        last = nc.tensor.transpose(ps_s[g % 3][:, t * P:(t + 1) * P], kn[:, t, g * HD:(g + 1) * HD], ident[:])
                    last.then_inc(k_turned, 1)

                def turn_queries(h):
                    pe.wait_ge(qs_ready, h + 1)
                    pe.wait_ge(qT_ready, h + 1)
                    pe.wait_ge(yzT_ready, h + 1)
                    for t in range(TT):
                        last = nc.tensor.transpose(ps_t[:, t * P:(t + 1) * P], qs[:, t * P:(t + 1) * P], ident[:])
                    last.then_inc(q_turned, 1)

                def scores(h):
                    pe.wait_ge(qT_ready, h + 2)
                    pe.wait_ge(max_ready, h + 1)
                    for t in range(LT):
                        nc.tensor.matmul(ps_s[t][:], qT[:, t * P:(t + 1) * P], kT[:, h // 4, :], start=True, stop=True)
                    for t in range(2):
                        last = nc.tensor.matmul(ps_s[2][:, t * NC:(t + 1) * NC], qT[:, (LT + t) * P:(LT + t + 1) * P],
                                                kT[:, h // 4, NL:NTOK], start=True, stop=True)
                    last.then_inc(scores_ready, 1)

                def turn_probabilities(h):
                    pe.wait_ge(exp_ready, h + 1)
                    pe.wait_ge(pT_act, h + 1)
                    pe.wait_ge(pT_dve, h * 2 + 1)
                    for b in range(3):
                        for j in range(4):
                            last = nc.tensor.transpose(ps_p[b][:, j * P:(j + 1) * P], p_sb[:, b, j * P:(j + 1) * P], ident[:])
                        last.then_inc(p_turned, 1)

                def mix(h, s):
                    pe.wait_ge(pT_act, h + 2)
                    pe.wait_ge(pT_dve, h * 2 + 3)
                    pe.wait_ge(yz_ready, h + 1)
                    vcols = bass.ts(h // 4, HD)
                    for t in range(LT):
                        for j in range(4):
                            nc.tensor.matmul(ps_y[:, t, :], pT[s][:, t, j * P:(j + 1) * P], v[:, j, vcols], start=j == 0, stop=j == 3)
                    for t in range(2):
                        for j in range(2):
                            last = nc.tensor.matmul(ps_y[:, LT + t, :], pT[s][:, 2, (t * 2 + j) * P:(t * 2 + j + 1) * P],
                                                    v[:, LT + j, vcols], start=j == 0, stop=j == 1)
                    last.then_inc(pv_ready, 1)

                def turn_outputs(h):
                    pe.wait_ge(yz_ready, h + 2)
                    pe.wait_ge(yzT_ready, h + 4)
                    pe.wait_ge(qT_ready, min(h + 5, NH + 1) if isinstance(h, int) else h + 5)
                    for t in range(TT):
                        last = nc.tensor.transpose(ps_t[:, t * P:(t + 1) * P], yz[:, t, :], ident[:])
                    last.then_inc(yz_turned, 1)

                prime(pe, p_turned, 1)
                prime(pe, scores_ready, 1)
                prime(pe, pv_ready, 2)
                prime(pe, yz_turned, 1)
                turn_queries(0)
                pe.wait_ge(kT_ready, KVH)

                def step(i, s):
                    if exists(i, 1):
                        scores(i + 1)
                    if exists(i, -2):
                        turn_outputs(i - 2)
                    if exists(i):
                        turn_probabilities(i)
                    if exists(i, 2):
                        turn_queries(i + 2)
                    if exists(i, -1):
                        mix(i - 1, 1 - s)
                schedule(pe, None, 0, step)

            @block.scalar
            def _(act):
                act.dma_start(mask[:], d["attn_mask"][:]).then_inc(loads, 16)
                act.dma_start(sink[:], d["attn_sink"][0:1, :].to_broadcast([P, NH])).then_inc(loads, 16)
                prime(act, pT_act, 1)
                prime(act, qT_ready, 1)
                prime(act, yzT_ready, 4)
                for g in range(KVH):
                    act.wait_ge(k_turned, g + 1)
                    nc.scalar.activation(kT[:, g, :], ps_s[g % 3][:], ACT.Copy).then_inc(kT_ready, 1)

                def queries(h):
                    act.wait_ge(q_turned, h + 1)
                    act.wait_ge(scores_ready, h + 1)
                    nc.scalar.activation(qT[:], ps_t[:], ACT.Copy).then_inc(qT_ready, 1)

                def exponentials(h):
                    act.wait_ge(max_ready, h + 2)
                    act.wait_ge(p_turned, h * 3 + 1)
                    for t in range(TT):
                        src = s_sb[:, t, :] if t < LT else s_sb[:, 2, (t - LT) * NC:(t - LT + 1) * NC]
                        dst = p_sb[:, t, :] if t < LT else p_sb[:, 2, (t - LT) * NC:(t - LT + 1) * NC]
                        nc.scalar.activation(dst, src, ACT.Exp, bias=nm[:, t:t + 1], accum_out=den[:, t:t + 1])
                    nc.scalar.activation(esk[:], sk[:], ACT.Exp).then_inc(exp_ready, 1)

                def step(i, s):
                    if exists(i, -2):
                        act.wait_ge(yz_turned, i)
                        nc.scalar.activation(yzT[:, i - 2, :], ps_t[:], ACT.Copy).then_inc(yzT_ready, 1)
                    if exists(i):
                        act.wait_ge(p_turned, i * 3 + 2)
                        act.wait_ge(pv_ready, i + 1)
                        nc.scalar.activation(pT[s][:, 0, :], ps_p[0][:], ACT.Copy).then_inc(pT_act, 1)
                    if exists(i, 2):
                        queries(i + 2)
                    if exists(i, 1):
                        exponentials(i + 1)
                act.wait_ge(q_turned, 1)
                nc.scalar.activation(qT[:], ps_t[:], ACT.Copy).then_inc(qT_ready, 1)
                schedule(act, None, 0, step)

            @block.vector
            def _(dve):
                chain = Chain(dve, steps)
                prime(dve, pT_dve, 1)
                prime(dve, max_ready, 1)
                prime(dve, yz_ready, 1)
                dve.wait_ge(loads, 32)

                def maxima(h):
                    dve.wait_ge(scores_ready, h + 2)
                    for t in range(LT):
                        nc.vector.scalar_tensor_tensor(out=s_sb[:, t, 0:NL], in0=ps_s[t][:, 0:NL], scalar=SC, in1=mask[:, t, :], op0=ALU.mult, op1=ALU.add)
                        nc.vector.tensor_scalar(s_sb[:, t, NL:NTOK], ps_s[t][:, NL:NTOK], SC, None, ALU.mult)
                    chain.run(nc.vector.tensor_scalar(s_sb[:, 2, :], ps_s[2][:], SC, None, ALU.mult))
                    nc.vector.tensor_reduce(mx[:, 0:LT], s_sb[:, 0:LT, :], AX, ALU.max)
                    chain.run(nc.vector.tensor_reduce(mx[:, LT:TT], s_sb[:, 2, :].rearrange("p (t w) -> p t w", t=2), AX, ALU.max))
                    chain.run(nc.vector.tensor_scalar(nm[:], mx[:], sink[:, bass.ds(h, 1)], -1.0, ALU.max, ALU.mult))
                    nc.vector.tensor_scalar(sk[:], nm[:], sink[:, bass.ds(h, 1)], None, ALU.add).then_inc(max_ready, 1)

                def step(i, s):
                    if exists(i):
                        dve.wait_ge(exp_ready, i + 1)
                        chain.run(nc.vector.tensor_tensor(tot[:], den[:], esk[:], ALU.add))
                        chain.run(nc.vector.reciprocal(rden[s][:], tot[:]))
                    if exists(i, 1):
                        maxima(i + 1)
                    if exists(i):
                        for b in (1, 2):
                            dve.wait_ge(p_turned, i * 3 + 2 + b)
                            if b == 1:
                                dve.wait_ge(pv_ready, i + 1)
                            nc.vector.tensor_copy(pT[s][:, b, :], ps_p[b][:]).then_inc(pT_dve, 1)
                    if exists(i, -1):
                        dve.wait_ge(pv_ready, i + 2)
                        dve.wait_ge(yz_turned, i)
                        for t in range(TT):
                            last = nc.vector.scalar_tensor_tensor(out=yz[:, t, :], in0=ps_y[:, t, :], scalar=rden[1 - s][:, t:t + 1],
                                                                  in1=z[:, t, bass.ts(i - 1, HD)], op0=ALU.mult, op1=ALU.mult)
                        last.then_inc(yz_ready, 1)
                schedule(dve, chain, 10, step)


def layer_norm_tile(core, chain, act_rstd, t, x, stats, mv, rstd, g_row, b_row):
    nc = core.nc
    for c in range(2):
        last = nc.vector.bn_stats(stats[:, c, :], x[:, c * NW:(c + 1) * NW])
    chain.run(last)
    chain.run(nc.vector.bn_aggr(mv[:], stats[:]))
    act_rstd()
    chain.run(nc.vector.reciprocal(rstd[:], rstd[:]))
    chain.run(nc.vector.tensor_scalar(x, x, mv[:, 0:1], rstd[:, 0:1], ALU.subtract, ALU.mult))
    chain.run(nc.vector.tensor_tensor(x, x, g_row[:], ALU.mult))
    chain.run(nc.vector.tensor_tensor(x, x, b_row[:], ALU.add))


def residual_norm(core, name, layer, weights, tiles, xs, lhsT, following):
    nc, d = core.nc, core.d
    n = len(xs)
    with phase(core, name) as ph:
        rows = sorted({r for _, r in xs})
        gate = ph.sb("gate", [P, 2, DM])
        g_row = ph.sb("g_row", [P, DM])
        b_row = ph.sb("b_row", [P, DM])
        stats = ph.sb("stats", [P, 2, 6])
        mv = ph.sb("mv", [P, 2])
        rstd = ph.sb("rstd", [P, 1])
        tmp = ph.sb("tmp", [P, NW])
        ps = [[ph.ps(f"ps{s}{t}", [P, NW]) for t in range(n)] for s in range(2)]
        names = ["mm_done", "half_used", "rows_ready", "steps", "var_ready", "std_ready", "ready"]
        mm_done, half_used, rows_ready, steps, var_ready, std_ready, ready = [ph.sem(x) for x in names]
        with ph.block() as block:
            @block.sync
            def _(sp):
                stream_loads(core, sp, d[weights], 2, 2, n, mm_done, half_used)
                sp.wait_ge(mm_done, 2 * n)
                if following:
                    prefetch(core, sp, d[following])

            @block.tensor
            def _(pe):
                stream_products(core, pe, 2, 2, n, lhsT, lambda s, t: ps[s][t], mm_done, half_used, [])

            @block.scalar
            def _(act):
                for r in rows:
                    act.dma_start(gate[:, r, :], d["mod"][layer:layer + 1, r, 2 * DM:3 * DM].to_broadcast([P, DM])).then_inc(rows_ready, 16)
                act.dma_start(g_row[:], d["ln_g"][layer:layer + 1, :].to_broadcast([P, DM])).then_inc(rows_ready, 16)
                act.dma_start(b_row[:], d["ln_b"][layer:layer + 1, :].to_broadcast([P, DM])).then_inc(rows_ready, 16)
                for t in range(n):
                    act.wait_ge(var_ready, t + 1)
                    nc.scalar.activation(rstd[:], mv[:, 1:2], ACT.Sqrt, bias=core.eps[:, 0:1]).then_inc(std_ready, 1)

            @block.vector
            def _(dve):
                chain = Chain(dve, steps)
                dve.wait_ge(rows_ready, 16 * (2 + len(rows)))
                for s in range(2):
                    for t in range(n):
                        x, r = xs[t]
                        cols = slice(s * NW, (s + 1) * NW)
                        dve.wait_ge(mm_done, s * n + t + 1)
                        chain.run(nc.vector.tensor_tensor(tmp[:], ps[s][t][:], gate[:, r, cols], ALU.mult))
                        chain.run(nc.vector.scalar_tensor_tensor(out=x[:, cols], in0=x[:, cols], scalar=ALPHA, in1=tmp[:], op0=ALU.mult, op1=ALU.add))
                for t in range(n):
                    def rstd_of(t=t):
                        dve.sem_inc(var_ready, 1)
                        dve.wait_ge(std_ready, t + 1)
                    layer_norm_tile(core, chain, rstd_of, t, xs[t][0], stats, mv, rstd, g_row, b_row)


SG = 16
SN = E // SG
SS = 64
CH = 8
LC, CC = NL // CH, NC // CH
GD = 2 * SN
BG = 4
BD = 2 * BG
NB = SN // BG
TWO_PI = 6.283185307179586
TP1 = 6.28125
TP2 = float(np.float32(np.floor((TWO_PI - TP1) * 2 ** 20) / 2 ** 20))
TP3 = float(TWO_PI - TP1 - TP2)
ROUND = 12582912.0
PI_BELOW = 3.1415925


def s5_projection(core, hT, ptab, qtab, a8):
    nc, d = core.nc, core.d
    with phase(core, "s5in") as ph:
        u = ph.sb("u", [P, TT, E])
        ps = [[ph.ps(f"ps{s}{t}", [P, NW]) for t in range(TT)] for s in range(2)]
        mm_done, act_free, dve_free, stored, tables = [ph.sem(x) for x in ("mm_done", "act_free", "dve_free", "stored", "tables")]
        G = E // NW
        with ph.block() as block:
            @block.sync
            def _(sp):
                stream_loads(core, sp, d["s5_w_in"], G, 1, TT, mm_done, None)
                for dst, src in ((ptab, "ptab"), (qtab, "qtab"), (a8, "a8")):
                    sp.dma_start(dst[:], d[src]).then_inc(tables, 16)
                for g in range(G):
                    sp.wait_ge(act_free, 3 + 2 * (g + 1))
                    sp.wait_ge(dve_free, 3 + 2 * (g + 1))
                    cols = slice(g * NW, (g + 1) * NW)
                    sp.dma_start(d["u"].rearrange("(t p) n -> p t n", p=P)[:, :, cols], u[:, :, cols]).then_inc(stored, 16)
                sp.wait_ge(stored, 16 * G)
                sp.wait_ge(tables, 48)

            @block.tensor
            def _(pe):
                stream_products(core, pe, G, 1, TT, lambda k, t: hT[:, k, t * P:(t + 1) * P],
                                lambda s, t: ps[s][t], mm_done, None, [(act_free, 2), (dve_free, 2)])

            @block.scalar
            def _(act):
                prime(act, act_free, 3)

                def empty(g, s):
                    for t in (2, 3):
                        act.wait_ge(mm_done, g * TT + t + 1)
                        nc.scalar.activation(u[:, t, bass.ts(g, NW)], ps[s][t][:], ACT.Copy).then_inc(act_free, 1)
                stream_turns(act, G)(empty)

            @block.vector
            def _(dve):
                prime(dve, dve_free, 3)

                def empty(g, s):
                    for t in range(LT):
                        dve.wait_ge(mm_done, g * TT + t + 1)
                        dve_copy(nc, u[:, t, bass.ts(g, NW)], ps[s][t][:]).then_inc(dve_free, 1)
                stream_turns(dve, G)(empty)


def s5_tables(core, ph, ptab, qtab, a8):
    nc, d = core.nc, core.d
    names = "lr li dt er ei k ea r absr co si pr pi nr ni den sr si2 t1 t2 t3 t4".split()
    T = {n: ph.sb(n, [P, GD]) for n in names}
    V = lambda n: T[n][:]
    half_pi = ph.sb("half_pi", [P, 1])
    loads, steps, to_act, from_act = [ph.sem(x) for x in ("loads", "steps", "to_act", "from_act")]
    def on_scalar(act):
        act.dma_start(T["lr"][:], d["s5_lam_re"][:]).then_inc(loads, 16)
        act.dma_start(T["li"][:], d["s5_lam_im"][:]).then_inc(loads, 16)
        act.dma_start(T["dt"][:], d["s5_log_step"][:].to_broadcast([P, GD])).then_inc(loads, 16)
        act.wait_ge(loads, 48)
        nc.scalar.activation(V("dt"), V("dt"), ACT.Exp).then_inc(from_act, 1)
        act.wait_ge(to_act, 1)
        nc.scalar.activation(V("ea"), V("er"), ACT.Exp).then_inc(from_act, 1)
        act.wait_ge(to_act, 2)
        nc.scalar.activation(V("si"), V("r"), ACT.Sin)
        nc.scalar.activation(V("co"), V("absr"), ACT.Sin, scale=-1.0, bias=half_pi[:, 0:1]).then_inc(from_act, 1)

    def on_vector(dve):
        chain = Chain(dve, steps)
        v = nc.vector
        lo, hi = slice(0, SS), slice(SS, P)

        def mul(o, a, b):
            chain.run(v.tensor_tensor(o, a, b, ALU.mult))

        def add(o, a, b, op=ALU.add):
            chain.run(v.tensor_tensor(o, a, b, op))
        chain.run(v.memset(half_pi[:], TWO_PI / 4))
        dve.wait_ge(loads, 48)
        dve.wait_ge(from_act, 1)
        mul(V("er"), V("lr"), V("dt"))
        dve.sem_inc(to_act, 1)
        mul(V("ei"), V("li"), V("dt"))
        chain.run(v.tensor_scalar(V("k"), V("ei"), 1.0 / TWO_PI, ROUND, ALU.mult, ALU.add))
        chain.run(v.tensor_scalar(V("k"), V("k"), -ROUND, None, ALU.add))
        chain.run(v.scalar_tensor_tensor(out=V("r"), in0=V("k"), scalar=-TP1, in1=V("ei"), op0=ALU.mult, op1=ALU.add))
        for part in (TP2, TP3):
            chain.run(v.scalar_tensor_tensor(out=V("r"), in0=V("k"), scalar=-part, in1=V("r"), op0=ALU.mult, op1=ALU.add))
        chain.run(v.tensor_scalar(V("r"), V("r"), PI_BELOW, -PI_BELOW, ALU.min, ALU.max))
        chain.run(v.tensor_scalar(V("t1"), V("r"), -1.0, None, ALU.mult))
        add(V("absr"), V("r"), V("t1"), ALU.max)
        dve.sem_inc(to_act, 1)
        dve.wait_ge(from_act, 3)
        mul(V("co"), V("co"), V("ea"))
        mul(V("si"), V("si"), V("ea"))
        chain.run(v.tensor_scalar(V("nr"), V("co"), -1.0, None, ALU.add))
        mul(V("t1"), V("lr"), V("lr"))
        mul(V("t2"), V("li"), V("li"))
        add(V("den"), V("t1"), V("t2"))
        chain.run(v.reciprocal(V("den"), V("den")))
        mul(V("t1"), V("nr"), V("lr"))
        mul(V("t2"), V("si"), V("li"))
        add(V("sr"), V("t1"), V("t2"))
        mul(V("sr"), V("sr"), V("den"))
        mul(V("t1"), V("si"), V("lr"))
        mul(V("t2"), V("nr"), V("li"))
        add(V("si2"), V("t1"), V("t2"), ALU.subtract)
        mul(V("si2"), V("si2"), V("den"))
        v.memset(V("pr"), 1.0)
        chain.run(v.memset(V("pi"), 0.0))
        by_dir = lambda ap: ap.rearrange("p (g r) -> p g r", r=2)
        slot = lambda tab, *at: tab[(slice(None), slice(None), *at)].rearrange("p (g r) -> p g r", r=2)
        for n in range(CH + 1):
            for r in range(2):
                k = n if r == 0 else CH - n
                dst_r = ptab[:, :, 0, k].rearrange("p (g r) -> p g r", r=2)[:, :, r]
                dst_i = ptab[:, :, 1, k].rearrange("p (g r) -> p g r", r=2)[:, :, r]
                v.tensor_copy(dst_r[lo], by_dir(V("pr"))[lo, :, r])
                v.tensor_scalar(dst_r[hi], by_dir(V("pr"))[hi, :, r], -1.0, None, ALU.mult)
                v.tensor_scalar(dst_i, by_dir(V("pi"))[:, :, r], -1.0, None, ALU.mult)
            if n < CH:
                v.tensor_tensor(V("t1"), V("pr"), V("sr"), ALU.mult)
                mul(V("t2"), V("pi"), V("si2"))
                v.tensor_tensor(V("t1"), V("t1"), V("t2"), ALU.subtract)
                v.tensor_tensor(V("t3"), V("pr"), V("si2"), ALU.mult)
                mul(V("t4"), V("pi"), V("sr"))
                add(V("t3"), V("t3"), V("t4"))
                for r in range(2):
                    i = n if r == 0 else CH - 1 - n
                    dst_r = qtab[:, :, i].rearrange("p (g r) -> p g r", r=2)[:, :, r]
                    dst_i = qtab[:, :, CH + i].rearrange("p (g r) -> p g r", r=2)[:, :, r]
                    v.tensor_copy(dst_r, by_dir(V("t1"))[:, :, r])
                    v.tensor_scalar(dst_i[lo], by_dir(V("t3"))[lo, :, r], -1.0, None, ALU.mult)
                    last = v.tensor_copy(dst_i[hi], by_dir(V("t3"))[hi, :, r])
                chain.run(last)
                v.tensor_tensor(V("t1"), V("pr"), V("co"), ALU.mult)
                v.tensor_tensor(V("t2"), V("pi"), V("si"), ALU.mult)
                v.tensor_tensor(V("t3"), V("pr"), V("si"), ALU.mult)
                mul(V("t4"), V("pi"), V("co"))
                v.tensor_tensor(V("pr"), V("t1"), V("t2"), ALU.subtract)
                add(V("pi"), V("t3"), V("t4"))
        v.tensor_copy(a8[:, 0, :], V("pr"))
        v.tensor_copy(a8[lo, 1, :], T["pi"][lo])
        chain.run(v.tensor_scalar(a8[hi, 1, :], T["pi"][hi], -1.0, None, ALU.mult))
    return on_scalar, on_vector


def s5_chunk_inputs(core, qtab, S, u8):
    nc, d = core.nc, core.d
    with phase(core, "s5a") as ph:
        def two(n, shape):
            return [ph.sb(f"{n}{s}", shape) for s in range(2)]
        bab = two("bab", [P, 2, BD, SG])
        uc = two("uc", [LC + CC, CH, BG * SG])
        uo = two("uo", [LC + CC, BG, P])
        ub = two("ub", [P, BG, LC + CC])
        w = two("w", [P, BD, P])
        wT = two("wT", [P, BD, P])
        parts = [[core.ring[:, s, m * BD * P:(m + 1) * BD * P].rearrange("p (g w) -> p g w", g=BD) for m in range(2)] for s in range(2)]
        ps_u = ph.ps("ps_u", [P, BG, LC + CC])
        ps_w = [ph.ps(f"ps_w{i}", [P, BG, P]) for i in range(2)]
        ps_s = [ph.ps(f"ps_s{i}", [P, BD, LC + CC]) for i in range(2)]
        names = "t1_made t2_made w_made turned u_ordered ub_ready wT_ready s_made s_kept u_kept passed".split()
        t1_made, t2_made, w_made, turned, u_ordered, ub_ready, wT_ready, s_made, s_kept, u_kept, passed = [ph.sem(n) for n in names]
        b_landed, u_landed = [[ph.sem(f"{n}{s}") for s in range(2)] for n in ("b_landed", "u_landed")]
        cols = lambda b: bass.ts(b, BD)
        ident = core.ident
        spread_q = lambda b, part: qtab[:, cols(b), part * CH:(part + 1) * CH].unsqueeze(3).to_broadcast([P, BD, CH, SG])
        spread_b = lambda s, part: bab[s][:, part].unsqueeze(2).to_broadcast([P, BD, CH, SG])
        by_token = lambda m: m.rearrange("p g (i m) -> p g i m", i=CH)
        HB = NB // 2

        def steps(eng, step, lead):
            for b in range(-lead, 0):
                step(b, b % 2, None)
            with eng.Fori(0, HB - 1) as n:
                for s in range(2):
                    step(n * 2 + s, s, n)
            for b in (NB - 2, NB - 1):
                step(b, b % 2, HB - 1)

        def exists(b, shift):
            return not isinstance(b, int) or 0 <= b + shift < NB

        with ph.block() as block:
            @block.sync
            def _(sp):
                def loads(b, s):
                    sp.dma_start(bab[s][:], d["s5_bab"][b]).then_inc(b_landed[s], 16)
                    sp.dma_start(uc[s][:], d["u"].rearrange("(c i) n -> c i n", i=CH)[:, :, bass.ts(b, BG * SG)]).then_inc(u_landed[s], 16)
                for s in range(2):
                    loads(s, s)
                with sp.Fori(0, HB - 1) as n:
                    for s in range(2):
                        b = n * 2 + s
                        sp.wait_ge(t1_made, b + 1)
                        sp.wait_ge(t2_made, b + 1)
                        sp.wait_ge(u_ordered, b + 1)
                        loads(b + 2, s)
                sp.wait_ge(w_made, NB + 2)
                prefetch(core, sp, d["s5_w_z"])

            @block.gpsimd
            def _(pool):
                with pool.Fori(0, HB) as n:
                    for s in range(2):
                        b = n * 2 + s
                        pool.wait_ge(b_landed[s], n * 16 + 16)
                        pool.wait_ge(w_made, b + 1)
                        pool.sem_inc(passed, 1)
                        nc.gpsimd.tensor_tensor(by_token(parts[s][1]), spread_q(b, 1), spread_b(s, 1), ALU.mult).then_inc(t2_made, 1)

            @block.vector
            def _(dve):
                prime(dve, s_kept, 2)
                prime(dve, w_made, 2)
                lat, con = slice(0, LC), slice(LC, LC + CC)

                def weights(b, s, n):
                    dve.wait_ge(b_landed[s], n * 16 + 16)
                    dve.wait_ge(w_made, b + 1)
                    nc.vector.tensor_tensor(by_token(parts[s][0]), spread_q(b, 0), spread_b(s, 0), ALU.mult).then_inc(t1_made, 1)
                    dve.wait_ge(t1_made, b + 1)
                    dve.wait_ge(t2_made, b + 1)
                    dve.wait_ge(turned, b + 1)
                    dve.wait_ge(u_kept, b + 1)
                    nc.vector.tensor_tensor(w[s][:], parts[s][0], parts[s][1], ALU.add).then_inc(w_made, 1)

                def step(b, s, n):
                    if exists(b, 2):
                        weights(b + 2, s, 0 if n is None else n + 1)
                    if exists(b, 0):
                        dve.wait_ge(s_made, b + 3)
                        by_dir = lambda r, steps: S[:, steps, cols(b)].rearrange("p s (g r) -> p g s r", r=2)[:, :, :, r]
                        of_dir = lambda r, chunks: ps_s[s][:].rearrange("p (g r) c -> p g r c", r=2)[:, :, r, chunks]
                        dve_copy(nc, by_dir(0, slice(CC, CC + LC)), of_dir(0, lat))
                        nc.vector.tensor_copy(by_dir(0, slice(0, CC)), of_dir(0, con))
                        nc.vector.tensor_copy(by_dir(1, slice(CC, CC + LC)), of_dir(1, lat)[:, :, ::-1])
                        nc.vector.tensor_copy(by_dir(1, slice(0, CC)), of_dir(1, con)[:, :, ::-1]).then_inc(s_kept, 1)
                steps(dve, step, 2)

            @block.scalar
            def _(act):
                prime(act, ub_ready, 1)
                prime(act, wT_ready, 1)
                prime(act, u_kept, 2)

                def order(b, s, n):
                    act.wait_ge(u_landed[s], n * 16 + 16)
                    act.wait_ge(turned, b + 1)
                    nc.scalar.activation(uo[s][:].rearrange("c g (i m) -> c g i m", i=CH)[:, :, ::-1, :],
                                         uc[s][:].rearrange("c i (g m) -> c g i m", g=BG), ACT.Copy).then_inc(u_ordered, 1)

                def step(b, s, n):
                    if exists(b, 2):
                        order(b + 2, s, 0 if n is None else n + 1)
                    if exists(b, 1):
                        act.wait_ge(turned, b + 4)
                        act.wait_ge(s_made, b + 2)
                        for i in range(2):
                            nc.scalar.activation(wT[1 - s][:, i * BG:(i + 1) * BG, :], ps_w[i][:], ACT.Copy)
                        nc.scalar.activation(ub[1 - s][:], ps_u[:], ACT.Copy).then_inc(wT_ready, 1)
                        for r, i in ((0, 0), (1, CH - 1)):
                            last = nc.scalar.activation(qtab[:, cols(b + 1), :].rearrange("p (g r) m -> p g r m", r=2)[:, :, r, :],
                                                        w[1 - s][:].rearrange("p (g r) m -> p g r m", r=2)[:, :, r, i * SG:(i + 1) * SG], ACT.Copy)
                        act.wait_ge(wT_ready, b + 3)
                        nc.scalar.activation(u8[:, bass.ts(b + 1, BG), :], ub[1 - s][:, :, 0:LC], ACT.Copy).then_inc(u_kept, 1)
                steps(act, step, 2)

            @block.tensor
            def _(pe):
                prime(pe, s_made, 2)
                prime(pe, turned, 2)

                def step(b, s, n):
                    if exists(b, 1):
                        pe.wait_ge(w_made, b + 4)
                        pe.wait_ge(u_ordered, b + 2)
                        pe.wait_ge(wT_ready, b + 2)
                        for c in range(BD):
                            nc.tensor.transpose(ps_w[c // BG][:, c % BG, :], w[1 - s][:, c, :], ident[:])
                        for g in range(BG):
                            last = nc.tensor.transpose(ps_u[:, g, :], uo[1 - s][:, g, :], ident[0:LC + CC, 0:LC + CC])
                        last.then_inc(turned, 1)
                    if exists(b, 0):
                        pe.wait_ge(wT_ready, b + 2)
                        pe.wait_ge(s_kept, b + 1)
                        for c in range(BD):
                            last = nc.tensor.matmul(ps_s[s][:, c, :], wT[s][:, c, :], ub[s][:, c // 2, :], start=True, stop=True)
                        last.then_inc(s_made, 1)
                steps(pe, step, 2)


def s5_carry(core, a8, S, hT):
    nc, d = core.nc, core.d
    CUT = (0, 96, 192, GD)
    with phase(core, "s5c") as ph:
        t1, t2 = ph.sb("t1", [P, GD]), ph.sb("t2", [P, GD])
        zb = [ph.sb(f"zb{s}", [P, LT, NW]) for s in range(2)]
        ps = [[ph.ps(f"ps{s}{t}", [P, NW]) for t in range(LT)] for s in range(2)]
        one, two, three, pool_steps, pool_passed, mm_done, z_made = [ph.sem(n) for n in "one two three pool_steps pool_passed mm_done z_made".split()]
        stored = [ph.sem(f"stored{s}") for s in range(2)]
        lo, hi = slice(0, SS), slice(SS, P)
        STEPS = CC + LC - 2
        G = E // NW

        def carry(dve, j, c, n):
            ops = nc.vector

            def rotate():
                dve.wait_ge(three, j * 2 + n + 1)
                ops.tensor_tensor(t1[:, c], a8[:, 0, c], S[:, j, c], ALU.mult)
                ops.tensor_tensor(t2[lo, c], a8[hi, 1, c], S[hi, j, c], ALU.mult)
                ops.tensor_tensor(t2[hi, c], a8[lo, 1, c], S[lo, j, c], ALU.mult).then_inc(one, 1)

            def join():
                dve.wait_ge(one, j * 2 + n + 1)
                ops.tensor_tensor(t1[:, c], t1[:, c], t2[:, c], ALU.add).then_inc(two, 1)

            def add():
                dve.wait_ge(two, j * 2 + n + 1)
                ops.tensor_tensor(S[:, j + 1, c], S[:, j + 1, c], t1[:, c], ALU.add).then_inc(three, 1)
            return rotate, join, add

        with ph.block() as block:
            @block.vector
            def _(dve):
                prime(dve, three, 2)
                halves = [slice(CUT[0], CUT[1]), slice(CUT[1], CUT[2])]
                with dve.Fori(0, STEPS) as j:
                    parts = [carry(dve, j, c, n) for n, c in enumerate(halves)]
                    for k in range(3):
                        for n in range(2):
                            parts[n][k]()

            @block.gpsimd
            def _(pool):
                chain = Chain(pool, pool_steps, pool_passed)
                c, ops = slice(CUT[2], CUT[3]), nc.gpsimd
                with chain.loop(STEPS, 5) as j:
                    chain.run(ops.tensor_tensor(t1[:, c], a8[:, 0, c], S[:, j, c], ALU.mult))
                    chain.run(ops.tensor_tensor(t2[lo, c], a8[hi, 1, c], S[hi, j, c], ALU.mult))
                    chain.run(ops.tensor_tensor(t2[hi, c], a8[lo, 1, c], S[lo, j, c], ALU.mult))
                    chain.run(ops.tensor_tensor(t1[:, c], t1[:, c], t2[:, c], ALU.add))
                    chain.run(ops.tensor_tensor(S[:, j + 1, c], S[:, j + 1, c], t1[:, c], ALU.add))

            @block.sync
            def _(sp):
                stream_loads(core, sp, d["s5_w_z"], G, 1, LT, mm_done, None)
                for g in range(G):
                    sp.wait_ge(z_made, LT + 1 + (g + 1) * LT)
                    sp.dma_start(d["z"].rearrange("(t p) n -> p t n", p=P)[:, :, g * NW:(g + 1) * NW], zb[g % 2][:]).then_inc(stored[g % 2], 16)
                for s in range(2):
                    sp.wait_ge(stored[s], 16 * G // 2)

            @block.scalar
            def _(act):
                prime(act, z_made, LT + 1)
                for g in range(G):
                    if g >= 2:
                        act.wait_ge(stored[g % 2], 16 * (g // 2))
                    for t in range(LT):
                        act.wait_ge(mm_done, g * LT + t + 1)
                        nc.scalar.activation(zb[g % 2][:, t, :], ps[g % 2][t][:], ACT.Silu).then_inc(z_made, 1)

            @block.tensor
            def _(pe):
                stream_products(core, pe, G, 1, LT, lambda k, t: hT[:, k, t * P:(t + 1) * P],
                                lambda s, t: ps[s][t], mm_done, None, [(z_made, LT)])


def s5_outputs(core, ptab, bbar, S, u8):
    nc, d = core.nc, core.d
    W9 = (CH + 1) * SG
    EW = (2 * CH - 1) * SG
    NV = 4
    with phase(core, "s5d") as ph:
        def two(n, shape):
            return [ph.sb(f"{n}{s}", shape) for s in range(2)]
        cab = two("cab", [P, 2, BD, SG])
        V = [ph.sb(f"V{s}", [P, BD, W9]) for s in range(NV)]
        bs, hs, us = two("bs", [P, BD, SG]), two("hs", [P, BD, LC]), two("us", [P, BG, LC])
        T = two("T", [P, BG, P])
        yb = two("yb", [LC, CH, BG * SG])
        parts = [[core.ring[:, s, m * BD * W9:(m + 1) * BD * W9].rearrange("p (g m) -> p g m", g=BD) for m in range(2)] for s in range(2)]
        Em = [core.ring[0:SG, s, 2 * BD * W9:2 * BD * W9 + BG * EW].rearrange("p (g w) -> p g w", g=BG) for s in range(2)]
        ps_f = [ph.ps(f"ps_f{s}", [SG, BG, P]) for s in range(2)]
        ps_b = [ph.ps(f"ps_b{s}", [SG, BG, P]) for s in range(2)]
        ps_y = [ph.ps(f"ps_y{s}", [LC, BG, P]) for s in range(2)]
        names = "v1_made v2_made V_made bs_ready hs_ready k_made e_back e_made y_made yb_made passed".split()
        v1_made, v2_made, V_made, bs_ready, hs_ready, k_made, e_back, e_made, y_made, yb_made, passed = [ph.sem(n) for n in names]
        c_landed, E_stored, T_landed, y_stored = [[ph.sem(f"{n}{s}") for s in range(2)] for n in ("c_landed", "E_stored", "T_landed", "y_stored")]
        cols = lambda b: bass.ts(b, BD)
        spread_p = lambda b, part: ptab[:, cols(b), part, :].unsqueeze(3).to_broadcast([P, BD, CH + 1, SG])
        spread_c = lambda s, part: cab[s][:, part].unsqueeze(2).to_broadcast([P, BD, CH + 1, SG])
        by_power = lambda m: m.rearrange("p g (i m) -> p g i m", i=CH + 1)
        lags_at = d["lags"]

        def windows(s):
            return bass.AP(tensor=lags_at.tensor, offset=lags_at.offset + s * SG * BG * EW, ap=[[SG, CH], [BG * EW, SG], [EW, BG], [1, P]])
        TURNS = NB // NV - 1

        def steps(eng, step):
            for b in (-2, -1):
                step(b, b % NV, -1)
            with eng.Fori(0, TURNS) as n:
                for k in range(NV):
                    step(n * NV + k, k, n)
            for b in range(NV * TURNS, NB):
                step(b, b % NV, TURNS)

        def nth(n, k):
            return n * 2 + k // 2

        def exists(b, shift):
            return not isinstance(b, int) or 0 <= b + shift < NB

        with ph.block() as block:
            @block.sync
            def _(sp):
                def load(b, s):
                    sp.dma_start(cab[s][:], d["s5_cab"][b]).then_inc(c_landed[s], 16)

                def step(b, k, n):
                    s = k % 2
                    if exists(b, 4):
                        sp.wait_ge(v1_made, b + 3)
                        sp.wait_ge(v2_made, b + 3)
                        load(b + 4, s)
                    if exists(b, 2):
                        sp.wait_ge(e_made, b + 5)
                        sp.dma_start(lags_at[s], Em[s]).then_inc(E_stored[s], 16)
                    if exists(b, 0):
                        sp.wait_ge(yb_made, b + 3)
                        sp.dma_start(d["y"].rearrange("(c t) n -> c t n", t=CH)[:, :, bass.ts(b, BG * SG)], yb[s][:]).then_inc(y_stored[s], 16)
                    if exists(b, 2):
                        sp.wait_ge(E_stored[s], nth(n, k + 2) * 16 + 16)
                        sp.wait_ge(y_made, b + 3)
                        sp.dma_start(T[s][:], windows(s)).then_inc(T_landed[s], 16)
                for s in range(2):
                    sp.sem_inc(y_stored[s], 16)
                    load(s, s)
                steps(sp, step)
                for s in range(2):
                    sp.wait_ge(y_stored[s], 16 * (NB // 2 + 1))
                prefetch(core, sp, d["s5_glu_w"])

            @block.gpsimd
            def _(pool):
                with pool.Fori(0, NB // 2) as n:
                    for s in range(2):
                        b = n * 2 + s
                        pool.wait_ge(c_landed[s], n * 16 + 16)
                        pool.wait_ge(V_made, b + 1)
                        pool.sem_inc(passed, 1)
                        nc.gpsimd.tensor_tensor(by_power(parts[s][1]), spread_p(b, 1), spread_c(s, 1), ALU.mult).then_inc(v2_made, 1)

            @block.vector
            def _(dve):
                prime(dve, V_made, 2)
                prime(dve, e_made, 2)

                def make_v(b, k, n):
                    s = k % 2
                    dve.wait_ge(c_landed[s], nth(n, k) * 16 + 16)
                    dve.wait_ge(V_made, b + 1)
                    nc.vector.tensor_tensor(by_power(parts[s][0]), spread_p(b, 0), spread_c(s, 0), ALU.mult).then_inc(v1_made, 1)
                    dve.wait_ge(v1_made, b + 1)
                    dve.wait_ge(v2_made, b + 1)
                    if isinstance(b, int) and b < NV:
                        pass
                    else:
                        dve.wait_ge(y_made, b - 1)
                    nc.vector.tensor_tensor(V[k % NV][:], parts[s][0], parts[s][1], ALU.add).then_inc(V_made, 1)

                def step(b, k, n):
                    if exists(b, 3):
                        make_v(b + 3, k + 3, n)
                    if exists(b, 2):
                        s = k % 2
                        dve.wait_ge(k_made, b + 3)
                        dve.wait_ge(e_back, b + 3)
                        mid = Em[s][:, :, EW // 2 - SG // 2:EW // 2 + SG // 2]
                        nc.vector.tensor_tensor(mid, mid, ps_f[s][:, :, 0:SG], ALU.add)
                        nc.vector.tensor_copy(Em[s][:, :, P:EW], ps_f[s][:, :, SG:P]).then_inc(e_made, 1)
                make_v(0, 0, 0)
                steps(dve, step)

            @block.scalar
            def _(act):
                def copy_bbar(b, s):
                    act.wait_ge(k_made, b - 1) if not isinstance(b, int) or b >= 2 else None
                    nc.scalar.activation(bs[s][:], bbar[:, cols(b), :], ACT.Copy).then_inc(bs_ready, 1)

                def copy_states(b, s):
                    act.wait_ge(y_made, b + 1)
                    back = S[:, CC - 1:CC + LC - 1, cols(b)].rearrange("p c (g r) -> p g r c", r=2)
                    hd = hs[s][:].rearrange("p (g r) c -> p g r c", r=2)
                    nc.scalar.activation(hd[:, :, 0, :], back[:, :, 0, :], ACT.Copy)
                    nc.scalar.activation(hd[:, :, 1, ::-1], back[:, :, 1, :], ACT.Copy)
                    nc.scalar.activation(us[s][:], u8[:, bass.ts(b, BG), :], ACT.Copy).then_inc(hs_ready, 1)

                def step(b, k, n):
                    s = k % 2
                    if exists(b, 3):
                        copy_bbar(b + 3, 1 - s)
                    if exists(b, 1):
                        copy_states(b + 1, 1 - s)
                    if exists(b, 2):
                        act.wait_ge(k_made, b + 3)
                        act.wait_ge(E_stored[s], nth(n, k + 2) * 16)
                        nc.scalar.activation(Em[s][:, :, 0:P], ps_b[s][:], ACT.Copy).then_inc(e_back, 1)
                    if exists(b, 0):
                        act.wait_ge(y_made, b + 3)
                        act.wait_ge(y_stored[s], nth(n, k) * 16 + 16)
                        nc.scalar.activation(yb[s][:].rearrange("c t (g n) -> c g t n", g=BG),
                                             ps_y[s][:].rearrange("c g (t n) -> c g t n", t=CH), ACT.Copy).then_inc(yb_made, 1)
                prime(act, yb_made, 2)
                copy_bbar(0, 0)
                steps(act, step)

            @block.tensor
            def _(pe):
                prime(pe, y_made, 2)

                def step(b, k, n):
                    s = k % 2
                    if exists(b, 2):
                        v = V[(k + 2) % NV]
                        pe.wait_ge(V_made, b + 5)
                        pe.wait_ge(bs_ready, b + 3)
                        pe.wait_ge(e_made, b + 3)
                        for g in range(BG):
                            nc.tensor.matmul(ps_f[s][:, g, :], bs[s][:, 2 * g, :], v[:, 2 * g, 0:P], start=True, stop=True)
                            last = nc.tensor.matmul(ps_b[s][:, g, :], bs[s][:, 2 * g + 1, :], v[:, 2 * g + 1, SG:W9], start=True, stop=True)
                        last.then_inc(k_made, 1)
                    if exists(b, 0):
                        v = V[k % NV]
                        pe.wait_ge(T_landed[s], nth(n, k) * 16 + 16)
                        pe.wait_ge(hs_ready, b + 1)
                        pe.wait_ge(yb_made, b + 1)
                        for g in range(BG):
                            nc.tensor.matmul(ps_y[s][:, g, :], hs[s][:, 2 * g, :], v[:, 2 * g, SG:W9], start=True, stop=False)
                            nc.tensor.matmul(ps_y[s][:, g, :], hs[s][:, 2 * g + 1, :], v[:, 2 * g + 1, 0:P], start=False, stop=False)
                            last = nc.tensor.matmul(ps_y[s][:, g, :], us[s][:, g, :], T[s][:, g, :], start=False, stop=True)
                        last.then_inc(y_made, 1)
                steps(pe, step)


def turn_tiles(pe, nc, src, bank, ident, tiles, turned, freed):
    for f in range(tiles):
        if f >= 2:
            pe.wait_ge(freed, f - 1)
        for t in range(LT):
            last = nc.tensor.transpose(bank(f)[:, t * P:(t + 1) * P], src(t, f), ident)
        last.then_inc(turned, 1)


def s5_gate(core, yzT):
    nc, d = core.nc, core.d
    with phase(core, "glu") as ph:
        y = ph.sb("y", [P, LT, E])
        u = ph.sb("u", [P, LT, E])
        z = ph.sb("z", [P, LT, E])
        row = ph.sb("row", [P, E])
        bias = ph.sb("bias", [P, E])
        gT = ph.sb("gT", [P, ET, NL])
        sg = ph.sb("sg", [P, 2, LT, NW])
        ps = [[ph.ps(f"ps{s}{t}", [P, NW]) for t in range(LT)] for s in range(2)]
        ps_t = [ph.ps(f"ps_t{s}", [P, NL]) for s in range(2)]
        names = "loads y_done g_done g_turned gT_done mm_done half_used biased sig yz_done yz_turned yzT_done steps".split()
        (loads, y_done, g_done, g_turned, gT_done, mm_done, half_used, biased, sig, yz_done, yz_turned,
         yzT_done, steps) = [ph.sem(n) for n in names]
        G = E // NW
        with ph.block() as block:
            @block.sync
            def _(sp):
                sp.dma_start(y[:], d["y"].rearrange("(t p) n -> p t n", p=P)).then_inc(loads, 16)
                sp.dma_start(u[:], d["u"][0:NL].rearrange("(t p) n -> p t n", p=P)).then_inc(loads, 16)
                sp.dma_start(row[:], d["s5_d"].to_broadcast([P, E])).then_inc(loads, 16)
                sp.dma_start(bias[:], d["s5_glu_b"].to_broadcast([P, E])).then_inc(loads, 16)
                sp.dma_start(z[:], d["z"].rearrange("(t p) n -> p t n", p=P)).then_inc(loads, 16)
                stream_loads(core, sp, d["s5_glu_w"], G, 2, LT, mm_done, half_used)
                sp.wait_ge(mm_done, G * LT)
                prefetch(core, sp, d["w_out1"])

            @block.vector
            def _(dve):
                chain = Chain(dve, steps)
                prime(dve, biased, LT + 1)
                dve.wait_ge(loads, 80)
                for t in range(LT):
                    chain.run(nc.vector.tensor_tensor(u[:, t, :], u[:, t, :], row[:], ALU.mult))
                    nc.vector.tensor_tensor(y[:, t, :], y[:, t, :], u[:, t, :], ALU.add).then_inc(y_done, 1)

                def gate(g, s):
                    cols = bass.ts(g, NW)
                    for t in range(LT):
                        dve.wait_ge(mm_done, g * LT + t + 1)
                        nc.vector.tensor_tensor(sg[:, s, t, :], ps[s][t][:], bias[:, cols], ALU.add).then_inc(biased, 1)
                    for t in range(LT):
                        dve.wait_ge(sig, g * LT + t + 1)
                        chain.run(nc.vector.tensor_tensor(sg[:, s, t, :], sg[:, s, t, :], y[:, t, cols], ALU.mult))
                        nc.vector.tensor_tensor(y[:, t, cols], sg[:, s, t, :], z[:, t, cols], ALU.mult).then_inc(yz_done, 1)
                with chain.loop(G // 2, 2 * LT) as i:
                    for s in range(2):
                        gate(i * 2 + s, s)

            @block.scalar
            def _(act):
                for t in range(LT):
                    act.wait_ge(y_done, t + 1)
                    nc.scalar.activation(y[:, t, :], y[:, t, :], ACT.Gelu_apprx_tanh).then_inc(g_done, 1)
                for f in range(ET):
                    act.wait_ge(g_turned, f + 1)
                    nc.scalar.activation(gT[:, f, :], ps_t[f % 2][:], ACT.Copy).then_inc(gT_done, 1)

                def sigmoid(g, s):
                    for t in range(LT):
                        act.wait_ge(biased, g * LT + t + LT + 2)
                        nc.scalar.activation(sg[:, s, t, :], sg[:, s, t, :], ACT.Sigmoid).then_inc(sig, 1)
                stream_turns(act, G)(sigmoid)
                for f in range(ET):
                    act.wait_ge(yz_turned, f + 1)
                    nc.scalar.activation(yzT[:, f, :], ps_t[f % 2][:], ACT.Copy).then_inc(yzT_done, 1)

            @block.tensor
            def _(pe):
                pe.wait_ge(g_done, LT)
                turn_tiles(pe, nc, lambda t, f: y[:, t, f * P:(f + 1) * P], lambda f: ps_t[f % 2], core.ident[:], ET, g_turned, gT_done)
                pe.wait_ge(gT_done, ET)
                stream_products(core, pe, G, 2, LT, lambda k, t: gT[:, k, t * P:(t + 1) * P], lambda s, t: ps[s][t],
                                mm_done, half_used, [(biased, LT)])
                pe.wait_ge(yz_done, G * LT)
                turn_tiles(pe, nc, lambda t, f: y[:, t, f * P:(f + 1) * P], lambda f: ps_t[f % 2], core.ident[:], ET, yz_turned, yzT_done)


AW = 512
AG, AGD = 8, 64
BH, BHD = 8, 64
BW = BH * BHD
EV_IN = 2 * AW + 3 * BW
CHD, CDK, CDV = 4, 128, 256
CR = 16
CTAU = 16.0
CCH = 64
CONV = 3
CK, CV = CHD * CDK, CHD * CDV
FF = 2816
FT = FF // P


def rms_transposes(core, name, g_cols, hT):
    nc, d = core.nc, core.d
    with phase(core, name) as ph:
        xn = ph.sb("xn", [P, LT, DM])
        g = ph.sb("g", [P, KT])
        ms = ph.sb("ms", [P, LT])
        rs = ph.sb("rs", [P, LT])
        ps = [ph.ps(f"ps{b}", [P, NL]) for b in range(4)]
        loaded, squared, std_ready, steps, xn_ready, turned, freed = [ph.sem(n) for n in "loaded squared std_ready steps xn_ready turned freed".split()]
        with ph.block() as block:
            @block.scalar
            def _(act):
                act.dma_start(g[:], g_cols).then_inc(loaded, 16)
                for t in range(LT):
                    last = nc.scalar.activation(xn[:, t, :], core.x[:, t, :], ACT.Square, accum_out=ms[:, t:t + 1])
                last.then_inc(squared, 1)
                act.wait_ge(squared, 1)
                nc.scalar.activation(rs[:], ms[:], ACT.Sqrt, scale=1.0 / DM, bias=core.eps[:, 1:2]).then_inc(std_ready, 1)

            @block.vector
            def _(dve):
                chain = Chain(dve, steps)
                dve.wait_ge(std_ready, 1)
                chain.run(nc.vector.reciprocal(rs[:], rs[:]))
                for t in range(LT):
                    nc.vector.tensor_scalar(xn[:, t, :], core.x[:, t, :], rs[:, t:t + 1], None, ALU.mult).then_inc(xn_ready, 1)
                dve.wait_ge(loaded, 16)
                for k in range(KT):
                    dve.wait_ge(turned, k + 1)
                    nc.vector.tensor_scalar(hT[:, k, :], ps[k % 4][:], g[:, k:k + 1], None, ALU.mult).then_inc(freed, 1)

            @block.tensor
            def _(pe):
                pe.wait_ge(xn_ready, LT)
                for k in range(KT):
                    if k >= 4:
                        pe.wait_ge(freed, k - 3)
                    for t in range(LT):
                        last = nc.tensor.transpose(ps[k % 4][:, t * P:(t + 1) * P], xn[:, t, k * P:(k + 1) * P], core.ident[:])
                    last.then_inc(turned, 1)


def project(core, name, weights, tiles, hT, dst, funcs, following, extra=None):
    nc, d = core.nc, core.d
    with phase(core, name) as ph:
        ps = [[ph.ps(f"ps{s}{t}", [P, NW]) for t in range(LT)] for s in range(2)]
        mm_done, freed = ph.sem("mm_done"), ph.sem("freed")
        if extra:
            xw = ph.sb("xw", [P, KT, CR])
            xl, xd, xm = ph.sem("xl"), ph.sem("xd"), ph.sem("xm")
            ps_x = ph.ps("ps_x", [CR, NL])
        with ph.block() as block:
            @block.sync
            def _(sp):
                if extra:
                    sp.dma_start(xw[:], extra[0]).then_inc(xl, 16)
                stream_loads(core, sp, d[weights], tiles, 1, LT, mm_done, None)
                sp.wait_ge(mm_done, tiles * LT)
                prefetch(core, sp, d[following])

            @block.tensor
            def _(pe):
                stream_products(core, pe, tiles, 1, LT, lambda k, t: hT[:, k, t * P:(t + 1) * P],
                                lambda s, t: ps[s][t], mm_done, None, [(freed, LT)])
                if extra:
                    pe.wait_ge(xl, 16)
                    for k in range(KT):
                        last = nc.tensor.matmul(ps_x[:], xw[:, k, :], hT[:, k, :], start=k == 0, stop=k == KT - 1)
                    last.then_inc(xm, 1)

            @block.scalar
            def _(act):
                prime(act, freed, LT + 1)

                def empty(g, s, func):
                    for t in range(LT):
                        act.wait_ge(mm_done, g * LT + t + 1)
                        nc.scalar.activation(dst[:, t, bass.ts(g, NW)], ps[s][t][:], func).then_inc(freed, 1)
                at = 0
                for func, n in funcs:
                    if n >= 4 and at % 2 == 0 and n % 2 == 0:
                        with act.Fori(0, n // 2) as i:
                            for s in range(2):
                                empty(i * 2 + at + s, s, func)
                    else:
                        for g in range(at, at + n):
                            empty(g, g % 2, func)
                    at += n
                if extra:
                    act.wait_ge(xm, 1)
                    nc.scalar.activation(extra[1][:], ps_x[:], ACT.Copy).then_inc(xd, 1)


def project_residual(core, name, weights, mixT, following):
    nc, d = core.nc, core.d
    with phase(core, name) as ph:
        ps = [[ph.ps(f"ps{s}{t}", [P, NW]) for t in range(LT)] for s in range(2)]
        mm_done, added = ph.sem("mm_done"), ph.sem("added")
        with ph.block() as block:
            @block.sync
            def _(sp):
                sp.wait_ge(mm_done, 2 * LT)
                if following:
                    prefetch(core, sp, d[following])

            @block.tensor
            def _(pe):
                stream_products(core, pe, 2, 1, LT, lambda k, t: mixT[:, k, t * P:(t + 1) * P], lambda s, t: ps[s][t], mm_done, None, [])

            @block.vector
            def _(dve):
                for s in range(2):
                    for t in range(LT):
                        dve.wait_ge(mm_done, s * LT + t + 1)
                        x = core.x[:, t, s * NW:(s + 1) * NW]
                        nc.vector.tensor_tensor(x, x, ps[s][t][:], ALU.add).then_inc(added, 1)


def gated_mlp(core, zz, mixT):
    nc, d = core.nc, core.d
    with phase(core, "mlp") as ph:
        g_row, b_row = ph.sb("g_row", [P, AW]), ph.sb("b_row", [P, AW])
        wsT = ph.sb("wsT", [P, AG, P])
        bsT = ph.sb("bsT", [P, AG])
        stats, mv, rstd = ph.sb("stats", [P, 6]), ph.sb("mv", [P, 2]), ph.sb("rstd", [P, LT])
        tri = ph.sb("tri", [P, P])
        ps = [ph.ps(f"ps{t}", [P, AW]) for t in range(LT)]
        ps_t = [ph.ps(f"ps_t{s}", [P, NL]) for s in range(2)]
        loads, steps, var, std, vn, mixed, a_done, turned, freed, masked = [ph.sem(n) for n in "loads steps var std vn mixed a_done turned freed masked".split()]
        with ph.block() as block:
            @block.sync
            def _(sp):
                sp.dma_start(g_row[:], d["ev_a_ln_g"].to_broadcast([P, AW])).then_inc(loads, 16)
                sp.dma_start(b_row[:], d["ev_a_ln_b"].to_broadcast([P, AW])).then_inc(loads, 16)
                sp.dma_start(wsT[:], d["ev_a_wsT"]).then_inc(loads, 16)
                sp.dma_start(bsT[:], d["ev_a_bsT"]).then_inc(loads, 16)
                sp.dma_start(tri[:], d["causal"]).then_inc(loads, 16)

            @block.gpsimd
            def _(pool):
                pool.wait_ge(loads, 80)
                nc.gpsimd.tensor_tensor(wsT[:], wsT[:], tri[:].unsqueeze(1).to_broadcast([P, AG, P]), ALU.mult).then_inc(masked, 1)

            @block.vector
            def _(dve):
                chain = Chain(dve, steps)
                dve.wait_ge(loads, 80)
                for t in range(LT):
                    v = zz[:, t, AW:2 * AW]
                    chain.run(nc.vector.bn_stats(stats[:], v))
                    chain.run(nc.vector.bn_aggr(mv[:], stats[:]))
                    dve.sem_inc(var, 1)
                    dve.wait_ge(std, t + 1)
                    chain.run(nc.vector.reciprocal(rstd[:, t:t + 1], rstd[:, t:t + 1]))
                    chain.run(nc.vector.tensor_scalar(v, v, mv[:, 0:1], rstd[:, t:t + 1], ALU.subtract, ALU.mult))
                    chain.run(nc.vector.tensor_tensor(v, v, g_row[:], ALU.mult))
                    nc.vector.tensor_tensor(v, v, b_row[:], ALU.add).then_inc(vn, 1)
                for t in range(LT):
                    dve.wait_ge(mixed, t + 1)
                    for g in range(AG):
                        cols = slice(g * AGD, (g + 1) * AGD)
                        last = nc.vector.scalar_tensor_tensor(out=zz[:, t, cols], in0=ps[t][:, cols], scalar=bsT[:, g:g + 1], in1=zz[:, t, cols], op0=ALU.add, op1=ALU.mult)
                    last.then_inc(a_done, 1)

            @block.scalar
            def _(act):
                for t in range(LT):
                    act.wait_ge(var, t + 1)
                    nc.scalar.activation(rstd[:, t:t + 1], mv[:, 1:2], ACT.Sqrt, bias=core.eps[:, 1:2]).then_inc(std, 1)
                for f in range(AW // P):
                    act.wait_ge(turned, f + 1)
                    nc.scalar.activation(mixT[:, f, :], ps_t[f % 2][:], ACT.Copy).then_inc(freed, 1)

            @block.tensor
            def _(pe):
                pe.wait_ge(masked, 1)
                for t in range(LT):
                    pe.wait_ge(vn, t + 1)
                    for g in range(AG):
                        cols = slice(g * AGD, (g + 1) * AGD)
                        last = nc.tensor.matmul(ps[t][:, cols], wsT[:, g, :], zz[:, t, AW + g * AGD:AW + (g + 1) * AGD], start=True, stop=True)
                    last.then_inc(mixed, 1)
                pe.wait_ge(a_done, LT)
                turn_tiles(pe, nc, lambda t, f: zz[:, t, f * P:(f + 1) * P], lambda f: ps_t[f % 2], core.ident[:], AW // P, turned, freed)


def dilated_attention(core, zz, mixT):
    nc, d = core.nc, core.d
    Q0, K0, V0 = 2 * AW, 2 * AW + BW, 2 * AW + 2 * BW
    HP = BH // 2
    with phase(core, "dil") as ph:
        gq, gk = ph.sb("gq", [P, BHD]), ph.sb("gk", [P, BHD])
        sq = ph.sb("sq", [P, LT, 2 * BW])
        ms = ph.sb("ms", [P, LT, 2 * BH])
        rs = ph.sb("rs", [P, LT, 2 * BH])
        count, bar = ph.sb("count", [P, LT, NL]), ph.sb("bar", [P, LT, NL])
        qkT = ph.sb("qkT", [P, 2, HP, NL])
        s_sb, p_sb = ph.sb("s_sb", [P, 2, LT, NL]), ph.sb("p_sb", [P, 2, LT, NL])
        pT = ph.sb("pT", [P, 2, LT, NL])
        mx, den = ph.sb("mx", [P, 2, LT]), ph.sb("den", [P, 2, LT])
        b_out = ph.sb("b_out", [P, LT, BW])
        ps_t = [ph.ps(f"ps_t{i}", [P, 2, NL]) for i in range(2)]
        ps_s = [ph.ps(f"ps_s{i}", [P, LT, NL]) for i in range(2)]
        ps_p = [ph.ps(f"ps_p{i}", [P, LT, NL]) for i in range(2)]
        ps_y = ph.ps("ps_y", [P, LT, 2, BHD])
        names = "loads steps squared std normed turned qkT_done scores smax expd weighed p_turned pT_done y_done b_done b_turned freed".split()
        (loads, steps, squared, std, normed, turned, qkT_done, scores, smax, expd, weighed, p_turned, pT_done, y_done, b_done,
         b_turned, freed) = [ph.sem(n) for n in names]
        SC = BHD ** -0.5
        with ph.block() as block:
            @block.sync
            def _(sp):
                sp.dma_start(gq[:], d["ev_q_g"].to_broadcast([P, BHD])).then_inc(loads, 16)
                sp.dma_start(gk[:], d["ev_k_g"].to_broadcast([P, BHD])).then_inc(loads, 16)
                sp.dma_start(count[:], d["branch_count"]).then_inc(loads, 16)
                sp.dma_start(bar[:], d["branch_bar"]).then_inc(loads, 16)

            @block.vector
            def _(dve):
                chain = Chain(dve, steps)
                dve.wait_ge(loads, 64)
                chain.run(nc.vector.tensor_tensor(sq[:], zz[:, :, Q0:V0], zz[:, :, Q0:V0], ALU.mult))
                chain.run(nc.vector.tensor_reduce(ms[:], sq[:].rearrange("p t (h w) -> p t h w", w=BHD), AX, ALU.add))
                dve.sem_inc(squared, 1)
                dve.wait_ge(std, 1)
                chain.run(nc.vector.reciprocal(rs[:], rs[:]))
                for t in range(LT):
                    for n, (c0, g) in enumerate(((Q0, gq), (K0, gk))):
                        blk = zz[:, t, c0:c0 + BW].rearrange("p (h w) -> p h w", w=BHD)
                        chain.run(nc.vector.tensor_tensor(blk, blk, rs[:, t, n * BH:(n + 1) * BH].unsqueeze(2).to_broadcast([P, BH, BHD]), ALU.mult))
                        nc.vector.tensor_tensor(blk, blk, g[:].unsqueeze(1).to_broadcast([P, BH, BHD]), ALU.mult).then_inc(normed, 1)
                for hp in range(HP):
                    for i in range(2):
                        dve.wait_ge(scores, hp * 2 + i + 1)
                        chain.run(nc.vector.scalar_tensor_tensor(out=s_sb[:, i], in0=ps_s[i][:], scalar=SC, in1=bar[:], op0=ALU.mult, op1=ALU.add))
                        chain.run(nc.vector.tensor_reduce(mx[:, i], s_sb[:, i], AX, ALU.max))
                        nc.vector.tensor_scalar(mx[:, i], mx[:, i], -1.0, None, ALU.mult).then_inc(smax, 1)
                    for i in range(2):
                        dve.wait_ge(expd, hp * 2 + i + 1)
                        chain.run(nc.vector.tensor_tensor(p_sb[:, i], p_sb[:, i], count[:], ALU.mult))
                        dve.sem_inc(weighed, 1)
                        chain.run(nc.vector.tensor_reduce(den[:, i], p_sb[:, i], AX, ALU.add))
                    chain.run(nc.vector.reciprocal(den[:], den[:]))
                    dve.wait_ge(y_done, hp + 1)
                    for i in range(2):
                        for t in range(LT):
                            last = nc.vector.tensor_scalar(b_out[:, t, (2 * hp + i) * BHD:(2 * hp + i + 1) * BHD], ps_y[:, t, i, :], den[:, i, t:t + 1], None, ALU.mult)
                    last.then_inc(b_done, 1)

            @block.scalar
            def _(act):
                act.wait_ge(squared, 1)
                nc.scalar.activation(rs[:], ms[:], ACT.Sqrt, scale=1.0 / BHD, bias=core.eps[:, 1:2]).then_inc(std, 1)
                for n in range(2):
                    for i in range(2):
                        act.wait_ge(turned, n * 2 + i + 1)
                        nc.scalar.activation(qkT[:, n, 2 * i:2 * i + 2, :], ps_t[i][:], ACT.Copy).then_inc(qkT_done, 1)
                for hp in range(HP):
                    for i in range(2):
                        act.wait_ge(smax, hp * 2 + i + 1)
                        if hp:
                            act.wait_ge(p_turned, (hp - 1) * 2 + i + 1)
                        for t in range(LT):
                            last = nc.scalar.activation(p_sb[:, i, t, :], s_sb[:, i, t, :], ACT.Exp, bias=mx[:, i, t:t + 1])
                        last.then_inc(expd, 1)
                    for i in range(2):
                        act.wait_ge(p_turned, hp * 2 + i + 1)
                        if hp:
                            act.wait_ge(y_done, hp)
                        nc.scalar.activation(pT[:, i], ps_p[i][:], ACT.Copy).then_inc(pT_done, 1)
                for f in range(BW // P):
                    act.wait_ge(b_turned, f + 1)
                    nc.scalar.activation(mixT[:, AW // P + f, :], ps_t[f % 2][:, 0, :], ACT.Copy).then_inc(freed, 1)

            @block.tensor
            def _(pe):
                pe.wait_ge(normed, 2 * LT)
                for n, c0 in enumerate((Q0, K0)):
                    for i in range(2):
                        if n:
                            pe.wait_ge(qkT_done, i + 1)
                        for j in range(2):
                            for t in range(LT):
                                hp = 2 * i + j
                                last = nc.tensor.transpose(ps_t[i][:, j, t * P:(t + 1) * P], zz[:, t, c0 + hp * P:c0 + (hp + 1) * P], core.ident[:])
                        last.then_inc(turned, 1)
                pe.wait_ge(qkT_done, 4)

                def make_scores(hp):
                    for i in range(2):
                        half = slice(i * BHD, (i + 1) * BHD)
                        if hp:
                            pe.wait_ge(smax, (hp - 1) * 2 + i + 1)
                        for t in range(LT):
                            last = nc.tensor.matmul(ps_s[i][:, t, :], qkT[half, 0, hp, t * P:(t + 1) * P], qkT[half, 1, hp, :], start=True, stop=True)
                        last.then_inc(scores, 1)
                make_scores(0)
                for hp in range(HP):
                    if hp + 1 < HP:
                        make_scores(hp + 1)
                    for i in range(2):
                        pe.wait_ge(weighed, hp * 2 + i + 1)
                        if hp:
                            pe.wait_ge(pT_done, (hp - 1) * 2 + i + 1)
                        for kt in range(LT):
                            for t in range(LT):
                                last = nc.tensor.transpose(ps_p[i][:, kt, t * P:(t + 1) * P], p_sb[:, i, t, kt * P:(kt + 1) * P], core.ident[:])
                        last.then_inc(p_turned, 1)
                    if hp:
                        pe.wait_ge(b_done, hp)
                    for i in range(2):
                        pe.wait_ge(pT_done, hp * 2 + i + 1)
                        h = 2 * hp + i
                        for t in range(LT):
                            for kt in range(LT):
                                last = nc.tensor.matmul(ps_y[:, t, i, :], pT[:, i, kt, t * P:(t + 1) * P], zz[:, kt, V0 + h * BHD:V0 + (h + 1) * BHD],
                                                        start=kt == 0, stop=kt == LT - 1)
                    last.then_inc(y_done, 1)
                pe.wait_ge(b_done, HP)
                turn_tiles(pe, nc, lambda t, f: b_out[:, t, f * P:(f + 1) * P], lambda f: ps_t[f % 2][:, 0, :], core.ident[:], BW // P, b_turned, freed)


def gla(core, zz, gaT, mixT):
    nc, d = core.nc, core.d
    K0, V0, R0 = CK, 2 * CK, 2 * CK + CV
    with phase(core, "gla") as ph:
        wa2, ba = ph.sb("wa2", [CR, CK]), ph.sb("ba", [P, CK])
        g_row = ph.sb("g_row", [P, CDV])
        sums, block_ones, ends = ph.sb("sums", [P, P]), ph.sb("block_ones", [P, P]), ph.sb("ends", [P, 2])
        la = ph.sb("la", [P, LT, CK])
        ex = ph.sb("ex", [P, LT, CK])
        tmp = ph.sb("tmp", [P, LT, CK])
        qt, kt_, ks = ph.sb("qt", [P, LT, CK]), ph.sb("kt", [P, LT, CK]), ph.sb("ks", [P, LT, CK])
        qT, kT = ph.sb("qT", [P, CHD, NL]), ph.sb("kT", [P, CHD, NL])
        att = ph.sb("att", [P, 2, LT, P])
        dec = ph.sb("dec", [P, CHD, LT, 2])
        st = ph.sb("st", [P, 2, 3, CDV])
        o = ph.sb("o", [P, LT, CV])
        ms, rs = ph.sb("ms", [P, LT, CHD]), ph.sb("rs", [P, LT, CHD])
        ps_b = [ph.ps(f"ps_b{t}", [P, CK]) for t in range(LT)]
        ps_l = [ph.ps(f"ps_l{t}", [P, CK]) for t in range(LT)]
        ps_a = [ph.ps(f"ps_a{t}", [P, LT, P]) for t in range(2)]
        ps_o = [ps_b[t][:, 0:CDV] for t in range(LT)]
        ps_kv = [ps_l[i][:, 0:CDV] for i in range(2)]
        ps_d = ph.ps("ps_d", [P, CHD, LT, 2])
        names = "loads steps asteps ks_done gate_mm xs ex1 la_done cum dec_mm e0 e1 dec_done qk_done turned qkT_done att_mm att_done kv_mm st_done o_mm o_done sq_done std out_done o_turned freed".split()
        S = {n: ph.sem(n) for n in names}
        with ph.block() as block:
            @block.sync
            def _(sp):
                for dst, src in ((wa2[:], d["od_w_a2"]), (ba[:], d["od_b_a"].to_broadcast([P, CK])), (g_row[:], d["od_head_g"].to_broadcast([P, CDV])),
                                 (sums[:], d["chunk_sums"]), (block_ones[:], d["chunk_ones"]), (ends[:], d["chunk_ends"])):
                    sp.dma_start(dst, src).then_inc(S["loads"], 16)

            @block.tensor
            def _(pe):
                pe.wait_ge(S["loads"], 96)
                for t in range(LT):
                    nc.tensor.matmul(ps_b[t][:], gaT[:, t * P:(t + 1) * P], wa2[:], start=True, stop=True).then_inc(S["gate_mm"], 1)
                for t in range(LT):
                    pe.wait_ge(S["la_done"], t + 1)
                    nc.tensor.matmul(ps_b[t][:], sums[:], la[:, t, :], start=True, stop=True)
                    nc.tensor.matmul(ps_l[t][:], block_ones[:], la[:, t, :], start=True, stop=True).then_inc(S["cum"], 1)
                for t in range(LT):
                    for h in range(CHD):
                        last = nc.tensor.matmul(ps_d[:, h, t, :], la[:, t, h * CDK:(h + 1) * CDK], ends[:], start=True, stop=True)
                last.then_inc(S["dec_mm"], 1)
                pe.wait_ge(S["qk_done"], 1)
                for n, (src, bank) in enumerate(((qt, ps_b), (kt_, ps_l))):
                    for i in range(2):
                        for j in range(2):
                            for t in range(LT):
                                last = nc.tensor.transpose(bank[i][:, (j * LT + t) * P:(j * LT + t + 1) * P], src[:, t, (2 * i + j) * P:(2 * i + j + 1) * P], core.ident[:])
                        last.then_inc(S["turned"], 1)
                pe.wait_ge(S["qkT_done"], 4)
                pe.wait_ge(S["ks_done"], 1)
                for h in range(CHD):
                    a = h % 2
                    if h >= 2:
                        pe.wait_ge(S["att_done"], h - 1)
                    for t in range(LT):
                        last = nc.tensor.matmul(ps_a[a][:, t, :], kT[:, h, t * P:(t + 1) * P], qT[:, h, t * P:(t + 1) * P], start=True, stop=True)
                    last.then_inc(S["att_mm"], 1)
                    for c in range(3):
                        t, r = c // 2, slice((c % 2) * CCH, (c % 2 + 1) * CCH)
                        if h * 3 + c >= 2:
                            pe.wait_ge(S["st_done"], h * 3 + c - 1)
                        nc.tensor.matmul(ps_kv[(h * 3 + c) % 2], ks[r, t, h * CDK:(h + 1) * CDK], zz[r, t, V0 + h * CDV:V0 + (h + 1) * CDV],
                                         start=True, stop=True).then_inc(S["kv_mm"], 1)
                    pe.wait_ge(S["att_done"], h + 1)
                    pe.wait_ge(S["st_done"], h * 3 + 3)
                    if h:
                        pe.wait_ge(S["o_done"], h)
                    for t in range(LT):
                        vv = zz[:, t, V0 + h * CDV:V0 + (h + 1) * CDV]
                        last = nc.tensor.matmul(ps_o[t], att[:, a, t, :], vv, start=True, stop=True)
                        if t:
                            nc.tensor.matmul(ps_o[t][0:CCH], qT[:, h, 2 * CCH:3 * CCH], st[:, a, 1, :], start=False, stop=True, skip_group_check=True)
                        last = nc.tensor.matmul(ps_o[t][CCH:P], qT[:, h, (2 * t + 1) * CCH:(2 * t + 2) * CCH], st[:, a, 2 * t, :], start=False, stop=True, skip_group_check=True)
                    last.then_inc(S["o_mm"], 1)
                pe.wait_ge(S["out_done"], 1)
                turn_tiles(pe, nc, lambda t, f: o[:, t, f * P:(f + 1) * P], lambda f: ps_l[f % 2], core.ident[:], KT, S["o_turned"], S["freed"])

            @block.vector
            def _(dve):
                chain = Chain(dve, S["steps"])
                v = nc.vector
                dve.wait_ge(S["loads"], 96)
                for t in range(LT):
                    dve.wait_ge(S["gate_mm"], t + 1)
                    chain.run(v.tensor_tensor(la[:, t, :], ps_b[t][:], ba[:], ALU.add))
                    chain.run(v.tensor_scalar(ex[:, t, :], la[:, t, :], -1.0, None, ALU.mult))
                    chain.run(v.tensor_tensor(ex[:, t, :], ex[:, t, :], la[:, t, :], ALU.max))
                    dve.sem_inc(S["xs"], 1)
                for t in range(LT):
                    dve.wait_ge(S["ex1"], t + 1)
                    chain.run(v.tensor_scalar(la[:, t, :], la[:, t, :], 0.0, None, ALU.min))
                    chain.run(v.tensor_tensor(la[:, t, :], la[:, t, :], ex[:, t, :], ALU.subtract))
                    v.tensor_scalar(la[:, t, :], la[:, t, :], 1.0 / CTAU, None, ALU.mult).then_inc(S["la_done"], 1)
                for t in range(LT):
                    dve.wait_ge(S["e1"], 2 * t + 1)
                    chain.run(v.tensor_tensor(qt[:, t, :], zz[:, t, 0:CK], ex[:, t, :], ALU.mult))
                    chain.run(v.tensor_scalar(qt[:, t, :], qt[:, t, :], float(CDK) ** -0.5, None, ALU.mult))
                    dve.wait_ge(S["e1"], 2 * t + 2)
                    v.tensor_tensor(kt_[:, t, :], zz[:, t, K0:V0], tmp[:, t, :], ALU.mult)
                    chain.run(v.tensor_copy(ks[:, t, :], ps_b[t][:]))
                    chain.run(v.tensor_tensor(ks[:, t, :], ps_l[t][:], ks[:, t, :], ALU.subtract))
                dve.sem_inc(S["qk_done"], 1)
                for t in range(LT):
                    dve.wait_ge(S["asteps"], t + 1)
                    chain.run(v.tensor_tensor(ks[:, t, :], zz[:, t, K0:V0], ks[:, t, :], ALU.mult))
                dve.sem_inc(S["ks_done"], 1)
                dve.wait_ge(S["dec_done"], 1)
                for h in range(CHD):
                    a = h % 2
                    dve.wait_ge(S["att_mm"], h + 1)
                    if h >= 2:
                        dve.wait_ge(S["o_mm"], h - 1)
                    chain.run(v.tensor_scalar(att[:, a], ps_a[a][:], 3.0e38, -3.0e38, ALU.min, ALU.max))
                    v.tensor_tensor(att[:, a], att[:, a], sums[:].unsqueeze(1).to_broadcast([P, LT, P]), ALU.mult).then_inc(S["att_done"], 1)
                    for c in range(3):
                        dve.wait_ge(S["kv_mm"], h * 3 + c + 1)
                        kv = ps_kv[(h * 3 + c) % 2]
                        if c == 0:
                            ins = v.tensor_copy(st[:, a, 0, :], kv)
                        else:
                            ins = v.scalar_tensor_tensor(out=st[:, a, c, :], in0=st[:, a, c - 1, :], scalar=dec[:, h, c // 2, c % 2:c % 2 + 1], in1=kv, op0=ALU.mult, op1=ALU.add)
                        ins.then_inc(S["st_done"], 1)
                        dve.wait_ge(S["st_done"], h * 3 + c + 1)
                    dve.wait_ge(S["o_mm"], h + 1)
                    for t in range(LT):
                        last = v.tensor_copy(o[:, t, h * CDV:(h + 1) * CDV], ps_o[t])
                    last.then_inc(S["o_done"], 1)
                dve.wait_ge(S["o_done"], CHD)
                for t in range(LT):
                    sq = zz[:, t, 0:CV]
                    chain.run(v.tensor_tensor(sq, o[:, t, :], o[:, t, :], ALU.mult))
                    chain.run(v.tensor_reduce(ms[:, t, :], sq.rearrange("p (h w) -> p h w", h=CHD), AX, ALU.add))
                dve.sem_inc(S["sq_done"], 1)
                dve.wait_ge(S["std"], 1)
                chain.run(v.reciprocal(rs[:], rs[:]))
                for t in range(LT):
                    ob = o[:, t, :].rearrange("p (h w) -> p h w", h=CHD)
                    chain.run(v.tensor_tensor(ob, ob, rs[:, t, :].unsqueeze(2).to_broadcast([P, CHD, CDV]), ALU.mult))
                    chain.run(v.tensor_tensor(ob, ob, g_row[:].unsqueeze(1).to_broadcast([P, CHD, CDV]), ALU.mult))
                    chain.run(v.tensor_tensor(o[:, t, :], o[:, t, :], zz[:, t, R0:R0 + CV], ALU.mult))
                dve.sem_inc(S["out_done"], 1)

            @block.scalar
            def _(act):
                sc = nc.scalar
                for t in range(LT):
                    act.wait_ge(S["xs"], t + 1)
                    sc.activation(ex[:, t, :], ex[:, t, :], ACT.Exp, scale=-1.0).then_inc(S["e0"], 1)
                    act.wait_ge(S["e0"], t + 1)
                    sc.activation(ex[:, t, :], ex[:, t, :], ACT.Ln, bias=1.0).then_inc(S["ex1"], 1)
                for t in range(LT):
                    act.wait_ge(S["cum"], t + 1)
                    sc.activation(ex[:, t, :], ps_b[t][:], ACT.Exp).then_inc(S["e1"], 1)
                    sc.activation(tmp[:, t, :], ps_b[t][:], ACT.Exp, scale=-1.0).then_inc(S["e1"], 1)
                act.wait_ge(S["dec_mm"], 1)
                sc.activation(dec[:], ps_d[:], ACT.Exp).then_inc(S["dec_done"], 1)
                act.wait_ge(S["qk_done"], 1)
                for t in range(LT):
                    sc.activation(ks[:, t, :], ks[:, t, :], ACT.Exp).then_inc(S["asteps"], 1)
                for n, (dst, bank) in enumerate(((qT, ps_b), (kT, ps_l))):
                    for i in range(2):
                        act.wait_ge(S["turned"], n * 2 + i + 1)
                        sc.activation(dst[:, 2 * i:2 * i + 2, :], bank[i][:].rearrange("p (j w) -> p j w", j=2), ACT.Copy).then_inc(S["qkT_done"], 1)
                act.wait_ge(S["sq_done"], 1)
                sc.activation(rs[:], ms[:], ACT.Sqrt, scale=1.0 / CDV, bias=core.eps[:, 1:2]).then_inc(S["std"], 1)
                for f in range(KT):
                    act.wait_ge(S["o_turned"], f + 1)
                    sc.activation(mixT[:, f, :], ps_l[f % 2][:, 0:NL], ACT.Copy).then_inc(S["freed"], 1)


def conv_ffn(core, name, layer, hT, following):
    nc, d = core.nc, core.d
    with phase(core, name) as ph:
        wd = [ph.sb(f"wd{s}", [P, 2, DM]) for s in range(2)]
        a = [ph.sb(f"a{s}", [P, 2, NL]) for s in range(2)]
        c = [ph.sb(f"c{s}", [P, 2, NL]) for s in range(2)]
        cw, cb = ph.sb("cw", [P, FT, CONV]), ph.sb("cb", [P, FT])
        ps = [[ph.ps(f"ps{s}{f}", [P, 2, NL]) for f in range(2)] for s in range(2)]
        acc = [[ph.ps(f"acc{t}{n}", [P, NW]) for n in range(2)] for t in range(LT)]
        names = "loads gu_done conv_done silu_done a_made down_done steps added".split()
        loads, gu_done, conv_done, silu_done, a_made, down_done, steps, added = [ph.sem(n) for n in names]
        wd_landed = [ph.sem(f"wd_landed{s}") for s in range(2)]
        NU = FT // 2
        HU = (NU - 3) // 2
        weights = d[f"ffn_gu{layer}"]
        down = d[f"ffn_down{layer}"]
        with ph.block() as block:
            @block.sync
            def _(sp):
                for s in range(2):
                    sp.dma_start(wd[s][:], down[s]).then_inc(wd_landed[s], 16)
                sp.dma_start(cw[:], d["ffn_conv_w"][layer]).then_inc(loads, 16)
                sp.dma_start(cb[:], d["ffn_conv_b"][layer]).then_inc(loads, 16)

                def turn(u, s):
                    sp.wait_ge(gu_done, u + 1)
                    core.load(sp, s, weights[u + 2])
                    sp.wait_ge(down_done, u + 3)
                    sp.dma_start(wd[s][:], down[u + 2]).then_inc(wd_landed[s], 16)
                with sp.Fori(0, (NU - 2) // 2) as i:
                    for s in range(2):
                        turn(i * 2 + s, s)
                for u in range((NU - 2) // 2 * 2, NU - 2):
                    turn(u, u % 2)
                sp.wait_ge(gu_done, NU)
                if following:
                    prefetch(core, sp, d[following])

            @block.tensor
            def _(pe):
                prime(pe, down_done, 2)

                def gate_up(u, turn, s, nth):
                    pe.wait_ge(core.landed[s], turn * 16 + 16 * (core.used[s] + nth + 1))
                    pe.wait_ge(a_made, u + 1)
                    w = core.ring[:, s, :].rearrange("p (m k n) -> p m k n", m=2, k=KT)
                    for f in range(2):
                        for m in range(2):
                            for k in range(KT):
                                last = nc.tensor.matmul(ps[s][f][:, m, :], w[:, m, k, f * P:(f + 1) * P], hT[:, k, :], start=k == 0, stop=k == KT - 1)
                    last.then_inc(gu_done, 1)

                def down_product(u, turn, s, nth, first=False, final=False):
                    pe.wait_ge(a_made, u + 3)
                    pe.wait_ge(wd_landed[s], turn * 16 + 16 * (nth + 1))
                    for f in range(2):
                        for t in range(LT):
                            for n in range(2):
                                last = nc.tensor.matmul(acc[t][n][:], a[s][:, f, t * P:(t + 1) * P], wd[s][:, f, n * NW:(n + 1) * NW],
                                                        start=first and f == 0, stop=final and f == 1)
                    last.then_inc(down_done, 1)
                gate_up(0, 0, 0, 0)
                gate_up(1, 0, 1, 0)
                down_product(0, 0, 0, 0, first=True)
                with pe.Fori(0, HU) as i:
                    gate_up(i * 2 + 2, i, 0, 1)
                    down_product(i * 2 + 1, i, 1, 0)
                    gate_up(i * 2 + 3, i, 1, 1)
                    down_product(i * 2 + 2, i, 0, 1)
                gate_up(NU - 1, 0, 0, HU + 1)
                down_product(NU - 2, 0, 1, HU)
                down_product(NU - 1, 0, 0, HU + 1, final=True)
                core.used[0] += NU // 2 + 1
                core.used[1] += NU // 2

            @block.scalar
            def _(act):
                def silus(u, s):
                    act.wait_ge(conv_done, u * 2 + 1)
                    nc.scalar.activation(c[s][:, 0, :], c[s][:, 0, :], ACT.Silu).then_inc(silu_done, 1)
                    act.wait_ge(conv_done, u * 2 + 2)
                    nc.scalar.activation(c[s][:, 1, :], c[s][:, 1, :], ACT.Silu).then_inc(silu_done, 1)
                with act.Fori(0, NU // 2) as i:
                    for s in range(2):
                        silus(i * 2 + s, s)
                silus(NU - 1, 0)

            @block.vector
            def _(dve):
                chain = Chain(dve, steps)
                v = nc.vector
                prime(dve, a_made, 2)
                dve.wait_ge(loads, 32)

                def unit(u, s):
                    dve.wait_ge(gu_done, u + 1)
                    dve.wait_ge(a_made, u + 1)
                    for f in range(2):
                        g, cf = ps[s][f][:, 0, :], c[s][:, f, :]
                        wk = lambda k: cw[:, bass.ds(u * 2 + f, 1), k]
                        chain.run(v.tensor_scalar(cf, g, wk(2), cb[:, bass.ds(u * 2 + f, 1)], ALU.mult, ALU.add))
                        chain.run(v.scalar_tensor_tensor(out=cf[:, 1:NL], in0=g[:, 0:NL - 1], scalar=wk(1), in1=cf[:, 1:NL], op0=ALU.mult, op1=ALU.add))
                        v.scalar_tensor_tensor(out=cf[:, 2:NL], in0=g[:, 0:NL - 2], scalar=wk(0), in1=cf[:, 2:NL], op0=ALU.mult, op1=ALU.add).then_inc(conv_done, 1)
                    dve.wait_ge(down_done, u + 1)
                    for f in range(2):
                        dve.wait_ge(silu_done, u * 2 + f + 1)
                        last = v.tensor_tensor(a[s][:, f, :], c[s][:, f, :], ps[s][f][:, 1, :], ALU.mult)
                    last.then_inc(a_made, 1)
                with chain.loop(NU // 2, 8) as i:
                    for s in range(2):
                        unit(i * 2 + s, s)
                unit(NU - 1, 0)
                dve.wait_ge(down_done, NU + 2)
                for t in range(LT):
                    for n in range(2):
                        x = core.x[:, t, n * NW:(n + 1) * NW]
                        v.tensor_tensor(x, x, acc[t][n][:], ALU.add).then_inc(added, 1)


def store(core, out):
    nc = core.nc
    with phase(core, "store") as ph:
        stored = ph.sem("stored")
        with ph.block() as block:
            @block.sync
            def _(sp):
                sp.dma_start(out.rearrange("a (t p) n -> p (a t) n", p=P), core.x[:]).then_inc(stored, 16)
                sp.wait_ge(stored, 16)


def load_context(core, xc):
    nc = core.nc
    with phase(core, "ctx") as ph:
        landed = ph.sem("landed")
        with ph.block() as block:
            @block.sync
            def _(sp):
                sp.dma_start(xc[:], core.d["ctx"].rearrange("(t p) n -> p t n", p=P)).then_inc(landed, 16)
                sp.wait_ge(landed, 16)


def build(nc, d, out, start=0):
    for name, shape in (("mod", [2, 2, 3 * DM]), ("u", [NTOK, E]), ("y", [NL, E]), ("z", [NL, E]), ("ptab", [P, GD, 2, CH + 1]),
                        ("qtab", [P, GD, 2 * CH]), ("a8", [P, 2, GD]), ("lags", [2, SG, BG, (2 * CH - 1) * SG])):
        d[name] = nc.dram_tensor(name + "_scratch", shape, F32, kind="Internal").ap()
    with ExitStack() as ctx:
        core = Core(nc, ctx, d)

        def within(stack, n, shape):
            return stack.enter_context(nc.sbuf_tensor(n, shape, F32))
        latent = [(core.x[:, t, :], 0) for t in range(LT)]
        modulation(core)
        with ExitStack() as first:
            hT = within(first, "hT", [P, KT, NTOK])
            with ExitStack() as mem:
                xc = within(mem, "xc", [P, LT, DM])
                load_context(core, xc)
                context = [(xc[:, t, :], 1) for t in range(LT)]
                modulated_transposes(core, "h0", 0, hT, xc)
                with ExitStack() as inner:
                    q, z = within(inner, "q", [P, TT, E]), within(inner, "z", [P, TT, E])
                    kn, v = within(inner, "kn", [P, TT, KVW]), within(inner, "v", [P, TT, KVW])
                    attention_projection(core, hT, q, kn, v, z)
                    kT, yzT = within(inner, "kT", [P, KVH, NTOK]), within(inner, "yzT", [P, ET, NTOK])
                    attention(core, q, kn, v, z, kT, hT, yzT)
                    residual_norm(core, "out0", 0, "w_out0", TT, latent + context, lambda k, t: yzT[:, k, t * P:(t + 1) * P], "s5_w_in")
                modulated_transposes(core, "h1", 1, hT, xc)
            ptab, qtab = within(first, "ptab", [P, GD, 2, CH + 1]), within(first, "qtab", [P, GD, 2 * CH])
            a8 = within(first, "a8", [P, 2, GD])
            s5_projection(core, hT, ptab, qtab, a8)
            S, u8 = within(first, "S", [P, LC + CC, GD]), within(first, "u8", [P, SN, LC])
            s5_chunk_inputs(core, qtab, S, u8)
            s5_carry(core, a8, S, hT)
            s5_outputs(core, ptab, qtab, S, u8)
        with ExitStack() as second:
            yzT = within(second, "yzT1", [P, ET, NL])
            s5_gate(core, yzT)
            residual_norm(core, "out1", 1, "w_out1", LT, latent, lambda k, t: yzT[:, k, t * P:(t + 1) * P], "ev_w_in")
        with ExitStack() as third:
            hT = within(third, "hT2", [P, KT, NL])
            mixT = within(third, "mixT", [P, KT, NL])
            with ExitStack() as mem:
                rms_transposes(core, "hm0", d["norm_mix_g"][0], hT)
                zz = within(mem, "zz0", [P, LT, EV_IN])
                project(core, "evin", "ev_w_in", EV_IN // NW, hT, zz, [(ACT.Gelu, 2), (ACT.Copy, 3)], "ev_w_out")
                gated_mlp(core, zz, mixT)
                dilated_attention(core, zz, mixT)
            project_residual(core, "evout", "ev_w_out", mixT, "ffn_gu0")
            rms_transposes(core, "hf0", d["norm_ffn_g"][0], hT)
            conv_ffn(core, "ffn0", 0, hT, "od_w_in")
            with ExitStack() as mem:
                rms_transposes(core, "hm1", d["norm_mix_g"][1], hT)
                zz, gaT = within(mem, "zz1", [P, LT, 2 * CK + 2 * CV]), within(mem, "gaT", [CR, NL])
                project(core, "odin", "od_w_in", (2 * CK + 2 * CV) // NW, hT, zz, [(ACT.Copy, 4), (ACT.Silu, 2)], "od_w_out",
                        extra=(d["od_w_ga"], gaT))
                gla(core, zz, gaT, mixT)
            project_residual(core, "odout", "od_w_out", mixT, "ffn_gu1")
            rms_transposes(core, "hf1", d["norm_ffn_g"][1], hT)
            conv_ffn(core, "ffn1", 1, hT, None)
            store(core, out)


def tiles_of(w, halves=1):
    k, n = w.shape
    a = w.reshape(halves, KT, P, n // NW, NW).transpose(3, 0, 2, 1, 4)
    return np.ascontiguousarray(a).reshape(n // NW * halves, P, KT * NW)


def constants():
    c = {"ident": np.eye(P, dtype=np.float32)}
    n = np.arange(NL, dtype=np.float32)
    row, col = np.floor(n / 64).astype(np.float32), (n % 64).astype(np.float32)
    inv = np.power(np.float32(10000.0), -np.arange(32, dtype=np.float32) / np.float32(32)).astype(np.float32)
    ar, ac = row[:, None] * inv, col[:, None] * inv
    cos = np.concatenate([np.cos(ar), np.cos(ar), np.cos(ac), np.cos(ac)], 1)
    sin = np.concatenate([-np.sin(ar), np.sin(ar), -np.sin(ac), np.sin(ac)], 1)
    lay = lambda a: np.ascontiguousarray(a.reshape(LT, P, P).transpose(1, 0, 2)).astype(np.float32)
    c["rope_cos"], c["rope_sin"] = lay(cos), lay(sin)
    i = np.arange(NL)
    m = np.where(np.abs(i[:, None] - i[None, :]) <= 128, 0.0, NEG).astype(np.float32)
    c["attn_mask"] = np.ascontiguousarray(m.reshape(LT, P, NL).transpose(1, 0, 2))
    t, s = i[:, None], i[None, :]
    seen = ((t - s >= 0) & (t - s <= 128)).astype(np.float32)
    for dilation in (4, 16):
        seen += (t >= s) & ((t - s) % dilation == 0)
    lay2 = lambda m: np.ascontiguousarray(m.reshape(LT, P, NL).transpose(1, 0, 2)).astype(np.float32)
    c["branch_count"], c["branch_bar"] = lay2(seen), lay2(np.where(seen > 0, 0.0, NEG))
    r = np.arange(P)
    c["causal"] = (r[:, None] <= r[None, :]).astype(np.float32)
    same = (r[:, None] // CCH == r[None, :] // CCH).astype(np.float32)
    c["chunk_sums"], c["chunk_ones"] = c["causal"] * same, same
    c["chunk_ends"] = np.ascontiguousarray(same[:, ::CCH])
    return c


def laid_out(i):
    a = {k: np.asarray(v) for k, v in i.items()}
    o = constants()
    o["x"], o["ctx"] = a["x"][0], a["ctx"][0]
    o["cc"] = np.ascontiguousarray(np.stack([a["c"][0], a["c_ctx"]]).reshape(2, KT, P).transpose(2, 1, 0))
    o["ada_w"] = np.concatenate([tiles_of(a["ada_w"][l]) for l in range(2)])
    o["ada_b"], o["ln_g"], o["ln_b"] = a["ada_b"], a["ln_g"], a["ln_b"]
    o["attn_w_in"] = tiles_of(a["attn_w_in"][0])
    o["attn_sink"] = a["attn_sink"]
    o["w_out0"], o["w_out1"] = tiles_of(a["w_out"][0], 2), tiles_of(a["w_out"][1], 2)
    s5 = {k: a["s5_" + k][0] for k in ("lam_re", "lam_im", "log_step", "b_re", "b_im", "c_re", "c_im")}
    o["s5_w_in"], o["s5_w_z"] = tiles_of(a["s5_w_in"][0][:, :E]), tiles_of(a["s5_w_in"][0][:, E:])
    twice = lambda m: np.concatenate([m, m])
    for k in ("lam_re", "lam_im"):
        o["s5_" + k] = twice(s5[k].transpose(2, 1, 0).reshape(SS, GD))
    o["s5_log_step"] = np.ascontiguousarray(s5["log_step"].T).reshape(1, GD)
    batched = lambda m: m.reshape(SS, NB, BD, SG).transpose(1, 0, 2, 3)
    b = {k: batched(s5[k].transpose(2, 1, 0, 3)) for k in ("b_re", "b_im")}
    c = {k: batched(s5[k].transpose(3, 1, 0, 2)) for k in ("c_re", "c_im")}
    both = lambda m, n: np.stack([np.concatenate([m, n], 1), np.concatenate([n, m], 1)], 2)
    o["s5_bab"], o["s5_cab"] = both(b["b_re"], b["b_im"]), both(c["c_re"], c["c_im"])
    o["s5_d"], o["s5_glu_b"] = a["s5_d"], a["s5_glu_b"]
    o["s5_glu_w"] = tiles_of(a["s5_glu_w"][0], 2)
    cols = lambda m: np.ascontiguousarray(m.reshape(m.shape[0], -1, P).transpose(0, 2, 1))
    o["norm_mix_g"], o["norm_ffn_g"] = cols(a["norm_mix_g_2"]), cols(a["norm_ffn_g_2"])
    o["ev_w_in"], o["ev_w_out"] = tiles_of(a["ev_w_in_2"][0]), tiles_of(a["ev_w_out_2"][0])
    o["ev_a_ln_g"], o["ev_a_ln_b"], o["ev_q_g"], o["ev_k_g"] = (a[f"ev_{k}_2"] for k in ("a_ln_g", "a_ln_b", "q_g", "k_g"))
    o["ev_a_wsT"] = np.ascontiguousarray(a["ev_a_ws_2"][0].transpose(2, 0, 1))
    o["ev_a_bsT"] = np.ascontiguousarray(a["ev_a_bs_2"][0].T)
    w = a["od_w_in_2"][0]
    wide = 2 * CK + 2 * CV
    o["od_w_in"], o["od_w_out"] = tiles_of(w[:, :wide]), tiles_of(a["od_w_out_2"][0])
    o["od_w_ga"] = np.ascontiguousarray(w[:, wide:].reshape(KT, P, CR).transpose(1, 0, 2))
    o["od_w_a2"], o["od_b_a"], o["od_head_g"] = a["od_w_a2_2"][0], a["od_b_a_2"], a["od_head_g_2"]
    for l in range(2):
        gu = np.stack([a["ffn_w_gate_2"][l], a["ffn_w_up_2"][l]])
        gu = gu.reshape(2, KT, P, FT // 2, 2 * P).transpose(3, 2, 0, 1, 4)
        o[f"ffn_gu{l}"] = np.ascontiguousarray(gu).reshape(FT // 2, P, KT * NW)
        o[f"ffn_down{l}"] = np.ascontiguousarray(a["ffn_w_down_2"][l].reshape(FT // 2, 2, P, DM).transpose(0, 2, 1, 3))
    cw = a["ffn_conv_w_2"].reshape(2, CONV, FT, P).transpose(0, 3, 2, 1)
    o["ffn_conv_w"], o["ffn_conv_b"] = np.ascontiguousarray(cw), cols(a["ffn_conv_b_2"])
    return o


def kernel(**inputs):
    import concourse.bacc as bacc
    from concourse.bass_utils import run_bass_kernel_spmd

    nc = bacc.Bacc("TRN2", target_bir_lowering=False, num_devices=1)
    arrays, d = {}, {}
    for name, a in laid_out(inputs).items():
        a = np.ascontiguousarray(a)
        arrays[f"in_{name}"] = a
        d[name] = nc.dram_tensor(f"in_{name}", a.shape, mybir.dt.from_np(a.dtype), kind="ExternalInput").ap()
    out = nc.dram_tensor("out_x", [1, NL, DM], F32, kind="ExternalOutput").ap()
    build(nc, d, out)
    r = run_bass_kernel_spmd(nc, [arrays], core_ids=[0])
    return r.results[0]["out_x"]
```

```python
from contextlib import ExitStack, contextmanager

import numpy as np
import concourse.bass as bass
from concourse import mybir

F32 = mybir.dt.float32
F32R = mybir.dt.float32r
I32 = mybir.dt.int32
ALU = mybir.AluOpType
ACT = mybir.ActivationFunctionType
AX = mybir.AxisListType.X

P = 128
DM = 1024
KT = DM // P
NL = 256
NC = 256
LT = NL // P
TT = (NL + NC) // P
NTOK = NL + NC
E = 2048
ET = E // P
HD = 128
NH = E // HD
KVH = NH // 4
KVW = KVH * HD
NW = 512
ALPHA = (2.0 * 2) ** 0.25
LN_EPS = 1e-5
RMS_EPS = 1e-6
NEG = -1e30


class Chain:

    def __init__(self, eng, sem, passed=None):
        self.eng, self.sem, self.base, self.k, self.passed = eng, sem, 0, 0, passed

    def run(self, ins):
        ins.then_inc(self.sem, 1)
        self.k += 1
        self.eng.wait_ge(self.sem, self.base + self.k)
        if self.passed is not None:
            self.eng.sem_inc(self.passed, 1)

    @contextmanager
    def loop(self, trips, per):
        start = self.base + self.k
        with self.eng.Fori(0, trips) as i:
            self.base, self.k = i * per + start, 0
            yield i
            assert self.k == per, (self.k, per)
        self.base, self.k = start + trips * per, 0


class Core:

    def __init__(self, nc, ctx, d):
        self.nc, self.d = nc, d
        sb = lambda name, shape: ctx.enter_context(nc.sbuf_tensor(f"resident_{name}", shape, F32))
        self.ring = sb("ring", [P, 2, KT * NW])
        self.x = sb("x", [P, LT, DM])
        self.ident = sb("ident", [P, P])
        self.modT = sb("modT", [P, 2, 16, 2])
        self.eps = sb("eps", [P, 2])
        self.landed = [ctx.enter_context(nc.semaphore(f"weights_landed{s}")) for s in range(2)]
        self.spent = []
        self.used = [0, 0]

    def load(self, eng, slot, src):
        eng.dma_start(self.ring[:, slot, :], src).then_inc(self.landed[slot], 16)

    def tile(self, slot):
        return self.ring[:, slot, :].rearrange("p (k n) -> p k n", k=KT)


def phase(core, name):
    nc = core.nc

    class Ph:
        def __enter__(s):
            s.ctx, s.sems = ExitStack(), []
            return s

        def __exit__(s, *e):
            core.spent += s.sems
            if len(core.spent) > 110:
                nc.clear_and_free_semaphores(core.spent)
                nc.all_engine_barrier()
                core.spent = []
            return s.ctx.__exit__(*e)

        def sb(s, n, shape, dt=F32):
            return s.ctx.enter_context(nc.sbuf_tensor(f"{name}_{n}", shape, dt))

        def ps(s, n, shape):
            return s.ctx.enter_context(nc.psum_tensor(f"{name}_{n}", shape, F32))

        def sem(s, n):
            s.sems.append(nc.alloc_semaphore(name=f"{name}_{n}"))
            return s.sems[-1]

        def block(s):
            return nc.Block()

    return Ph()



def prefetch(core, eng, units):
    for s in range(2):
        core.load(eng, s, units[s])


def stream_loads(core, sp, tiles, groups, halves, ntt, mm_done, half_used):
    if halves == 2:
        with sp.Fori(0, groups - 1) as i:
            sp.wait_ge(half_used, i + 1)
            core.load(sp, 0, tiles[i * 2 + 2])
            sp.wait_ge(mm_done, i * ntt + ntt)
            core.load(sp, 1, tiles[i * 2 + 3])
        return
    if groups > 3:
        with sp.Fori(0, (groups - 2) // 2) as i:
            for s in range(2):
                sp.wait_ge(mm_done, i * (2 * ntt) + (s + 1) * ntt)
                core.load(sp, s, tiles[i * 2 + 2 + s])
    for u in range(2 + (groups - 2) // 2 * 2, groups):
        sp.wait_ge(mm_done, (u - 1) * ntt)
        core.load(sp, u % 2, tiles[u])


def stream_products(core, pe, groups, halves, ntt, lhs, bank, mm_done, half_used, free, rows=P):
    def group(g, parity):
        for sem, n in free:
            pe.wait_ge(sem, g * n + 1)
        for h in range(halves):
            ub = parity * halves + h
            slot = ub % 2
            nth = (g * halves + h - slot) // 2 if isinstance(g, int) else None
            if nth is None:
                turn_tiles = halves
                pe.wait_ge(core.landed[slot], turn * (16 * turn_tiles) + 16 * (core.used[slot] + ub // 2 + 1))
            else:
                pe.wait_ge(core.landed[slot], 16 * (core.used[slot] + nth + 1))
            for t in range(ntt):
                for k in range(KT):
                    last = nc.tensor.matmul(bank(parity, t)[0:rows], lhs(h * KT + k, t), core.tile(slot)[:, k, :],
                                            start=h == 0 and k == 0, stop=h == halves - 1 and k == KT - 1)
                if h == halves - 1:
                    last.then_inc(mm_done, 1)
            if h < halves - 1:
                last.then_inc(half_used, 1)

    nc = core.nc
    if groups > 3:
        with pe.Fori(0, groups // 2) as turn:
            for parity in range(2):
                group(turn * 2 + parity, parity)
        for g in range(groups // 2 * 2, groups):
            group(g, g % 2)
    else:
        for g in range(groups):
            group(g, g % 2)
    for s in range(2):
        core.used[s] += (groups * halves + 1 - s) // 2


def stream_turns(eng, groups):
    def run(body):
        if groups > 3:
            with eng.Fori(0, groups // 2) as i:
                for parity in range(2):
                    body(i * 2 + parity, parity)
            for g in range(groups // 2 * 2, groups):
                body(g, g % 2)
        else:
            for g in range(groups):
                body(g, g % 2)
    return run


HK = KT // 2


class Split:

    def __init__(self, core, ph, groups, halves, ntt, mm_done, src=None, lhs=None):
        self.core, self.groups, self.halves, self.ntt, self.mm_done, self.src = core, groups, halves, ntt, mm_done, src
        part = lambda name, shape: ph.sb(name, shape, F32R)
        self.w = [part("w_lead", [P, 2, HK, NW]), part("w_rest", [P, 2, HK, NW])]
        if src is not None:
            lhs = [part("x_lead", [P, halves * KT, ntt * P]), part("x_rest", [P, halves * KT, ntt * P])]
        self.lhs = lhs
        self.lead_made, self.rest_made, self.x_lead_made, self.x_rest_made = [ph.sem(n) for n in ("lead_made", "rest_made", "x_lead_made", "x_rest_made")]
        self.used = [ph.sem(f"used{j}") for j in range(2)]
        self.landed_before = list(core.used)
        for s in range(2):
            core.used[s] += (groups * halves + 1 - s) // 2

    def loads(self, sp, tiles):
        n = self.groups * self.halves
        if n > 4:
            with sp.Fori(0, (n - 2) // 2) as i:
                for s in range(2):
                    sp.wait_ge(self.rest_made, i * 4 + 2 * (s + 1))
                    self.core.load(sp, s, tiles[i * 2 + 2 + s])
        for u in range(2 + (n - 2) // 2 * 2 if n > 4 else 2, n):
            sp.wait_ge(self.rest_made, 2 * (u - 1))
            self.core.load(sp, u % 2, tiles[u])

    def following(self, sp, tiles):
        sp.wait_ge(self.rest_made, 2 * self.groups * self.halves)
        prefetch(self.core, sp, tiles)

    def _slot(self, g, parity, h):
        return h % 2 if self.halves == 2 else parity

    def lead(self, act, g, parity, h, j, first=False):
        r = self._slot(g, parity, h)
        per = 16 if self.halves == 2 else 8
        act.wait_ge(self.core.landed[r], g * per + (0 if self.halves == 2 else -8 * r) + 16 * (self.landed_before[r] + 1))
        if not first:
            if j == 0:
                act.wait_ge(self.used[0], g * self.halves + h)
            elif h > 0:
                act.wait_ge(self.used[1], g * (self.halves - 1) + h)
            else:
                act.wait_ge(self.mm_done, g * self.ntt)
        self.core.nc.scalar.activation(self.w[0][:, j], self.core.tile(r)[:, j * HK:(j + 1) * HK, :], ACT.Copy).then_inc(self.lead_made, 1)

    def rest(self, dve, g, parity, h, j):
        dve.wait_ge(self.lead_made, g * (2 * self.halves) + 2 * h + j + 1)
        r = self._slot(g, parity, h)
        self.core.nc.vector.tensor_tensor(self.w[1][:, j], self.core.tile(r)[:, j * HK:(j + 1) * HK, :], self.w[0][:, j].bitcast(F32),
                                          ALU.subtract).then_inc(self.rest_made, 1)

    def _x_pieces(self):
        return range(2 * self.halves) if self.src is not None else ()

    def start_scalar(self, act):
        for piece in range(2 * self.halves):
            if piece < 2:
                self.lead(act, 0, 0, 0, piece, first=True)
            if self.src is not None:
                ks = slice(piece * HK, (piece + 1) * HK)
                self.core.nc.scalar.activation(self.lhs[0][:, ks], self.src[:, ks], ACT.Copy).then_inc(self.x_lead_made, 1)

    def start_vector(self, dve):
        for piece in range(2 * self.halves):
            if piece < 2:
                self.rest(dve, 0, 0, 0, piece)
            if self.src is not None:
                ks = slice(piece * HK, (piece + 1) * HK)
                dve.wait_ge(self.x_lead_made, piece + 1)
                self.core.nc.vector.tensor_tensor(self.lhs[1][:, ks], self.src[:, ks], self.lhs[0][:, ks].bitcast(F32), ALU.subtract).then_inc(self.x_rest_made, 1)

    def _ahead(self, g, parity, final):
        for h in range(1, self.halves):
            for j in range(2):
                yield g, parity, h, j
        if not final:
            for j in range(2):
                yield g + 1, 1 - parity, 0, j

    def ahead_scalar(self, act, g, parity, final=False):
        for at in self._ahead(g, parity, final):
            self.lead(act, *at)

    def ahead_vector(self, dve, g, parity, final=False):
        for at in self._ahead(g, parity, final):
            self.rest(dve, *at)

    def turns(self, eng, ahead, body):
        looped = (self.groups - 2) // 2 if self.groups > 4 else 0
        if looped:
            with eng.Fori(0, looped) as i:
                for parity in range(2):
                    ahead(eng, i * 2 + parity, parity)
                    body(i * 2 + parity, parity)
        for g in range(2 * looped, self.groups):
            ahead(eng, g, g % 2, g == self.groups - 1)
            body(g, g % 2)

    def products(self, pe, bank, free):
        nc, last_half = self.core.nc, 2 * self.halves - 1

        def group(g, parity):
            for sem, n in free:
                pe.wait_ge(sem, g * n + 1)
            for half in range(2 * self.halves):
                j = half % 2
                pe.wait_ge(self.rest_made, g * (2 * self.halves) + half + 1)
                if self.src is not None:
                    pe.wait_ge(self.x_rest_made, half + 1)
                for t in range(self.ntt):
                    for k in range(HK):
                        for x, w in ((0, 0), (0, 1), (1, 0)):
                            last = nc.tensor.matmul(bank(parity, t), self.lhs[x][:, half * HK + k, t * P:(t + 1) * P], self.w[w][:, j, k, :],
                                                    start=(half, k, x, w) == (0, 0, 0, 0),
                                                    stop=(half, k, x) == (last_half, HK - 1, 1))
                    if half == last_half:
                        last.then_inc(self.mm_done, 1)
                if half < last_half:
                    last.then_inc(self.used[j], 1)
        looped = self.groups // 2 if self.groups > 3 else 0
        if looped:
            with pe.Fori(0, looped) as turn:
                for parity in range(2):
                    group(turn * 2 + parity, parity)
        for g in range(2 * looped, self.groups):
            group(g, g % 2)


def prime(eng, sem, n):
    eng.sem_inc(sem, n)


def dve_copy(nc, dst, src):
    return nc.vector.tensor_scalar(dst, src, 1.0, None, ALU.mult)


def modulation(core, xc):
    nc, d = core.nc, core.d
    with phase(core, "ada") as ph:
        ccT = ph.sb("ccT", [P, KT, 2])
        sT = ph.sb("sT", [P, KT, 2])
        mod = ph.sb("mod", [2, 2, 3 * DM])
        bias = ph.sb("bias", [2, 2, 3 * DM])
        ps = [ph.ps(f"ps{s}", [P, 512]) for s in range(2)]
        psT = ph.ps("psT", [P, 64])
        s_in, s_silu, s_const = ph.sem("in"), ph.sem("silu"), ph.sem("const")
        mm_done, mod_done, turned = ph.sem("mm_done"), ph.sem("mod_done"), ph.sem("turned")
        modT_done, stored, biased = ph.sem("modT_done"), ph.sem("stored"), ph.sem("biased")
        NT = 2 * 3 * DM // NW
        ptab, qtab = ph.sb("ptab", [P, GD, 2, CH + 1]), ph.sb("qtab", [P, GD, 2 * CH])
        a8 = ph.sb("a8", [P, 2, GD])
        tables_done = ph.sem("tables_done")
        tables_on_scalar, tables_on_vector = s5_tables(core, ph, ptab, qtab, a8)

        with ph.block() as block:
            @block.sync
            def _(sp):
                prefetch(core, sp, d["ada_w"])
                stream_loads(core, sp, d["ada_w"], NT, 1, 1, mm_done, None)
                sp.wait_ge(mm_done, NT)
                prefetch(core, sp, d["attn_w_in"])
                sp.wait_ge(tables_done, 1)
                for dst, src in (("ptab", ptab), ("qtab", qtab), ("a8", a8)):
                    sp.dma_start(d[dst], src[:]).then_inc(stored, 16)
                sp.wait_ge(biased, 1)
                sp.dma_start(d["mod"][:].rearrange("l r n -> r l n"), mod[:]).then_inc(stored, 16)
                sp.wait_ge(stored, 64)

            @block.scalar
            def _(act):
                act.dma_start(ccT[:], d["cc"][:]).then_inc(s_in, 16)
                act.dma_start(core.ident[:], d["ident"][:]).then_inc(s_const, 16)
                for r in range(2):
                    act.dma_start(bias[r:r + 1], d["ada_b"][:].rearrange("(a l) n -> a l n", a=1)).then_inc(s_const, 16)
                for t in range(LT):
                    act.dma_start(core.x[:, t, :], d["x"][t * P:(t + 1) * P, :]).then_inc(s_const, 16)
                act.dma_start(xc[:], d["ctx"].rearrange("(t p) n -> p t n", p=P)).then_inc(s_const, 16)
                act.wait_ge(s_in, 16)
                nc.scalar.activation(sT[:], ccT[:], ACT.Silu).then_inc(s_silu, 1)
                tables_on_scalar(act)
                prime(act, mod_done, 2)

                def empty(g, parity):
                    act.wait_ge(mm_done, g + 1)
                    nc.scalar.activation(mod[:].rearrange("r l n -> r (l n)")[:, bass.ts(g, NW)], ps[parity][0:2, :], ACT.Copy).then_inc(mod_done, 1)
                stream_turns(act, NT)(empty)

            @block.vector
            def _(dve):
                nc.vector.memset(core.eps[:, 0:1], LN_EPS)
                nc.vector.memset(core.eps[:, 1:2], RMS_EPS)
                tables_on_vector(dve)
                dve.sem_inc(tables_done, 1)
                dve.wait_ge(s_const, 16 * (4 + LT))
                dve.wait_ge(mod_done, NT + 2)
                nc.vector.tensor_tensor(mod[:], mod[:], bias[:], ALU.add).then_inc(biased, 1)
                dve.wait_ge(turned, 1)
                nc.vector.tensor_copy(core.modT[:].rearrange("p l b r -> p (l b r)"), psT[:]).then_inc(modT_done, 1)
                dve.wait_ge(modT_done, 1)
                nc.vector.tensor_scalar(core.modT[:, :, 8:16, :], core.modT[:, :, 8:16, :], 1.0, None, ALU.add).then_inc(modT_done, 1)

            @block.tensor
            def _(pe):
                pe.wait_ge(s_silu, 1)
                stream_products(core, pe, NT, 1, 1, lambda k, t: sT[:, k, :], lambda parity, t: ps[parity],
                                mm_done, None, [(mod_done, 1)], rows=2)
                pe.wait_ge(biased, 1)
                pe.wait_ge(s_const, 16 * (4 + LT))
                for l in range(2):
                    for b in range(16):
                        c = (l * 16 + b) * 2
                        last = nc.tensor.transpose(psT[:, c:c + 2], mod[:, l, b * P:(b + 1) * P], core.ident[0:2, 0:2])
                last.then_inc(turned, 1)


def modulated_transposes(core, name, layer, hT, xc, parts=None):
    nc = core.nc
    with phase(core, name) as ph:
        lead_made = ph.sem("lead_made")
        rest_made = ph.sem("rest_made")
        if parts is not None:
            hT = ph.sb("hT", [P, KT, NTOK])
        ps = [ph.ps(f"ps{b}", [P, NTOK]) for b in range(4)]
        turned, act_free, dve_free = ph.sem("turned"), ph.sem("act_free"), ph.sem("dve_free")
        halves = ((0, slice(0, NL)), (1, slice(NL, NTOK)))
        with ph.block() as block:
            @block.tensor
            def _(pe):
                for k in range(KT):
                    if k >= 4:
                        pe.wait_ge(dve_free if k % 2 else act_free, (k - 4) // 2 + 1)
                    for t in range(TT):
                        src = (core.x if t < LT else xc)[:, t % LT, k * P:(k + 1) * P]
                        last = nc.tensor.transpose(ps[k % 4][:, t * P:(t + 1) * P], src, core.ident[:])
                    last.then_inc(turned, 1)

            @block.scalar
            def _(act):
                for k in range(0, KT, 2):
                    act.wait_ge(turned, k + 1)
                    for r, cols in halves:
                        last = nc.scalar.activation(hT[:, k, cols], ps[k % 4][:, cols], ACT.Identity, bias=core.modT[:, layer, k, r:r + 1],
                                                    scale=core.modT[:, layer, 8 + k, r:r + 1])
                    last.then_inc(act_free, 1)
                if parts is not None:
                    for h in range(2):
                        act.wait_ge(act_free, (h + 1) * HK // 2)
                        act.wait_ge(dve_free, (h + 1) * HK // 2)
                        ks = slice(h * HK, (h + 1) * HK)
                        nc.scalar.activation(parts[0][:, ks], hT[:, ks], ACT.Copy).then_inc(lead_made, 1)

            @block.vector
            def _(dve):
                for k in range(1, KT, 2):
                    dve.wait_ge(turned, k + 1)
                    for r, cols in halves:
                        last = nc.vector.tensor_scalar(hT[:, k, cols], ps[k % 4][:, cols], core.modT[:, layer, 8 + k, r:r + 1],
                                                       core.modT[:, layer, k, r:r + 1], ALU.mult, ALU.add)
                    last.then_inc(dve_free, 1)
                if parts is not None:
                    for h in range(2):
                        dve.wait_ge(lead_made, h + 1)
                        ks = slice(h * HK, (h + 1) * HK)
                        nc.vector.tensor_tensor(parts[1][:, ks], hT[:, ks], parts[0][:, ks].bitcast(F32), ALU.subtract).then_inc(rest_made, 1)


def attention_projection(core, hparts, q, kn, v, z):
    nc, d = core.nc, core.d
    with phase(core, "qkvz") as ph:
        cos = ph.sb("cos", [P, LT, P])
        sin = ph.sb("sin", [P, LT, P])
        straight = ph.sb("straight", [P, LT, NW])
        crossed = ph.sb("crossed", [P, LT, NW])
        ps = [[ph.ps(f"ps{s}{t}", [P, NW]) for t in range(TT)] for s in range(2)]
        mm_done, act_free, dve_free, tables = ph.sem("mm_done"), ph.sem("act_free"), ph.sem("dve_free"), ph.sem("tables")
        steps, silu_done = ph.sem("steps"), ph.sem("silu_done")
        NT = (2 * E + 2 * KVW) // NW
        split = Split(core, ph, NT, 1, TT, mm_done, lhs=hparts)
        with ph.block() as block:
            @block.sync
            def _(sp):
                split.loads(sp, d["attn_w_in"])
                split.following(sp, d["w_out0"])

            @block.tensor
            def _(pe):
                split.products(pe, lambda s, t: ps[s][t][:], [(act_free, 2), (dve_free, 2)])

            @block.scalar
            def _(act):
                act.dma_start(cos[:], d["rope_cos"][:]).then_inc(tables, 16)
                act.dma_start(sin[:], d["rope_sin"][:]).then_inc(tables, 16)
                prime(act, act_free, 3)
                split.start_scalar(act)

                def empty(g, s, dst, tiles, func):
                    split.ahead_scalar(act, g, s, isinstance(g, int) and g == NT - 1)
                    for t in tiles:
                        act.wait_ge(mm_done, g * TT + t + 1)
                        nc.scalar.activation(dst(t), ps[s][t][:], func).then_inc(act_free, 1)
                with act.Fori(0, 2) as i:
                    for s in range(2):
                        empty(i * 2 + s, s, lambda t: q[:, t, bass.ts(i * 2 + s, NW)], (2, 3), ACT.Copy)
                empty(4, 0, lambda t: kn[:, t, :], (2, 3), ACT.Copy)
                empty(5, 1, lambda t: v[:, t, :], (2, 3), ACT.Copy)
                for g in range(6, NT):
                    empty(g, g % 2, lambda t: z[:, t, (g - 6) * NW:(g - 5) * NW], (2, 3), ACT.Silu)
                    for t in range(LT):
                        nc.scalar.activation(z[:, t, (g - 6) * NW:(g - 5) * NW], ps[g % 2][t][:], ACT.Silu).then_inc(silu_done, 1)

            @block.vector
            def _(dve):
                prime(dve, dve_free, 3)
                dve.wait_ge(tables, 32)
                chain = Chain(dve, steps)
                split.start_vector(dve)

                def rotate(g, s, dst):
                    split.ahead_vector(dve, g, s)
                    for t in range(LT):
                        dve.wait_ge(mm_done, g * TT + t + 1)
                        x4 = ps[s][t][:].rearrange("p (h c b w) -> p h c b w", h=4, c=2, b=2)
                        y4 = crossed[:, t, :].rearrange("p (h c b w) -> p h c b w", h=4, c=2, b=2)
                        tb = lambda tab, b: tab[:, t, :].rearrange("p (c b w) -> p c b w", c=2, b=2)[:, :, b, :]
                        nc.vector.tensor_tensor(straight[:, t, :].rearrange("p (h w) -> p h w", h=4), ps[s][t][:].rearrange("p (h w) -> p h w", h=4),
                                                cos[:, t, :].unsqueeze(1).to_broadcast([P, 4, P]), ALU.mult)
                        for b in range(2):
                            last = nc.vector.tensor_tensor(y4[:, :, :, b, :], x4[:, :, :, 1 - b, :],
                                                           tb(sin, b).unsqueeze(1).to_broadcast([P, 4, 2, 32]), ALU.mult)
                        chain.run(last)
                        nc.vector.tensor_tensor(dst(t), straight[:, t, :], crossed[:, t, :], ALU.add).then_inc(dve_free, 1)
                with chain.loop(2, 4) as i:
                    for s in range(2):
                        rotate(i * 2 + s, s, lambda t: q[:, t, bass.ts(i * 2 + s, NW)])
                rotate(4, 0, lambda t: kn[:, t, :])

                def empty(g, s, dst):
                    split.ahead_vector(dve, g, s)
                    for t in range(LT):
                        dve.wait_ge(mm_done, g * TT + t + 1)
                        nc.vector.tensor_copy(dst(t), ps[s][t][:]).then_inc(dve_free, 1)
                empty(5, 1, lambda t: v[:, t, :])
                dve.wait_ge(dve_free, 3 + 6 * LT)
                for g in range(6, NT):
                    split.ahead_vector(dve, g, g % 2, g == NT - 1)
                    dve.wait_ge(silu_done, (g - 5) * LT)
                    dve.sem_inc(dve_free, LT)


def attention(core, q, kn, v, z, kT, work, yzT):
    nc, d = core.nc, core.d
    SC = HD ** -0.5
    with phase(core, "attn") as ph:
        s_sb = work[:, 0:3, :]
        p_sb = work[:, 3:6, :]
        qs = work[:, 6, :]
        qT = work[:, 7, :]
        pT = [ph.sb(f"pT{s}", [P, 3, NW]) for s in range(2)]
        yz = ph.sb("yz", [P, TT, HD])
        mask = ph.sb("mask", [P, LT, NL])
        sink = ph.sb("sink", [P, NH])
        mx = ph.sb("mx", [P, TT])
        nm = ph.sb("nm", [P, TT])
        sk = ph.sb("sk", [P, TT])
        esk = ph.sb("esk", [P, TT])
        den = ph.sb("den", [P, TT])
        tot = ph.sb("tot", [P, TT])
        rden = [ph.sb(f"rden{s}", [P, TT]) for s in range(2)]
        ps_t = ph.ps("ps_t", [P, NW])
        ps_s = [ph.ps(f"ps_s{b}", [P, NW]) for b in range(3)]
        ps_p = [ph.ps(f"ps_p{b}", [P, NW]) for b in range(3)]
        ps_y = ph.ps("ps_y", [P, TT, HD])
        names = ["qs_ready", "q_turned", "qT_ready", "scores_ready", "max_ready", "exp_ready", "p_turned",
                 "pT_act", "pT_dve", "pv_ready", "yz_ready", "yz_turned", "yzT_ready", "k_turned", "kT_ready",
                 "loads", "steps"]
        (qs_ready, q_turned, qT_ready, scores_ready, max_ready, exp_ready, p_turned, pT_act, pT_dve, pv_ready,
         yz_ready, yz_turned, yzT_ready, k_turned, kT_ready, loads, steps) = [ph.sem(n) for n in names]
        ident = core.ident

        def schedule(eng, chain, per, step):
            for i in (-1, 0, 1):
                step(i, i % 2)
            turns = (NH - 4) // 2
            loop = chain.loop(turns, per) if chain else eng.Fori(0, turns)
            with loop as n:
                for s in range(2):
                    step(n * 2 + 2 + s, s)
            for i in range(2 + 2 * turns, NH + 2):
                step(i, i % 2)

        def exists(i, shift=0):
            return not isinstance(i, int) or 0 <= i + shift < NH

        with ph.block() as block:
            @block.gpsimd
            def _(pool):
                heads = lambda h: nc.gpsimd.tensor_copy(qs.rearrange("p (t w) -> p t w", t=TT), q[:, :, bass.ts(h, HD)]).then_inc(qs_ready, 1)
                heads(0)
                with pool.Fori(0, NH - 1) as h:
                    pool.wait_ge(q_turned, h + 1)
                    heads(h + 1)

            @block.tensor
            def _(pe):
                for g in range(KVH):
                    if g >= 3:
                        pe.wait_ge(kT_ready, g - 2)
                    for t in range(TT):
                        last = nc.tensor.transpose(ps_s[g % 3][:, t * P:(t + 1) * P], kn[:, t, g * HD:(g + 1) * HD], ident[:])
                    last.then_inc(k_turned, 1)

                def turn_queries(h):
                    pe.wait_ge(qs_ready, h + 1)
                    pe.wait_ge(qT_ready, h + 1)
                    pe.wait_ge(yzT_ready, h + 1)
                    for t in range(TT):
                        last = nc.tensor.transpose(ps_t[:, t * P:(t + 1) * P], qs[:, t * P:(t + 1) * P], ident[:])
                    last.then_inc(q_turned, 1)

                def scores(h):
                    pe.wait_ge(qT_ready, h + 2)
                    pe.wait_ge(max_ready, h + 1)
                    for t in range(LT):
                        nc.tensor.matmul(ps_s[t][:], qT[:, t * P:(t + 1) * P], kT[:, h // 4, :], start=True, stop=True)
                    for t in range(2):
                        last = nc.tensor.matmul(ps_s[2][:, t * NC:(t + 1) * NC], qT[:, (LT + t) * P:(LT + t + 1) * P],
                                                kT[:, h // 4, NL:NTOK], start=True, stop=True)
                    last.then_inc(scores_ready, 1)

                def turn_probabilities(h):
                    pe.wait_ge(exp_ready, h + 1)
                    pe.wait_ge(pT_act, h + 1)
                    pe.wait_ge(pT_dve, h * 2 + 1)
                    for b in range(3):
                        for j in range(4):
                            last = nc.tensor.transpose(ps_p[b][:, j * P:(j + 1) * P], p_sb[:, b, j * P:(j + 1) * P], ident[:])
                        last.then_inc(p_turned, 1)

                def mix(h, s):
                    pe.wait_ge(pT_act, h + 2)
                    pe.wait_ge(pT_dve, h * 2 + 3)
                    pe.wait_ge(yz_ready, h + 1)
                    vcols = bass.ts(h // 4, HD)
                    for t in range(LT):
                        for j in range(4):
                            nc.tensor.matmul(ps_y[:, t, :], pT[s][:, t, j * P:(j + 1) * P], v[:, j, vcols], start=j == 0, stop=j == 3)
                    for t in range(2):
                        for j in range(2):
                            last = nc.tensor.matmul(ps_y[:, LT + t, :], pT[s][:, 2, (t * 2 + j) * P:(t * 2 + j + 1) * P],
                                                    v[:, LT + j, vcols], start=j == 0, stop=j == 1)
                    last.then_inc(pv_ready, 1)

                def turn_outputs(h):
                    pe.wait_ge(yz_ready, h + 2)
                    pe.wait_ge(yzT_ready, h + 4)
                    pe.wait_ge(qT_ready, min(h + 5, NH + 1) if isinstance(h, int) else h + 5)
                    for t in range(TT):
                        last = nc.tensor.transpose(ps_t[:, t * P:(t + 1) * P], yz[:, t, :], ident[:])
                    last.then_inc(yz_turned, 1)

                prime(pe, p_turned, 1)
                prime(pe, scores_ready, 1)
                prime(pe, pv_ready, 2)
                prime(pe, yz_turned, 1)
                turn_queries(0)
                pe.wait_ge(kT_ready, KVH)

                def step(i, s):
                    if exists(i, 1):
                        scores(i + 1)
                    if exists(i, -2):
                        turn_outputs(i - 2)
                    if exists(i):
                        turn_probabilities(i)
                    if exists(i, 2):
                        turn_queries(i + 2)
                    if exists(i, -1):
                        mix(i - 1, 1 - s)
                schedule(pe, None, 0, step)

            @block.scalar
            def _(act):
                act.dma_start(mask[:], d["attn_mask"][:]).then_inc(loads, 16)
                act.dma_start(sink[:], d["attn_sink"][0:1, :].to_broadcast([P, NH])).then_inc(loads, 16)
                prime(act, pT_act, 1)
                prime(act, qT_ready, 1)
                prime(act, yzT_ready, 4)
                for g in range(KVH):
                    act.wait_ge(k_turned, g + 1)
                    nc.scalar.activation(kT[:, g, :], ps_s[g % 3][:], ACT.Copy).then_inc(kT_ready, 1)

                def queries(h):
                    act.wait_ge(q_turned, h + 1)
                    act.wait_ge(scores_ready, h + 1)
                    nc.scalar.activation(qT[:], ps_t[:], ACT.Copy).then_inc(qT_ready, 1)

                def exponentials(h):
                    act.wait_ge(max_ready, h + 2)
                    act.wait_ge(p_turned, h * 3 + 1)
                    for t in range(TT):
                        src = s_sb[:, t, :] if t < LT else s_sb[:, 2, (t - LT) * NC:(t - LT + 1) * NC]
                        dst = p_sb[:, t, :] if t < LT else p_sb[:, 2, (t - LT) * NC:(t - LT + 1) * NC]
                        nc.scalar.activation(dst, src, ACT.Exp, bias=nm[:, t:t + 1], accum_out=den[:, t:t + 1])
                    nc.scalar.activation(esk[:], sk[:], ACT.Exp).then_inc(exp_ready, 1)

                def step(i, s):
                    if exists(i, -2):
                        act.wait_ge(yz_turned, i)
                        nc.scalar.activation(yzT[:, i - 2, :], ps_t[:], ACT.Copy).then_inc(yzT_ready, 1)
                    if exists(i):
                        act.wait_ge(p_turned, i * 3 + 2)
                        act.wait_ge(pv_ready, i + 1)
                        nc.scalar.activation(pT[s][:, 0, :], ps_p[0][:], ACT.Copy).then_inc(pT_act, 1)
                    if exists(i, 2):
                        queries(i + 2)
                    if exists(i, 1):
                        exponentials(i + 1)
                act.wait_ge(q_turned, 1)
                nc.scalar.activation(qT[:], ps_t[:], ACT.Copy).then_inc(qT_ready, 1)
                schedule(act, None, 0, step)

            @block.vector
            def _(dve):
                chain = Chain(dve, steps)
                prime(dve, pT_dve, 1)
                prime(dve, max_ready, 1)
                prime(dve, yz_ready, 1)
                dve.wait_ge(loads, 32)

                def maxima(h):
                    dve.wait_ge(scores_ready, h + 2)
                    for t in range(LT):
                        nc.vector.scalar_tensor_tensor(out=s_sb[:, t, 0:NL], in0=ps_s[t][:, 0:NL], scalar=SC, in1=mask[:, t, :], op0=ALU.mult, op1=ALU.add)
                        nc.vector.tensor_scalar(s_sb[:, t, NL:NTOK], ps_s[t][:, NL:NTOK], SC, None, ALU.mult)
                    chain.run(nc.vector.tensor_scalar(s_sb[:, 2, :], ps_s[2][:], SC, None, ALU.mult))
                    nc.vector.tensor_reduce(mx[:, 0:LT], s_sb[:, 0:LT, :], AX, ALU.max)
                    chain.run(nc.vector.tensor_reduce(mx[:, LT:TT], s_sb[:, 2, :].rearrange("p (t w) -> p t w", t=2), AX, ALU.max))
                    chain.run(nc.vector.tensor_scalar(nm[:], mx[:], sink[:, bass.ds(h, 1)], -1.0, ALU.max, ALU.mult))
                    nc.vector.tensor_scalar(sk[:], nm[:], sink[:, bass.ds(h, 1)], None, ALU.add).then_inc(max_ready, 1)

                def step(i, s):
                    if exists(i):
                        dve.wait_ge(exp_ready, i + 1)
                        chain.run(nc.vector.tensor_tensor(tot[:], den[:], esk[:], ALU.add))
                        chain.run(nc.vector.reciprocal(rden[s][:], tot[:]))
                    if exists(i, 1):
                        maxima(i + 1)
                    if exists(i):
                        for b in (1, 2):
                            dve.wait_ge(p_turned, i * 3 + 2 + b)
                            if b == 1:
                                dve.wait_ge(pv_ready, i + 1)
                            nc.vector.tensor_copy(pT[s][:, b, :], ps_p[b][:]).then_inc(pT_dve, 1)
                    if exists(i, -1):
                        dve.wait_ge(pv_ready, i + 2)
                        dve.wait_ge(yz_turned, i)
                        for t in range(TT):
                            last = nc.vector.scalar_tensor_tensor(out=yz[:, t, :], in0=ps_y[:, t, :], scalar=rden[1 - s][:, t:t + 1],
                                                                  in1=z[:, t, bass.ts(i - 1, HD)], op0=ALU.mult, op1=ALU.mult)
                        last.then_inc(yz_ready, 1)
                schedule(dve, chain, 10, step)


def layer_norm_tile(core, chain, act_rstd, t, x, stats, mv, rstd, g_row, b_row):
    nc = core.nc
    for c in range(2):
        last = nc.vector.bn_stats(stats[:, c, :], x[:, c * NW:(c + 1) * NW])
    chain.run(last)
    chain.run(nc.vector.bn_aggr(mv[:], stats[:]))
    act_rstd()
    chain.run(nc.vector.reciprocal(rstd[:], rstd[:]))
    chain.run(nc.vector.tensor_scalar(x, x, mv[:, 0:1], rstd[:, 0:1], ALU.subtract, ALU.mult))
    chain.run(nc.vector.tensor_tensor(x, x, g_row[:], ALU.mult))
    chain.run(nc.vector.tensor_tensor(x, x, b_row[:], ALU.add))


def residual_norm(core, name, layer, weights, tiles, xs, yzT, following):
    nc, d = core.nc, core.d
    n = len(xs)
    with phase(core, name) as ph:
        rows = sorted({r for _, r in xs})
        gate = ph.sb("gate", [P, 2, DM])
        g_row = ph.sb("g_row", [P, DM])
        b_row = ph.sb("b_row", [P, DM])
        stats = ph.sb("stats", [P, 2, 6])
        mv = ph.sb("mv", [P, 2])
        rstd = ph.sb("rstd", [P, 1])
        tmp = ph.sb("tmp", [P, NW])
        ps = [[ph.ps(f"ps{s}{t}", [P, NW]) for t in range(n)] for s in range(2)]
        names = ["mm_done", "rows_ready", "steps", "var_ready", "std_ready", "ready"]
        mm_done, rows_ready, steps, var_ready, std_ready, ready = [ph.sem(x) for x in names]
        split = Split(core, ph, 2, 2, n, mm_done, src=yzT)
        with ph.block() as block:
            @block.sync
            def _(sp):
                split.loads(sp, d[weights])
                split.following(sp, d[following])

            @block.tensor
            def _(pe):
                split.products(pe, lambda s, t: ps[s][t][:], [])

            @block.scalar
            def _(act):
                for r in rows:
                    act.dma_start(gate[:, r, :], d["mod"][layer:layer + 1, r, 2 * DM:3 * DM].to_broadcast([P, DM])).then_inc(rows_ready, 16)
                act.dma_start(g_row[:], d["ln_g"][layer:layer + 1, :].to_broadcast([P, DM])).then_inc(rows_ready, 16)
                act.dma_start(b_row[:], d["ln_b"][layer:layer + 1, :].to_broadcast([P, DM])).then_inc(rows_ready, 16)
                split.start_scalar(act)
                for g in range(2):
                    split.ahead_scalar(act, g, g, g == 1)
                for t in range(n):
                    act.wait_ge(var_ready, t + 1)
                    nc.scalar.activation(rstd[:], mv[:, 1:2], ACT.Sqrt, bias=core.eps[:, 0:1]).then_inc(std_ready, 1)

            @block.vector
            def _(dve):
                chain = Chain(dve, steps)
                split.start_vector(dve)
                dve.wait_ge(rows_ready, 16 * (2 + len(rows)))
                for s in range(2):
                    split.ahead_vector(dve, s, s, s == 1)
                    for t in range(n):
                        x, r = xs[t]
                        cols = slice(s * NW, (s + 1) * NW)
                        dve.wait_ge(mm_done, s * n + t + 1)
                        chain.run(nc.vector.tensor_tensor(tmp[:], ps[s][t][:], gate[:, r, cols], ALU.mult))
                        chain.run(nc.vector.scalar_tensor_tensor(out=x[:, cols], in0=x[:, cols], scalar=ALPHA, in1=tmp[:], op0=ALU.mult, op1=ALU.add))
                for t in range(n):
                    def rstd_of(t=t):
                        dve.sem_inc(var_ready, 1)
                        dve.wait_ge(std_ready, t + 1)
                    layer_norm_tile(core, chain, rstd_of, t, xs[t][0], stats, mv, rstd, g_row, b_row)


SG = 16
SN = E // SG
SS = 64
CH = 8
LC, CC = NL // CH, NC // CH
GD = 2 * SN
BG = 4
BD = 2 * BG
NB = SN // BG
TWO_PI = 6.283185307179586
TP1 = 6.28125
TP2 = float(np.float32(np.floor((TWO_PI - TP1) * 2 ** 20) / 2 ** 20))
TP3 = float(TWO_PI - TP1 - TP2)
ROUND = 12582912.0
PI_BELOW = 3.1415925


def s5_projection(core, hT, ptab, qtab, a8):
    nc, d = core.nc, core.d
    with phase(core, "s5in") as ph:
        u = ph.sb("u", [P, TT, E])
        ps = [[ph.ps(f"ps{s}{t}", [P, NW]) for t in range(TT)] for s in range(2)]
        mm_done, act_free, dve_free, stored, tables = [ph.sem(x) for x in ("mm_done", "act_free", "dve_free", "stored", "tables")]
        G = E // NW
        split = Split(core, ph, G, 1, TT, mm_done, src=hT)
        with ph.block() as block:
            @block.sync
            def _(sp):
                split.loads(sp, d["s5_w_in"])
                for dst, src in ((ptab, "ptab"), (qtab, "qtab"), (a8, "a8")):
                    sp.dma_start(dst[:], d[src]).then_inc(tables, 16)
                for g in range(G):
                    sp.wait_ge(act_free, 3 + 2 * (g + 1))
                    sp.wait_ge(dve_free, 3 + 2 * (g + 1))
                    cols = slice(g * NW, (g + 1) * NW)
                    sp.dma_start(d["u"].rearrange("(t p) n -> p t n", p=P)[:, :, cols], u[:, :, cols]).then_inc(stored, 16)
                sp.wait_ge(stored, 16 * G)
                sp.wait_ge(tables, 48)

            @block.tensor
            def _(pe):
                split.products(pe, lambda s, t: ps[s][t][:], [(act_free, 2), (dve_free, 2)])

            @block.scalar
            def _(act):
                prime(act, act_free, 3)
                split.start_scalar(act)

                def empty(g, s):
                    for t in (2, 3):
                        act.wait_ge(mm_done, g * TT + t + 1)
                        nc.scalar.activation(u[:, t, bass.ts(g, NW)], ps[s][t][:], ACT.Copy).then_inc(act_free, 1)
                split.turns(act, split.ahead_scalar, empty)

            @block.vector
            def _(dve):
                prime(dve, dve_free, 3)
                split.start_vector(dve)

                def empty(g, s):
                    for t in range(LT):
                        dve.wait_ge(mm_done, g * TT + t + 1)
                        dve_copy(nc, u[:, t, bass.ts(g, NW)], ps[s][t][:]).then_inc(dve_free, 1)
                split.turns(dve, split.ahead_vector, empty)


def s5_tables(core, ph, ptab, qtab, a8):
    nc, d = core.nc, core.d
    names = "lr li dt er ei k ea r absr co si pr pi nr ni den sr si2 t1 t2 t3 t4".split()
    T = {n: ph.sb(n, [P, GD]) for n in names}
    V = lambda n: T[n][:]
    half_pi = ph.sb("half_pi", [P, 1])
    loads, steps, to_act, from_act = [ph.sem(x) for x in ("loads", "steps", "to_act", "from_act")]
    def on_scalar(act):
        act.dma_start(T["lr"][:], d["s5_lam_re"][:]).then_inc(loads, 16)
        act.dma_start(T["li"][:], d["s5_lam_im"][:]).then_inc(loads, 16)
        act.dma_start(T["dt"][:], d["s5_log_step"][:].to_broadcast([P, GD])).then_inc(loads, 16)
        act.wait_ge(loads, 48)
        nc.scalar.activation(V("dt"), V("dt"), ACT.Exp).then_inc(from_act, 1)
        act.wait_ge(to_act, 1)
        nc.scalar.activation(V("ea"), V("er"), ACT.Exp).then_inc(from_act, 1)
        act.wait_ge(to_act, 2)
        nc.scalar.activation(V("si"), V("r"), ACT.Sin)
        nc.scalar.activation(V("co"), V("absr"), ACT.Sin, scale=-1.0, bias=half_pi[:, 0:1]).then_inc(from_act, 1)

    def on_vector(dve):
        chain = Chain(dve, steps)
        v = nc.vector
        lo, hi = slice(0, SS), slice(SS, P)

        def mul(o, a, b):
            chain.run(v.tensor_tensor(o, a, b, ALU.mult))

        def add(o, a, b, op=ALU.add):
            chain.run(v.tensor_tensor(o, a, b, op))
        chain.run(v.memset(half_pi[:], TWO_PI / 4))
        dve.wait_ge(loads, 48)
        dve.wait_ge(from_act, 1)
        mul(V("er"), V("lr"), V("dt"))
        dve.sem_inc(to_act, 1)
        mul(V("ei"), V("li"), V("dt"))
        chain.run(v.tensor_scalar(V("k"), V("ei"), 1.0 / TWO_PI, ROUND, ALU.mult, ALU.add))
        chain.run(v.tensor_scalar(V("k"), V("k"), -ROUND, None, ALU.add))
        chain.run(v.scalar_tensor_tensor(out=V("r"), in0=V("k"), scalar=-TP1, in1=V("ei"), op0=ALU.mult, op1=ALU.add))
        for part in (TP2, TP3):
            chain.run(v.scalar_tensor_tensor(out=V("r"), in0=V("k"), scalar=-part, in1=V("r"), op0=ALU.mult, op1=ALU.add))
        chain.run(v.tensor_scalar(V("r"), V("r"), PI_BELOW, -PI_BELOW, ALU.min, ALU.max))
        chain.run(v.tensor_scalar(V("t1"), V("r"), -1.0, None, ALU.mult))
        add(V("absr"), V("r"), V("t1"), ALU.max)
        dve.sem_inc(to_act, 1)
        dve.wait_ge(from_act, 3)
        mul(V("co"), V("co"), V("ea"))
        mul(V("si"), V("si"), V("ea"))
        chain.run(v.tensor_scalar(V("nr"), V("co"), -1.0, None, ALU.add))
        mul(V("t1"), V("lr"), V("lr"))
        mul(V("t2"), V("li"), V("li"))
        add(V("den"), V("t1"), V("t2"))
        chain.run(v.reciprocal(V("den"), V("den")))
        mul(V("t1"), V("nr"), V("lr"))
        mul(V("t2"), V("si"), V("li"))
        add(V("sr"), V("t1"), V("t2"))
        mul(V("sr"), V("sr"), V("den"))
        mul(V("t1"), V("si"), V("lr"))
        mul(V("t2"), V("nr"), V("li"))
        add(V("si2"), V("t1"), V("t2"), ALU.subtract)
        mul(V("si2"), V("si2"), V("den"))
        v.memset(V("pr"), 1.0)
        chain.run(v.memset(V("pi"), 0.0))
        by_dir = lambda ap: ap.rearrange("p (g r) -> p g r", r=2)
        for n in range(CH + 1):
            for r in range(2):
                k = n if r == 0 else CH - n
                dst_r = ptab[:, :, 0, k].rearrange("p (g r) -> p g r", r=2)[:, :, r]
                dst_i = ptab[:, :, 1, k].rearrange("p (g r) -> p g r", r=2)[:, :, r]
                v.tensor_copy(dst_r[lo], by_dir(V("pr"))[lo, :, r])
                v.tensor_scalar(dst_r[hi], by_dir(V("pr"))[hi, :, r], -1.0, None, ALU.mult)
                v.tensor_scalar(dst_i, by_dir(V("pi"))[:, :, r], -1.0, None, ALU.mult)
            if n < CH:
                v.tensor_tensor(V("t1"), V("pr"), V("sr"), ALU.mult)
                mul(V("t2"), V("pi"), V("si2"))
                v.tensor_tensor(V("t1"), V("t1"), V("t2"), ALU.subtract)
                v.tensor_tensor(V("t3"), V("pr"), V("si2"), ALU.mult)
                mul(V("t4"), V("pi"), V("sr"))
                add(V("t3"), V("t3"), V("t4"))
                for r in range(2):
                    i = n if r == 0 else CH - 1 - n
                    dst_r = qtab[:, :, i].rearrange("p (g r) -> p g r", r=2)[:, :, r]
                    dst_i = qtab[:, :, CH + i].rearrange("p (g r) -> p g r", r=2)[:, :, r]
                    v.tensor_copy(dst_r, by_dir(V("t1"))[:, :, r])
                    v.tensor_scalar(dst_i[lo], by_dir(V("t3"))[lo, :, r], -1.0, None, ALU.mult)
                    last = v.tensor_copy(dst_i[hi], by_dir(V("t3"))[hi, :, r])
                chain.run(last)
                v.tensor_tensor(V("t1"), V("pr"), V("co"), ALU.mult)
                v.tensor_tensor(V("t2"), V("pi"), V("si"), ALU.mult)
                v.tensor_tensor(V("t3"), V("pr"), V("si"), ALU.mult)
                mul(V("t4"), V("pi"), V("co"))
                v.tensor_tensor(V("pr"), V("t1"), V("t2"), ALU.subtract)
                add(V("pi"), V("t3"), V("t4"))
        v.tensor_copy(a8[:, 0, :], V("pr"))
        v.tensor_copy(a8[lo, 1, :], T["pi"][lo])
        chain.run(v.tensor_scalar(a8[hi, 1, :], T["pi"][hi], -1.0, None, ALU.mult))
    return on_scalar, on_vector


def s5_chunk_inputs(core, qtab, S, u8):
    nc, d = core.nc, core.d
    with phase(core, "s5a") as ph:
        def two(n, shape):
            return [ph.sb(f"{n}{s}", shape) for s in range(2)]
        bab = two("bab", [P, 2, BD, SG])
        uc = two("uc", [LC + CC, CH, BG * SG])
        uo = two("uo", [LC + CC, BG, P])
        ub = two("ub", [P, BG, LC + CC])
        w = two("w", [P, BD, P])
        wT = two("wT", [P, BD, P])
        parts = [[core.ring[:, s, m * BD * P:(m + 1) * BD * P].rearrange("p (g w) -> p g w", g=BD) for m in range(2)] for s in range(2)]
        ps_u = [ph.ps(f"ps_u{s}", [P, BG, LC + CC]) for s in range(2)]
        ps_w = [[ph.ps(f"ps_w{s}{i}", [P, BG, P]) for i in range(2)] for s in range(2)]
        ps_s = [ph.ps(f"ps_s{i}", [P, BD, LC + CC]) for i in range(2)]
        names = "t1_made t2_made w_made turned u_ordered ub_ready wT_ready s_made s_kept u_kept passed".split()
        t1_made, t2_made, w_made, turned, u_ordered, ub_ready, wT_ready, s_made, s_kept, u_kept, passed = [ph.sem(n) for n in names]
        b_landed, u_landed = [[ph.sem(f"{n}{s}") for s in range(2)] for n in ("b_landed", "u_landed")]
        cols = lambda b: bass.ts(b, BD)
        ident = core.ident
        spread_q = lambda b, part: qtab[:, cols(b), part * CH:(part + 1) * CH].unsqueeze(3).to_broadcast([P, BD, CH, SG])
        spread_b = lambda s, part: bab[s][:, part].unsqueeze(2).to_broadcast([P, BD, CH, SG])
        by_token = lambda m: m.rearrange("p g (i m) -> p g i m", i=CH)
        HB = NB // 2

        def steps(eng, step, lead):
            for b in range(-lead, 0):
                step(b, b % 2, None)
            with eng.Fori(0, HB - 1) as n:
                for s in range(2):
                    step(n * 2 + s, s, n)
            for b in (NB - 2, NB - 1):
                step(b, b % 2, HB - 1)

        def exists(b, shift):
            return not isinstance(b, int) or 0 <= b + shift < NB

        with ph.block() as block:
            @block.sync
            def _(sp):
                def loads(b, s):
                    sp.dma_start(bab[s][:], d["s5_bab"][b]).then_inc(b_landed[s], 16)
                    sp.dma_start(uc[s][:], d["u"].rearrange("(c i) n -> c i n", i=CH)[:, :, bass.ts(b, BG * SG)]).then_inc(u_landed[s], 16)
                for s in range(2):
                    loads(s, s)
                with sp.Fori(0, HB - 1) as n:
                    for s in range(2):
                        b = n * 2 + s
                        sp.wait_ge(t1_made, b + 1)
                        sp.wait_ge(t2_made, b + 1)
                        sp.wait_ge(u_ordered, b + 1)
                        loads(b + 2, s)
                sp.wait_ge(w_made, NB + 2)
                prefetch(core, sp, d["s5_w_z"])

            @block.gpsimd
            def _(pool):
                with pool.Fori(0, HB) as n:
                    for s in range(2):
                        b = n * 2 + s
                        pool.wait_ge(b_landed[s], n * 16 + 16)
                        pool.wait_ge(w_made, b + 1)
                        pool.sem_inc(passed, 1)
                        nc.gpsimd.tensor_tensor(by_token(parts[s][1]), spread_q(b, 1), spread_b(s, 1), ALU.mult).then_inc(t2_made, 1)

            @block.vector
            def _(dve):
                prime(dve, s_kept, 2)
                prime(dve, w_made, 2)
                lat, con = slice(0, LC), slice(LC, LC + CC)

                def weights(b, s, n):
                    dve.wait_ge(b_landed[s], n * 16 + 16)
                    dve.wait_ge(w_made, b + 1)
                    nc.vector.tensor_tensor(by_token(parts[s][0]), spread_q(b, 0), spread_b(s, 0), ALU.mult).then_inc(t1_made, 1)
                    dve.wait_ge(t1_made, b + 1)
                    dve.wait_ge(t2_made, b + 1)
                    dve.wait_ge(turned, b + 1)
                    dve.wait_ge(u_kept, b + 1)
                    nc.vector.tensor_tensor(w[s][:], parts[s][0], parts[s][1], ALU.add).then_inc(w_made, 1)

                def step(b, s, n):
                    if exists(b, 2):
                        weights(b + 2, s, 0 if n is None else n + 1)
                    if exists(b, 0):
                        dve.wait_ge(s_made, b + 3)
                        by_dir = lambda r, steps: S[:, steps, cols(b)].rearrange("p s (g r) -> p g s r", r=2)[:, :, :, r]
                        of_dir = lambda r, chunks: ps_s[s][:].rearrange("p (g r) c -> p g r c", r=2)[:, :, r, chunks]
                        dve_copy(nc, by_dir(0, slice(CC, CC + LC)), of_dir(0, lat))
                        nc.vector.tensor_copy(by_dir(0, slice(0, CC)), of_dir(0, con))
                        nc.vector.tensor_copy(by_dir(1, slice(CC, CC + LC)), of_dir(1, lat)[:, :, ::-1])
                        nc.vector.tensor_copy(by_dir(1, slice(0, CC)), of_dir(1, con)[:, :, ::-1]).then_inc(s_kept, 1)
                steps(dve, step, 2)

            @block.scalar
            def _(act):
                prime(act, ub_ready, 1)
                prime(act, wT_ready, 2)
                prime(act, u_kept, 2)

                def order(b, s, n):
                    act.wait_ge(u_landed[s], n * 16 + 16)
                    act.wait_ge(turned, b + 1)
                    nc.scalar.activation(uo[s][:].rearrange("c g (i m) -> c g i m", i=CH)[:, :, ::-1, :],
                                         uc[s][:].rearrange("c i (g m) -> c g i m", g=BG), ACT.Copy).then_inc(u_ordered, 1)

                def step(b, s, n):
                    if exists(b, 2):
                        order(b + 2, s, 0 if n is None else n + 1)
                    if exists(b, 1):
                        act.wait_ge(turned, b + 4)
                        act.wait_ge(s_made, b + 2)
                        for i in range(2):
                            nc.scalar.activation(wT[1 - s][:, i * BG:(i + 1) * BG, :], ps_w[1 - s][i][:], ACT.Copy)
                        nc.scalar.activation(ub[1 - s][:], ps_u[1 - s][:], ACT.Copy).then_inc(wT_ready, 1)
                        for r, i in ((0, 0), (1, CH - 1)):
                            last = nc.scalar.activation(qtab[:, cols(b + 1), :].rearrange("p (g r) m -> p g r m", r=2)[:, :, r, :],
                                                        w[1 - s][:].rearrange("p (g r) m -> p g r m", r=2)[:, :, r, i * SG:(i + 1) * SG], ACT.Copy)
                        act.wait_ge(wT_ready, b + 4)
                        nc.scalar.activation(u8[:, bass.ts(b + 1, BG), :], ub[1 - s][:, :, 0:LC], ACT.Copy).then_inc(u_kept, 1)
                steps(act, step, 2)

            @block.tensor
            def _(pe):
                prime(pe, s_made, 2)
                prime(pe, turned, 2)

                def step(b, s, n):
                    if exists(b, 1):
                        pe.wait_ge(w_made, b + 4)
                        pe.wait_ge(u_ordered, b + 2)
                        pe.wait_ge(wT_ready, b + 2)
                        for c in range(BD):
                            nc.tensor.transpose(ps_w[1 - s][c // BG][:, c % BG, :], w[1 - s][:, c, :], ident[:])
                        for g in range(BG):
                            last = nc.tensor.transpose(ps_u[1 - s][:, g, :], uo[1 - s][:, g, :], ident[0:LC + CC, 0:LC + CC])
                        last.then_inc(turned, 1)
                    if exists(b, 0):
                        pe.wait_ge(wT_ready, b + 3)
                        pe.wait_ge(s_kept, b + 1)
                        for c in range(BD):
                            last = nc.tensor.matmul(ps_s[s][:, c, :], wT[s][:, c, :], ub[s][:, c // 2, :], start=True, stop=True)
                        last.then_inc(s_made, 1)
                steps(pe, step, 2)


def s5_carry(core, a8, S, hT):
    nc, d = core.nc, core.d
    CUT = (0, 112, 224, GD)
    with phase(core, "s5c") as ph:
        t1, t2 = ph.sb("t1", [P, GD]), ph.sb("t2", [P, GD])
        zb = [ph.sb(f"zb{s}", [P, LT, NW]) for s in range(2)]
        ps = [[ph.ps(f"ps{s}{t}", [P, NW]) for t in range(LT)] for s in range(2)]
        carried, pool_steps, pool_passed, mm_done, z_made = [ph.sem(n) for n in "carried pool_steps pool_passed mm_done z_made".split()]
        stored = [ph.sem(f"stored{s}") for s in range(2)]
        lo, hi = slice(0, SS), slice(SS, P)
        STEPS = CC + LC - 2
        G = E // NW

        with ph.block() as block:
            @block.vector
            def _(dve):
                ops = nc.vector
                a, b = slice(CUT[0], CUT[1]), slice(CUT[1], CUT[2])
                WORK = 10
                ops.memset(t2[:, b], 0.0).then_inc(carried, WORK)
                with dve.Fori(0, STEPS) as j:
                    def at(place, turn=0):
                        return j * WORK + ((turn + 1) * WORK + place + 1)

                    def times(c):
                        return [lambda: ops.tensor_tensor(t1[:, c], a8[:, 0, c], S[:, j, c], ALU.mult).then_inc(carried, 1),
                                lambda: ops.tensor_tensor(t2[lo, c], a8[hi, 1, c], S[hi, j, c], ALU.mult).then_inc(carried, 1),
                                lambda: ops.tensor_tensor(t2[hi, c], a8[lo, 1, c], S[lo, j, c], ALU.mult).then_inc(carried, 1)]

                    def add(c, t, step):
                        ops.tensor_tensor(S[:, step, c], S[:, step, c], t[:, c], ALU.add).then_inc(carried, 1)
                    a1, a2, a3 = times(a)
                    b1, b2, b3 = times(b)
                    dve.wait_ge(carried, at(7, -1))
                    a1()
                    a2()
                    dve.wait_ge(carried, at(9, -1))
                    add(b, t2, j)
                    dve.wait_ge(carried, at(0))
                    add(a, t1, j + 1)
                    a3()
                    dve.wait_ge(carried, at(2))
                    b1()
                    b2()
                    dve.wait_ge(carried, at(4))
                    add(a, t2, j + 1)
                    dve.wait_ge(carried, at(5))
                    add(b, t1, j + 1)
                    b3()
                dve.wait_ge(carried, STEPS * WORK + WORK)
                ops.tensor_tensor(S[:, STEPS, b], S[:, STEPS, b], t2[:, b], ALU.add).then_inc(carried, 1)

            @block.gpsimd
            def _(pool):
                chain = Chain(pool, pool_steps, pool_passed)
                c, ops = slice(CUT[2], CUT[3]), nc.gpsimd
                with chain.loop(STEPS, 5) as j:
                    chain.run(ops.tensor_tensor(t1[:, c], a8[:, 0, c], S[:, j, c], ALU.mult))
                    chain.run(ops.tensor_tensor(t2[lo, c], a8[hi, 1, c], S[hi, j, c], ALU.mult))
                    chain.run(ops.tensor_tensor(t2[hi, c], a8[lo, 1, c], S[lo, j, c], ALU.mult))
                    chain.run(ops.tensor_tensor(t1[:, c], t1[:, c], t2[:, c], ALU.add))
                    chain.run(ops.tensor_tensor(S[:, j + 1, c], S[:, j + 1, c], t1[:, c], ALU.add))

            @block.sync
            def _(sp):
                stream_loads(core, sp, d["s5_w_z"], G, 1, LT, mm_done, None)
                for g in range(G):
                    sp.wait_ge(z_made, LT + 1 + (g + 1) * LT)
                    sp.dma_start(d["z"].rearrange("(t p) n -> p t n", p=P)[:, :, g * NW:(g + 1) * NW], zb[g % 2][:]).then_inc(stored[g % 2], 16)
                for s in range(2):
                    sp.wait_ge(stored[s], 16 * G // 2)

            @block.scalar
            def _(act):
                prime(act, z_made, LT + 1)
                for g in range(G):
                    if g >= 2:
                        act.wait_ge(stored[g % 2], 16 * (g // 2))
                    for t in range(LT):
                        act.wait_ge(mm_done, g * LT + t + 1)
                        nc.scalar.activation(zb[g % 2][:, t, :], ps[g % 2][t][:], ACT.Silu).then_inc(z_made, 1)

            @block.tensor
            def _(pe):
                stream_products(core, pe, G, 1, LT, lambda k, t: hT[:, k, t * P:(t + 1) * P],
                                lambda s, t: ps[s][t], mm_done, None, [(z_made, LT)])


def s5_outputs(core, ptab, bbar, S, u8, feed):
    nc, d = core.nc, core.d
    W9 = (CH + 1) * SG
    EW = (2 * CH - 1) * SG
    NV = 4
    with phase(core, "s5d") as ph:
        def two(n, shape):
            return [ph.sb(f"{n}{s}", shape) for s in range(2)]
        cab = [ph.sb(f"cab{s}", [P, 2, BD, SG]) for s in range(NV)]
        V = [ph.sb(f"V{s}", [P, BD, W9]) for s in range(NV)]
        bs, hs, us = two("bs", [P, BD, SG]), two("hs", [P, BD, LC]), two("us", [P, BG, LC])
        T = two("T", [P, BG, P])
        yb = two("yb", [LC, CH, BG * SG])
        parts = [[core.ring[:, s, m * BD * W9:(m + 1) * BD * W9].rearrange("p (g m) -> p g m", g=BD) for m in range(2)] for s in range(2)]
        Em = [core.ring[0:SG, s, 2 * BD * W9:2 * BD * W9 + BG * EW].rearrange("p (g w) -> p g w", g=BG) for s in range(2)]
        ps_f = [ph.ps(f"ps_f{s}", [SG, BG, P]) for s in range(2)]
        ps_b = [ph.ps(f"ps_b{s}", [SG, BG, P]) for s in range(2)]
        ps_y = [ph.ps(f"ps_y{s}", [LC, BG, P]) for s in range(2)]
        lag0 = two("lag0", [SG, BG, SG])
        lag0_made, feed_in, feed_made = ph.sem("lag0_made"), ph.sem("feed_in"), ph.sem("feed_made")
        names = "v1_made v2_made V_made bs_ready hs_ready k_made e_back e_made y_made yb_made passed".split()
        v1_made, v2_made, V_made, bs_ready, hs_ready, k_made, e_back, e_made, y_made, yb_made, passed = [ph.sem(n) for n in names]
        c_landed = [ph.sem(f"c_landed{s}") for s in range(NV)]
        E_stored, T_landed, y_stored = [[ph.sem(f"{n}{s}") for s in range(2)] for n in ("E_stored", "T_landed", "y_stored")]
        cols = lambda b: bass.ts(b, BD)
        spread_p = lambda b, part: ptab[:, cols(b), part, :].unsqueeze(3).to_broadcast([P, BD, CH + 1, SG])
        spread_c = lambda k, part: cab[k][:, part].unsqueeze(2).to_broadcast([P, BD, CH + 1, SG])
        by_power = lambda m: m.rearrange("p g (i m) -> p g i m", i=CH + 1)
        lags_at = d["lags"]

        def windows(s):
            return bass.AP(tensor=lags_at.tensor, offset=lags_at.offset + s * SG * BG * EW, ap=[[SG, CH], [BG * EW, SG], [EW, BG], [1, P]])
        TURNS = NB // NV - 2

        def steps(eng, step):
            for b in (-2, -1):
                step(b, b % NV, -1)
            with eng.Fori(0, TURNS) as n:
                for k in range(NV):
                    step(n * NV + k, k, n)
            for b in range(NV * TURNS, NB):
                step(b, b % NV, b // NV)

        def nth(n, k):
            return n * 2 + k // 2

        def exists(b, shift):
            return not isinstance(b, int) or 0 <= b + shift < NB

        with ph.block() as block:
            @block.sync
            def _(sp):
                def load(b, k):
                    sp.dma_start(cab[k][:], d["s5_cab"][b]).then_inc(c_landed[k], 16)

                def step(b, k, n):
                    s = k % 2
                    if exists(b, 6):
                        sp.wait_ge(v1_made, b + 3)
                        sp.wait_ge(v2_made, b + 3)
                        load(b + 6, (k + 2) % NV)
                    if exists(b, 2):
                        sp.wait_ge(e_made, b + 5)
                        sp.dma_start(lags_at[s], Em[s]).then_inc(E_stored[s], 16)
                    if exists(b, 2):
                        sp.wait_ge(E_stored[s], nth(n, k + 2) * 16 + 16)
                        sp.wait_ge(y_made, b + 3)
                        sp.dma_start(T[s][:], windows(s)).then_inc(T_landed[s], 16)
                    if exists(b, 0):
                        sp.wait_ge(yb_made, b + 3)
                        sp.dma_start(d["y"].rearrange("(c t) n -> c t n", t=CH)[:, :, bass.ts(b, BG * SG)], yb[s][:]).then_inc(y_stored[s], 16)
                for k in range(NV):
                    load(k, k)
                for s in range(2):
                    sp.sem_inc(y_stored[s], 16)
                sp.dma_start(feed, d["s5_d"].to_broadcast([SG, E]).rearrange("m (g n) -> m g n", n=SG)).then_inc(feed_in, 16)
                steps(sp, step)
                for s in range(2):
                    sp.wait_ge(y_stored[s], 16 * (NB // 2 + 1))
                prefetch(core, sp, d["s5_glu_w"])

            @block.gpsimd
            def _(pool):
                pool.wait_ge(feed_in, 16)
                nc.gpsimd.tensor_tensor(feed, feed, core.ident[0:SG, 0:SG].unsqueeze(1).to_broadcast([SG, SN, SG]), ALU.mult).then_inc(feed_made, 1)
                with pool.Fori(0, NB // NV) as n:
                    for k in range(NV):
                        b, s = n * NV + k, k % 2
                        pool.wait_ge(c_landed[k], n * 16 + 16)
                        pool.wait_ge(V_made, b + 1)
                        pool.sem_inc(passed, 1)
                        nc.gpsimd.tensor_tensor(by_power(parts[s][1]), spread_p(b, 1), spread_c(k, 1), ALU.mult).then_inc(v2_made, 1)

            @block.vector
            def _(dve):
                prime(dve, V_made, 2)
                prime(dve, e_made, 2)

                def make_v(b, k, n):
                    s = k % 2
                    dve.wait_ge(c_landed[k % NV], (n + k // NV) * 16 + 16)
                    dve.wait_ge(V_made, b + 1)
                    nc.vector.tensor_tensor(by_power(parts[s][0]), spread_p(b, 0), spread_c(k % NV, 0), ALU.mult).then_inc(v1_made, 1)
                    dve.wait_ge(v1_made, b + 1)
                    dve.wait_ge(v2_made, b + 1)
                    if not isinstance(b, int) or b >= NV:
                        dve.wait_ge(y_made, b - 1)
                    nc.vector.tensor_tensor(V[k % NV][:], parts[s][0], parts[s][1], ALU.add).then_inc(V_made, 1)

                def step(b, k, n):
                    if exists(b, 3):
                        make_v(b + 3, k + 3, n)
                    if exists(b, 2):
                        s = k % 2
                        dve.wait_ge(k_made, b + 3)
                        dve.wait_ge(e_back, b + 3)
                        mid = Em[s][:, :, EW // 2 - SG // 2:EW // 2 + SG // 2]
                        nc.vector.tensor_tensor(lag0[s][:], ps_f[s][:, :, 0:SG], feed[:, bass.ts(b + 2, BG), :], ALU.add).then_inc(lag0_made, 1)
                        nc.vector.tensor_copy(Em[s][:, :, P:EW], ps_f[s][:, :, SG:P])
                        dve.wait_ge(lag0_made, b + 3)
                        nc.vector.tensor_tensor(mid, mid, lag0[s][:], ALU.add).then_inc(e_made, 1)
                make_v(0, 0, 0)
                dve.wait_ge(feed_made, 1)
                steps(dve, step)

            @block.scalar
            def _(act):
                def copy_bbar(b, s):
                    if not isinstance(b, int) or b >= 2:
                        act.wait_ge(k_made, b - 1)
                    nc.scalar.activation(bs[s][:], bbar[:, cols(b), :], ACT.Copy).then_inc(bs_ready, 1)

                def copy_states(b, s):
                    act.wait_ge(y_made, b + 1)
                    back = S[:, CC - 1:CC + LC - 1, cols(b)].rearrange("p c (g r) -> p g r c", r=2)
                    hd = hs[s][:].rearrange("p (g r) c -> p g r c", r=2)
                    nc.scalar.activation(hd[:, :, 0, :], back[:, :, 0, :], ACT.Copy)
                    nc.scalar.activation(hd[:, :, 1, ::-1], back[:, :, 1, :], ACT.Copy)
                    nc.scalar.activation(us[s][:], u8[:, bass.ts(b, BG), :], ACT.Copy).then_inc(hs_ready, 1)

                def step(b, k, n):
                    s = k % 2
                    if exists(b, 3):
                        copy_bbar(b + 3, 1 - s)
                    if exists(b, 1):
                        copy_states(b + 1, 1 - s)
                    if exists(b, 2):
                        act.wait_ge(k_made, b + 3)
                        act.wait_ge(E_stored[s], nth(n, k + 2) * 16)
                        nc.scalar.activation(Em[s][:, :, 0:P], ps_b[s][:], ACT.Copy).then_inc(e_back, 1)
                    if exists(b, 0):
                        act.wait_ge(y_made, b + 3)
                        act.wait_ge(y_stored[s], nth(n, k) * 16 + 16)
                        nc.scalar.activation(yb[s][:].rearrange("c t (g n) -> c g t n", g=BG),
                                             ps_y[s][:].rearrange("c g (t n) -> c g t n", t=CH), ACT.Copy).then_inc(yb_made, 1)
                prime(act, yb_made, 2)
                copy_bbar(0, 0)
                steps(act, step)

            @block.tensor
            def _(pe):
                prime(pe, y_made, 2)

                def step(b, k, n):
                    s = k % 2
                    if exists(b, 2):
                        v = V[(k + 2) % NV]
                        pe.wait_ge(V_made, b + 5)
                        pe.wait_ge(bs_ready, b + 3)
                        pe.wait_ge(e_made, b + 3)
                        for g in range(BG):
                            nc.tensor.matmul(ps_f[s][:, g, :], bs[s][:, 2 * g, :], v[:, 2 * g, 0:P], start=True, stop=True)
                            last = nc.tensor.matmul(ps_b[s][:, g, :], bs[s][:, 2 * g + 1, :], v[:, 2 * g + 1, SG:W9], start=True, stop=True)
                        last.then_inc(k_made, 1)
                    if exists(b, 0):
                        v = V[k % NV]
                        pe.wait_ge(T_landed[s], nth(n, k) * 16 + 16)
                        pe.wait_ge(hs_ready, b + 1)
                        pe.wait_ge(yb_made, b + 1)
                        for g in range(BG):
                            nc.tensor.matmul(ps_y[s][:, g, :], hs[s][:, 2 * g, :], v[:, 2 * g, SG:W9], start=True, stop=False)
                            nc.tensor.matmul(ps_y[s][:, g, :], hs[s][:, 2 * g + 1, :], v[:, 2 * g + 1, 0:P], start=False, stop=False)
                            last = nc.tensor.matmul(ps_y[s][:, g, :], us[s][:, g, :], T[s][:, g, :], start=False, stop=True)
                        last.then_inc(y_made, 1)
                steps(pe, step)


def turn_tiles(pe, nc, src, bank, ident, tiles, turned, freed):
    for f in range(tiles):
        if f >= 2:
            pe.wait_ge(freed, f - 1)
        for t in range(LT):
            last = nc.tensor.transpose(bank(f)[:, t * P:(t + 1) * P], src(t, f), ident)
        last.then_inc(turned, 1)


def s5_gate(core, yzT):
    nc, d = core.nc, core.d
    with phase(core, "glu") as ph:
        y = ph.sb("y", [P, LT, E])
        z = ph.sb("z", [P, LT, E])
        bias = ph.sb("bias", [P, E])
        gT = ph.sb("gT", [P, ET, NL])
        sg = ph.sb("sg", [P, 2, LT, NW])
        ps = [[ph.ps(f"ps{s}{t}", [P, NW]) for t in range(LT)] for s in range(2)]
        ps_t = [ph.ps(f"ps_t{s}", [P, NL]) for s in range(2)]
        names = "loads gates_in g_done g_turned gT_done mm_done biased sig yz_done yz_turned yzT_done steps".split()
        (loads, gates_in, g_done, g_turned, gT_done, mm_done, biased, sig, yz_done, yz_turned,
         yzT_done, steps) = [ph.sem(n) for n in names]
        G = E // NW
        split = Split(core, ph, G, 2, LT, mm_done, src=gT)
        with ph.block() as block:
            @block.sync
            def _(sp):
                sp.dma_start(y[:], d["y"].rearrange("(t p) n -> p t n", p=P)).then_inc(loads, 16)
                sp.dma_start(bias[:], d["s5_glu_b"].to_broadcast([P, E])).then_inc(gates_in, 16)
                sp.dma_start(z[:], d["z"].rearrange("(t p) n -> p t n", p=P)).then_inc(gates_in, 16)
                split.loads(sp, d["s5_glu_w"])
                split.following(sp, d["w_out1"])

            @block.vector
            def _(dve):
                chain = Chain(dve, steps)
                prime(dve, biased, LT + 1)

                def gate(g, s):
                    cols = bass.ts(g, NW)
                    for t in range(LT):
                        dve.wait_ge(mm_done, g * LT + t + 1)
                        nc.vector.tensor_tensor(sg[:, s, t, :], ps[s][t][:], bias[:, cols], ALU.add).then_inc(biased, 1)
                    for t in range(LT):
                        dve.wait_ge(sig, g * LT + t + 1)
                        chain.run(nc.vector.tensor_tensor(sg[:, s, t, :], sg[:, s, t, :], y[:, t, cols], ALU.mult))
                        nc.vector.tensor_tensor(y[:, t, cols], sg[:, s, t, :], z[:, t, cols], ALU.mult).then_inc(yz_done, 1)
                dve.wait_ge(gT_done, ET)
                split.start_vector(dve)
                dve.wait_ge(gates_in, 32)
                dve.wait_ge(g_done, LT)
                for g in range(G):
                    split.ahead_vector(dve, g, g % 2, g == G - 1)
                    gate(g, g % 2)

            @block.scalar
            def _(act):
                for f in range(ET):
                    act.wait_ge(g_turned, f + 1)
                    nc.scalar.activation(gT[:, f, :], ps_t[f % 2][:], ACT.Gelu_apprx_tanh).then_inc(gT_done, 1)

                def sigmoid(g, s):
                    for t in range(LT):
                        act.wait_ge(biased, g * LT + t + LT + 2)
                        nc.scalar.activation(sg[:, s, t, :], sg[:, s, t, :], ACT.Sigmoid).then_inc(sig, 1)
                act.wait_ge(gT_done, ET)
                split.start_scalar(act)
                for t in range(LT):
                    nc.scalar.activation(y[:, t, :], y[:, t, :], ACT.Gelu_apprx_tanh).then_inc(g_done, 1)
                split.turns(act, split.ahead_scalar, sigmoid)
                for f in range(ET):
                    act.wait_ge(yz_turned, f + 1)
                    nc.scalar.activation(yzT[:, f, :], ps_t[f % 2][:], ACT.Copy).then_inc(yzT_done, 1)

            @block.tensor
            def _(pe):
                pe.wait_ge(loads, 16)
                turn_tiles(pe, nc, lambda t, f: y[:, t, f * P:(f + 1) * P], lambda f: ps_t[f % 2], core.ident[:], ET, g_turned, gT_done)
                pe.wait_ge(gT_done, ET)
                split.products(pe, lambda s, t: ps[s][t][:], [(biased, LT)])
                pe.wait_ge(yz_done, G * LT)
                turn_tiles(pe, nc, lambda t, f: y[:, t, f * P:(f + 1) * P], lambda f: ps_t[f % 2], core.ident[:], ET, yz_turned, yzT_done)


AW = 512
AG, AGD = 8, 64
BH, BHD = 8, 64
BW = BH * BHD
EV_IN = 2 * AW + 3 * BW
CHD, CDK, CDV = 4, 128, 256
CR = 16
CTAU = 16.0
CCH = 64
CONV = 3
CK, CV = CHD * CDK, CHD * CDV
FF = 2816
FT = FF // P


def rms_transposes(core, name, g_cols, hT):
    nc, d = core.nc, core.d
    with phase(core, name) as ph:
        xn = ph.sb("xn", [P, LT, DM])
        g = ph.sb("g", [P, KT])
        ms = ph.sb("ms", [P, LT])
        rs = ph.sb("rs", [P, LT])
        ps = [ph.ps(f"ps{b}", [P, NL]) for b in range(4)]
        loaded, squared, std_ready, steps, xn_ready, turned, freed = [ph.sem(n) for n in "loaded squared std_ready steps xn_ready turned freed".split()]
        with ph.block() as block:
            @block.scalar
            def _(act):
                act.dma_start(g[:], g_cols).then_inc(loaded, 16)
                for t in range(LT):
                    last = nc.scalar.activation(xn[:, t, :], core.x[:, t, :], ACT.Square, accum_out=ms[:, t:t + 1])
                last.then_inc(squared, 1)
                act.wait_ge(squared, 1)
                nc.scalar.activation(rs[:], ms[:], ACT.Sqrt, scale=1.0 / DM, bias=core.eps[:, 1:2]).then_inc(std_ready, 1)

            @block.vector
            def _(dve):
                chain = Chain(dve, steps)
                dve.wait_ge(std_ready, 1)
                chain.run(nc.vector.reciprocal(rs[:], rs[:]))
                for t in range(LT):
                    nc.vector.tensor_scalar(xn[:, t, :], core.x[:, t, :], rs[:, t:t + 1], None, ALU.mult).then_inc(xn_ready, 1)
                dve.wait_ge(loaded, 16)
                for k in range(KT):
                    dve.wait_ge(turned, k + 1)
                    nc.vector.tensor_scalar(hT[:, k, :], ps[k % 4][:], g[:, k:k + 1], None, ALU.mult).then_inc(freed, 1)

            @block.tensor
            def _(pe):
                pe.wait_ge(xn_ready, LT)
                for k in range(KT):
                    if k >= 4:
                        pe.wait_ge(freed, k - 3)
                    for t in range(LT):
                        last = nc.tensor.transpose(ps[k % 4][:, t * P:(t + 1) * P], xn[:, t, k * P:(k + 1) * P], core.ident[:])
                    last.then_inc(turned, 1)


def project(core, name, weights, tiles, hT, dst, funcs, following, extra=None):
    nc, d = core.nc, core.d
    with phase(core, name) as ph:
        ps = [[ph.ps(f"ps{s}{t}", [P, NW]) for t in range(LT)] for s in range(2)]
        mm_done, freed = ph.sem("mm_done"), ph.sem("freed")
        if extra:
            xw = ph.sb("xw", [P, KT, CR])
            xl, xd, xm = ph.sem("xl"), ph.sem("xd"), ph.sem("xm")
            ps_x = ph.ps("ps_x", [CR, NL])
        split = Split(core, ph, tiles, 1, LT, mm_done, src=hT)
        with ph.block() as block:
            @block.sync
            def _(sp):
                if extra:
                    sp.dma_start(xw[:], extra[0]).then_inc(xl, 16)
                split.loads(sp, d[weights])
                split.following(sp, d[following])

            @block.vector
            def _(dve):
                split.start_vector(dve)
                split.turns(dve, split.ahead_vector, lambda g, s: None)

            @block.tensor
            def _(pe):
                split.products(pe, lambda s, t: ps[s][t][:], [(freed, LT)])
                if extra:
                    pe.wait_ge(xl, 16)
                    for k in range(KT):
                        last = nc.tensor.matmul(ps_x[:], xw[:, k, :], hT[:, k, :], start=k == 0, stop=k == KT - 1)
                    last.then_inc(xm, 1)

            @block.scalar
            def _(act):
                prime(act, freed, LT + 1)
                split.start_scalar(act)

                def empty(g, s, func):
                    split.ahead_scalar(act, g, s, isinstance(g, int) and g == tiles - 1)
                    for t in range(LT):
                        act.wait_ge(mm_done, g * LT + t + 1)
                        nc.scalar.activation(dst[:, t, bass.ts(g, NW)], ps[s][t][:], func).then_inc(freed, 1)
                at = 0
                for func, n in funcs:
                    if n >= 4 and at % 2 == 0 and n % 2 == 0 and at + n < tiles:
                        with act.Fori(0, n // 2) as i:
                            for s in range(2):
                                empty(i * 2 + at + s, s, func)
                    else:
                        for g in range(at, at + n):
                            empty(g, g % 2, func)
                    at += n
                if extra:
                    act.wait_ge(xm, 1)
                    nc.scalar.activation(extra[1][:], ps_x[:], ACT.Copy).then_inc(xd, 1)


def project_residual(core, name, weights, mixT, following):
    nc, d = core.nc, core.d
    with phase(core, name) as ph:
        ps = [[ph.ps(f"ps{s}{t}", [P, NW]) for t in range(LT)] for s in range(2)]
        mm_done, added = ph.sem("mm_done"), ph.sem("added")
        split = Split(core, ph, 2, 1, LT, mm_done, src=mixT)
        with ph.block() as block:
            @block.sync
            def _(sp):
                split.following(sp, d[following])

            @block.scalar
            def _(act):
                split.start_scalar(act)
                split.turns(act, split.ahead_scalar, lambda g, s: None)

            @block.tensor
            def _(pe):
                split.products(pe, lambda s, t: ps[s][t][:], [])

            @block.vector
            def _(dve):
                split.start_vector(dve)
                for s in range(2):
                    split.ahead_vector(dve, s, s, s == 1)
                    for t in range(LT):
                        dve.wait_ge(mm_done, s * LT + t + 1)
                        x = core.x[:, t, s * NW:(s + 1) * NW]
                        nc.vector.tensor_tensor(x, x, ps[s][t][:], ALU.add).then_inc(added, 1)


def gated_mlp(core, zz, mixT):
    nc, d = core.nc, core.d
    with phase(core, "mlp") as ph:
        g_row, b_row = ph.sb("g_row", [P, AW]), ph.sb("b_row", [P, AW])
        wsT = ph.sb("wsT", [P, AG, P])
        bsT = ph.sb("bsT", [P, AG])
        stats, mv, rstd = ph.sb("stats", [P, 6]), ph.sb("mv", [P, 2]), ph.sb("rstd", [P, LT])
        tri = ph.sb("tri", [P, P])
        ps = [ph.ps(f"ps{t}", [P, AW]) for t in range(LT)]
        ps_t = [ph.ps(f"ps_t{s}", [P, NL]) for s in range(2)]
        loads, steps, var, std, vn, mixed, a_done, turned, freed, masked = [ph.sem(n) for n in "loads steps var std vn mixed a_done turned freed masked".split()]
        with ph.block() as block:
            @block.sync
            def _(sp):
                sp.dma_start(g_row[:], d["ev_a_ln_g"].to_broadcast([P, AW])).then_inc(loads, 16)
                sp.dma_start(b_row[:], d["ev_a_ln_b"].to_broadcast([P, AW])).then_inc(loads, 16)
                sp.dma_start(wsT[:], d["ev_a_wsT"]).then_inc(loads, 16)
                sp.dma_start(bsT[:], d["ev_a_bsT"]).then_inc(loads, 16)
                sp.dma_start(tri[:], d["causal"]).then_inc(loads, 16)

            @block.gpsimd
            def _(pool):
                pool.wait_ge(loads, 80)
                nc.gpsimd.tensor_tensor(wsT[:], wsT[:], tri[:].unsqueeze(1).to_broadcast([P, AG, P]), ALU.mult).then_inc(masked, 1)

            @block.vector
            def _(dve):
                chain = Chain(dve, steps)
                dve.wait_ge(loads, 80)
                for t in range(LT):
                    v = zz[:, t, AW:2 * AW]
                    chain.run(nc.vector.bn_stats(stats[:], v))
                    chain.run(nc.vector.bn_aggr(mv[:], stats[:]))
                    dve.sem_inc(var, 1)
                    dve.wait_ge(std, t + 1)
                    chain.run(nc.vector.reciprocal(rstd[:, t:t + 1], rstd[:, t:t + 1]))
                    chain.run(nc.vector.tensor_scalar(v, v, mv[:, 0:1], rstd[:, t:t + 1], ALU.subtract, ALU.mult))
                    chain.run(nc.vector.tensor_tensor(v, v, g_row[:], ALU.mult))
                    nc.vector.tensor_tensor(v, v, b_row[:], ALU.add).then_inc(vn, 1)
                for t in range(LT):
                    dve.wait_ge(mixed, t + 1)
                    for g in range(AG):
                        cols = slice(g * AGD, (g + 1) * AGD)
                        last = nc.vector.scalar_tensor_tensor(out=zz[:, t, cols], in0=ps[t][:, cols], scalar=bsT[:, g:g + 1], in1=zz[:, t, cols], op0=ALU.add, op1=ALU.mult)
                    last.then_inc(a_done, 1)

            @block.scalar
            def _(act):
                for t in range(LT):
                    act.wait_ge(var, t + 1)
                    nc.scalar.activation(rstd[:, t:t + 1], mv[:, 1:2], ACT.Sqrt, bias=core.eps[:, 1:2]).then_inc(std, 1)
                for f in range(AW // P):
                    act.wait_ge(turned, f + 1)
                    nc.scalar.activation(mixT[:, f, :], ps_t[f % 2][:], ACT.Copy).then_inc(freed, 1)

            @block.tensor
            def _(pe):
                pe.wait_ge(masked, 1)
                for t in range(LT):
                    pe.wait_ge(vn, t + 1)
                    for g in range(AG):
                        cols = slice(g * AGD, (g + 1) * AGD)
                        last = nc.tensor.matmul(ps[t][:, cols], wsT[:, g, :], zz[:, t, AW + g * AGD:AW + (g + 1) * AGD], start=True, stop=True)
                    last.then_inc(mixed, 1)
                pe.wait_ge(a_done, LT)
                turn_tiles(pe, nc, lambda t, f: zz[:, t, f * P:(f + 1) * P], lambda f: ps_t[f % 2], core.ident[:], AW // P, turned, freed)


def dilated_attention(core, zz, mixT):
    nc, d = core.nc, core.d
    Q0, K0, V0 = 2 * AW, 2 * AW + BW, 2 * AW + 2 * BW
    HP = BH // 2
    with phase(core, "dil") as ph:
        gq, gk = ph.sb("gq", [P, BHD]), ph.sb("gk", [P, BHD])
        sq = ph.sb("sq", [P, LT, 2 * BW])
        ms = ph.sb("ms", [P, LT, 2 * BH])
        rs = ph.sb("rs", [P, LT, 2 * BH])
        count, bar = ph.sb("count", [P, LT, NL]), ph.sb("bar", [P, LT, NL])
        qkT = ph.sb("qkT", [P, 2, HP, NL])
        s_sb, p_sb = ph.sb("s_sb", [P, 2, LT, NL]), ph.sb("p_sb", [P, 2, LT, NL])
        pT = ph.sb("pT", [P, 2, LT, NL])
        mx, den = ph.sb("mx", [P, 2, LT]), ph.sb("den", [P, 2, LT])
        b_out = ph.sb("b_out", [P, LT, BW])
        ps_t = [ph.ps(f"ps_t{i}", [P, 2, NL]) for i in range(2)]
        ps_s = [ph.ps(f"ps_s{i}", [P, LT, NL]) for i in range(2)]
        ps_p = [ph.ps(f"ps_p{i}", [P, LT, NL]) for i in range(2)]
        ps_y = ph.ps("ps_y", [P, LT, 2, BHD])
        names = "loads steps squared std normed turned qkT_done scores smax expd weighed p_turned pT_done y_done b_done b_turned freed".split()
        (loads, steps, squared, std, normed, turned, qkT_done, scores, smax, expd, weighed, p_turned, pT_done, y_done, b_done,
         b_turned, freed) = [ph.sem(n) for n in names]
        SC = BHD ** -0.5
        with ph.block() as block:
            @block.sync
            def _(sp):
                sp.dma_start(gq[:], d["ev_q_g"].to_broadcast([P, BHD])).then_inc(loads, 16)
                sp.dma_start(gk[:], d["ev_k_g"].to_broadcast([P, BHD])).then_inc(loads, 16)
                sp.dma_start(count[:], d["branch_count"]).then_inc(loads, 16)
                sp.dma_start(bar[:], d["branch_bar"]).then_inc(loads, 16)

            @block.vector
            def _(dve):
                chain = Chain(dve, steps)
                dve.wait_ge(loads, 64)
                chain.run(nc.vector.tensor_tensor(sq[:], zz[:, :, Q0:V0], zz[:, :, Q0:V0], ALU.mult))
                chain.run(nc.vector.tensor_reduce(ms[:], sq[:].rearrange("p t (h w) -> p t h w", w=BHD), AX, ALU.add))
                dve.sem_inc(squared, 1)
                dve.wait_ge(std, 1)
                chain.run(nc.vector.reciprocal(rs[:], rs[:]))
                for t in range(LT):
                    for n, (c0, g) in enumerate(((Q0, gq), (K0, gk))):
                        blk = zz[:, t, c0:c0 + BW].rearrange("p (h w) -> p h w", w=BHD)
                        chain.run(nc.vector.tensor_tensor(blk, blk, rs[:, t, n * BH:(n + 1) * BH].unsqueeze(2).to_broadcast([P, BH, BHD]), ALU.mult))
                        nc.vector.tensor_tensor(blk, blk, g[:].unsqueeze(1).to_broadcast([P, BH, BHD]), ALU.mult).then_inc(normed, 1)
                for hp in range(HP):
                    for i in range(2):
                        dve.wait_ge(scores, hp * 2 + i + 1)
                        chain.run(nc.vector.scalar_tensor_tensor(out=s_sb[:, i], in0=ps_s[i][:], scalar=SC, in1=bar[:], op0=ALU.mult, op1=ALU.add))
                        chain.run(nc.vector.tensor_reduce(mx[:, i], s_sb[:, i], AX, ALU.max))
                        nc.vector.tensor_scalar(mx[:, i], mx[:, i], -1.0, None, ALU.mult).then_inc(smax, 1)
                    for i in range(2):
                        dve.wait_ge(expd, hp * 2 + i + 1)
                        chain.run(nc.vector.tensor_tensor(p_sb[:, i], p_sb[:, i], count[:], ALU.mult))
                        dve.sem_inc(weighed, 1)
                        chain.run(nc.vector.tensor_reduce(den[:, i], p_sb[:, i], AX, ALU.add))
                    chain.run(nc.vector.reciprocal(den[:], den[:]))
                    dve.wait_ge(y_done, hp + 1)
                    for i in range(2):
                        for t in range(LT):
                            last = nc.vector.tensor_scalar(b_out[:, t, (2 * hp + i) * BHD:(2 * hp + i + 1) * BHD], ps_y[:, t, i, :], den[:, i, t:t + 1], None, ALU.mult)
                    last.then_inc(b_done, 1)

            @block.scalar
            def _(act):
                act.wait_ge(squared, 1)
                nc.scalar.activation(rs[:], ms[:], ACT.Sqrt, scale=1.0 / BHD, bias=core.eps[:, 1:2]).then_inc(std, 1)
                for n in range(2):
                    for i in range(2):
                        act.wait_ge(turned, n * 2 + i + 1)
                        nc.scalar.activation(qkT[:, n, 2 * i:2 * i + 2, :], ps_t[i][:], ACT.Copy).then_inc(qkT_done, 1)
                for hp in range(HP):
                    for i in range(2):
                        act.wait_ge(smax, hp * 2 + i + 1)
                        if hp:
                            act.wait_ge(p_turned, (hp - 1) * 2 + i + 1)
                        for t in range(LT):
                            last = nc.scalar.activation(p_sb[:, i, t, :], s_sb[:, i, t, :], ACT.Exp, bias=mx[:, i, t:t + 1])
                        last.then_inc(expd, 1)
                    for i in range(2):
                        act.wait_ge(p_turned, hp * 2 + i + 1)
                        if hp:
                            act.wait_ge(y_done, hp)
                        nc.scalar.activation(pT[:, i], ps_p[i][:], ACT.Copy).then_inc(pT_done, 1)
                for f in range(BW // P):
                    act.wait_ge(b_turned, f + 1)
                    nc.scalar.activation(mixT[:, AW // P + f, :], ps_t[f % 2][:, 0, :], ACT.Copy).then_inc(freed, 1)

            @block.tensor
            def _(pe):
                pe.wait_ge(normed, 2 * LT)
                for n, c0 in enumerate((Q0, K0)):
                    for i in range(2):
                        if n:
                            pe.wait_ge(qkT_done, i + 1)
                        for j in range(2):
                            for t in range(LT):
                                hp = 2 * i + j
                                last = nc.tensor.transpose(ps_t[i][:, j, t * P:(t + 1) * P], zz[:, t, c0 + hp * P:c0 + (hp + 1) * P], core.ident[:])
                        last.then_inc(turned, 1)
                pe.wait_ge(qkT_done, 4)

                def make_scores(hp):
                    for i in range(2):
                        half = slice(i * BHD, (i + 1) * BHD)
                        if hp:
                            pe.wait_ge(smax, (hp - 1) * 2 + i + 1)
                        for t in range(LT):
                            last = nc.tensor.matmul(ps_s[i][:, t, :], qkT[half, 0, hp, t * P:(t + 1) * P], qkT[half, 1, hp, :], start=True, stop=True)
                        last.then_inc(scores, 1)
                make_scores(0)
                for hp in range(HP):
                    if hp + 1 < HP:
                        make_scores(hp + 1)
                    for i in range(2):
                        pe.wait_ge(weighed, hp * 2 + i + 1)
                        if hp:
                            pe.wait_ge(pT_done, (hp - 1) * 2 + i + 1)
                        for kt in range(LT):
                            for t in range(LT):
                                last = nc.tensor.transpose(ps_p[i][:, kt, t * P:(t + 1) * P], p_sb[:, i, t, kt * P:(kt + 1) * P], core.ident[:])
                        last.then_inc(p_turned, 1)
                    if hp:
                        pe.wait_ge(b_done, hp)
                    for i in range(2):
                        pe.wait_ge(pT_done, hp * 2 + i + 1)
                        h = 2 * hp + i
                        for t in range(LT):
                            for kt in range(LT):
                                last = nc.tensor.matmul(ps_y[:, t, i, :], pT[:, i, kt, t * P:(t + 1) * P], zz[:, kt, V0 + h * BHD:V0 + (h + 1) * BHD],
                                                        start=kt == 0, stop=kt == LT - 1)
                    last.then_inc(y_done, 1)
                pe.wait_ge(b_done, HP)
                turn_tiles(pe, nc, lambda t, f: b_out[:, t, f * P:(f + 1) * P], lambda f: ps_t[f % 2][:, 0, :], core.ident[:], BW // P, b_turned, freed)


def gla(core, zz, gaT, mixT):
    nc, d = core.nc, core.d
    K0, V0, R0 = CK, 2 * CK, 2 * CK + CV
    with phase(core, "gla") as ph:
        wa2, ba = ph.sb("wa2", [CR, CK]), ph.sb("ba", [P, CK])
        g_row = ph.sb("g_row", [P, CDV])
        sums, block_ones, ends = ph.sb("sums", [P, P]), ph.sb("block_ones", [P, P]), ph.sb("ends", [P, 2])
        la = ph.sb("la", [P, LT, CK])
        ex = ph.sb("ex", [P, LT, CK])
        tmp = ph.sb("tmp", [P, LT, CK])
        qt, kt_, ks = ph.sb("qt", [P, LT, CK]), ph.sb("kt", [P, LT, CK]), ph.sb("ks", [P, LT, CK])
        qT, kT = ph.sb("qT", [P, CHD, NL]), ph.sb("kT", [P, CHD, NL])
        att = ph.sb("att", [P, 2, LT, P])
        dec = ph.sb("dec", [P, CHD, LT, 2])
        st = ph.sb("st", [P, 2, 3, CDV])
        o = ph.sb("o", [P, LT, CV])
        ms, rs = ph.sb("ms", [P, LT, CHD]), ph.sb("rs", [P, LT, CHD])
        ps_b = [ph.ps(f"ps_b{t}", [P, CK]) for t in range(LT)]
        ps_l = [ph.ps(f"ps_l{t}", [P, CK]) for t in range(LT)]
        ps_a = [ph.ps(f"ps_a{t}", [P, LT, P]) for t in range(2)]
        ps_o = [ps_b[t][:, 0:CDV] for t in range(LT)]
        ps_kv = [ps_l[i][:, 0:CDV] for i in range(2)]
        ps_d = ph.ps("ps_d", [P, CHD, LT, 2])
        names = "loads steps ks_made ks_done gate_mm xs ex1 la_done cum dec_mm e0 e1 dec_done qk_done turned qkT_done att_mm att_done kv_mm st_done o_mm o_done sq_done std out_done o_turned freed".split()
        S = {n: ph.sem(n) for n in names}
        with ph.block() as block:
            @block.sync
            def _(sp):
                for dst, src in ((wa2[:], d["od_w_a2"]), (ba[:], d["od_b_a"].to_broadcast([P, CK])), (g_row[:], d["od_head_g"].to_broadcast([P, CDV])),
                                 (sums[:], d["chunk_sums"]), (block_ones[:], d["chunk_ones"]), (ends[:], d["chunk_ends"])):
                    sp.dma_start(dst, src).then_inc(S["loads"], 16)

            @block.tensor
            def _(pe):
                pe.wait_ge(S["loads"], 96)
                for t in range(LT):
                    nc.tensor.matmul(ps_b[t][:], gaT[:, t * P:(t + 1) * P], wa2[:], start=True, stop=True).then_inc(S["gate_mm"], 1)
                for t in range(LT):
                    pe.wait_ge(S["la_done"], t + 1)
                    nc.tensor.matmul(ps_b[t][:], sums[:], la[:, t, :], start=True, stop=True)
                    nc.tensor.matmul(ps_l[t][:], block_ones[:], la[:, t, :], start=True, stop=True).then_inc(S["cum"], 1)
                for t in range(LT):
                    for h in range(CHD):
                        last = nc.tensor.matmul(ps_d[:, h, t, :], la[:, t, h * CDK:(h + 1) * CDK], ends[:], start=True, stop=True)
                last.then_inc(S["dec_mm"], 1)
                pe.wait_ge(S["qk_done"], 1)
                for n, (src, bank) in enumerate(((qt, ps_b), (kt_, ps_l))):
                    for i in range(2):
                        for j in range(2):
                            for t in range(LT):
                                last = nc.tensor.transpose(bank[i][:, (j * LT + t) * P:(j * LT + t + 1) * P], src[:, t, (2 * i + j) * P:(2 * i + j + 1) * P], core.ident[:])
                        last.then_inc(S["turned"], 1)
                pe.wait_ge(S["qkT_done"], 4)
                pe.wait_ge(S["ks_done"], 1)
                for h in range(CHD):
                    a = h % 2
                    if h >= 2:
                        pe.wait_ge(S["att_done"], h - 1)
                    for t in range(LT):
                        last = nc.tensor.matmul(ps_a[a][:, t, :], kT[:, h, t * P:(t + 1) * P], qT[:, h, t * P:(t + 1) * P], start=True, stop=True)
                    last.then_inc(S["att_mm"], 1)
                    for c in range(3):
                        t, r = c // 2, slice((c % 2) * CCH, (c % 2 + 1) * CCH)
                        if h * 3 + c >= 2:
                            pe.wait_ge(S["st_done"], h * 3 + c - 1)
                        nc.tensor.matmul(ps_kv[(h * 3 + c) % 2], ks[r, t, h * CDK:(h + 1) * CDK], zz[r, t, V0 + h * CDV:V0 + (h + 1) * CDV],
                                         start=True, stop=True).then_inc(S["kv_mm"], 1)
                    pe.wait_ge(S["att_done"], h + 1)
                    pe.wait_ge(S["st_done"], h * 3 + 3)
                    if h:
                        pe.wait_ge(S["o_done"], h)
                    for t in range(LT):
                        vv = zz[:, t, V0 + h * CDV:V0 + (h + 1) * CDV]
                        last = nc.tensor.matmul(ps_o[t], att[:, a, t, :], vv, start=True, stop=True)
                        if t:
                            nc.tensor.matmul(ps_o[t][0:CCH], qT[:, h, 2 * CCH:3 * CCH], st[:, a, 1, :], start=False, stop=True, skip_group_check=True)
                        last = nc.tensor.matmul(ps_o[t][CCH:P], qT[:, h, (2 * t + 1) * CCH:(2 * t + 2) * CCH], st[:, a, 2 * t, :], start=False, stop=True, skip_group_check=True)
                    last.then_inc(S["o_mm"], 1)
                pe.wait_ge(S["out_done"], 1)
                turn_tiles(pe, nc, lambda t, f: o[:, t, f * P:(f + 1) * P], lambda f: ps_l[f % 2], core.ident[:], KT, S["o_turned"], S["freed"])

            @block.vector
            def _(dve):
                chain = Chain(dve, S["steps"])
                v = nc.vector
                dve.wait_ge(S["loads"], 96)
                for t in range(LT):
                    dve.wait_ge(S["gate_mm"], t + 1)
                    chain.run(v.tensor_tensor(la[:, t, :], ps_b[t][:], ba[:], ALU.add))
                    chain.run(v.tensor_scalar(ex[:, t, :], la[:, t, :], -1.0, None, ALU.mult))
                    chain.run(v.tensor_tensor(ex[:, t, :], ex[:, t, :], la[:, t, :], ALU.max))
                    dve.sem_inc(S["xs"], 1)
                for t in range(LT):
                    dve.wait_ge(S["ex1"], t + 1)
                    chain.run(v.tensor_scalar(la[:, t, :], la[:, t, :], 0.0, None, ALU.min))
                    chain.run(v.tensor_tensor(la[:, t, :], la[:, t, :], ex[:, t, :], ALU.subtract))
                    v.tensor_scalar(la[:, t, :], la[:, t, :], 1.0 / CTAU, None, ALU.mult).then_inc(S["la_done"], 1)
                for t in range(LT):
                    dve.wait_ge(S["e1"], 2 * t + 1)
                    chain.run(v.tensor_tensor(qt[:, t, :], zz[:, t, 0:CK], ex[:, t, :], ALU.mult))
                    chain.run(v.tensor_scalar(qt[:, t, :], qt[:, t, :], float(CDK) ** -0.5, None, ALU.mult))
                    dve.wait_ge(S["e1"], 2 * t + 2)
                    v.tensor_tensor(kt_[:, t, :], zz[:, t, K0:V0], tmp[:, t, :], ALU.mult)
                    chain.run(v.tensor_copy(ks[:, t, :], ps_b[t][:]))
                    chain.run(v.tensor_tensor(ks[:, t, :], ps_l[t][:], ks[:, t, :], ALU.subtract))
                dve.sem_inc(S["qk_done"], 1)
                for t in range(LT):
                    dve.wait_ge(S["ks_made"], t + 1)
                    chain.run(v.tensor_tensor(ks[:, t, :], zz[:, t, K0:V0], ks[:, t, :], ALU.mult))
                dve.sem_inc(S["ks_done"], 1)
                dve.wait_ge(S["dec_done"], 1)
                for h in range(CHD):
                    a = h % 2
                    dve.wait_ge(S["att_mm"], h + 1)
                    if h >= 2:
                        dve.wait_ge(S["o_mm"], h - 1)
                    chain.run(v.tensor_scalar(att[:, a], ps_a[a][:], 3.0e38, -3.0e38, ALU.min, ALU.max))
                    v.tensor_tensor(att[:, a], att[:, a], sums[:].unsqueeze(1).to_broadcast([P, LT, P]), ALU.mult).then_inc(S["att_done"], 1)
                    for c in range(3):
                        dve.wait_ge(S["kv_mm"], h * 3 + c + 1)
                        kv = ps_kv[(h * 3 + c) % 2]
                        if c == 0:
                            ins = v.tensor_copy(st[:, a, 0, :], kv)
                        else:
                            ins = v.scalar_tensor_tensor(out=st[:, a, c, :], in0=st[:, a, c - 1, :], scalar=dec[:, h, c // 2, c % 2:c % 2 + 1], in1=kv, op0=ALU.mult, op1=ALU.add)
                        ins.then_inc(S["st_done"], 1)
                        dve.wait_ge(S["st_done"], h * 3 + c + 1)
                    dve.wait_ge(S["o_mm"], h + 1)
                    for t in range(LT):
                        last = v.tensor_copy(o[:, t, h * CDV:(h + 1) * CDV], ps_o[t])
                    last.then_inc(S["o_done"], 1)
                dve.wait_ge(S["o_done"], CHD)
                for t in range(LT):
                    sq = zz[:, t, 0:CV]
                    chain.run(v.tensor_tensor(sq, o[:, t, :], o[:, t, :], ALU.mult))
                    chain.run(v.tensor_reduce(ms[:, t, :], sq.rearrange("p (h w) -> p h w", h=CHD), AX, ALU.add))
                dve.sem_inc(S["sq_done"], 1)
                dve.wait_ge(S["std"], 1)
                chain.run(v.reciprocal(rs[:], rs[:]))
                for t in range(LT):
                    ob = o[:, t, :].rearrange("p (h w) -> p h w", h=CHD)
                    chain.run(v.tensor_tensor(ob, ob, rs[:, t, :].unsqueeze(2).to_broadcast([P, CHD, CDV]), ALU.mult))
                    chain.run(v.tensor_tensor(ob, ob, g_row[:].unsqueeze(1).to_broadcast([P, CHD, CDV]), ALU.mult))
                    chain.run(v.tensor_tensor(o[:, t, :], o[:, t, :], zz[:, t, R0:R0 + CV], ALU.mult))
                dve.sem_inc(S["out_done"], 1)

            @block.scalar
            def _(act):
                sc = nc.scalar
                for t in range(LT):
                    act.wait_ge(S["xs"], t + 1)
                    sc.activation(ex[:, t, :], ex[:, t, :], ACT.Exp, scale=-1.0).then_inc(S["e0"], 1)
                    act.wait_ge(S["e0"], t + 1)
                    sc.activation(ex[:, t, :], ex[:, t, :], ACT.Ln, bias=1.0).then_inc(S["ex1"], 1)
                for t in range(LT):
                    act.wait_ge(S["cum"], t + 1)
                    sc.activation(ex[:, t, :], ps_b[t][:], ACT.Exp).then_inc(S["e1"], 1)
                    sc.activation(tmp[:, t, :], ps_b[t][:], ACT.Exp, scale=-1.0).then_inc(S["e1"], 1)
                act.wait_ge(S["dec_mm"], 1)
                sc.activation(dec[:], ps_d[:], ACT.Exp).then_inc(S["dec_done"], 1)
                act.wait_ge(S["qk_done"], 1)
                for t in range(LT):
                    sc.activation(ks[:, t, :], ks[:, t, :], ACT.Exp).then_inc(S["ks_made"], 1)
                for n, (dst, bank) in enumerate(((qT, ps_b), (kT, ps_l))):
                    for i in range(2):
                        act.wait_ge(S["turned"], n * 2 + i + 1)
                        sc.activation(dst[:, 2 * i:2 * i + 2, :], bank[i][:].rearrange("p (j w) -> p j w", j=2), ACT.Copy).then_inc(S["qkT_done"], 1)
                act.wait_ge(S["sq_done"], 1)
                sc.activation(rs[:], ms[:], ACT.Sqrt, scale=1.0 / CDV, bias=core.eps[:, 1:2]).then_inc(S["std"], 1)
                for f in range(KT):
                    act.wait_ge(S["o_turned"], f + 1)
                    sc.activation(mixT[:, f, :], ps_l[f % 2][:, 0:NL], ACT.Copy).then_inc(S["freed"], 1)


def conv_ffn(core, name, layer, hT, following):
    nc, d = core.nc, core.d
    with phase(core, name) as ph:
        wd = [ph.sb(f"wd{s}", [P, 2, DM]) for s in range(2)]
        a = [ph.sb(f"a{s}", [P, 2, NL]) for s in range(2)]
        c = [ph.sb(f"c{s}", [P, 2, NL]) for s in range(2)]
        cw, cb = ph.sb("cw", [P, FT, CONV]), ph.sb("cb", [P, FT])
        ps = [[ph.ps(f"ps{s}{f}", [P, 2, NL]) for f in range(2)] for s in range(2)]
        acc = [[ph.ps(f"acc{t}{n}", [P, NW]) for n in range(2)] for t in range(LT)]
        w_part = [ph.sb(n, [P, 2, KT, NL], F32R) for n in ("w_lead", "w_rest")]
        x_part = [ph.sb(n, [P, KT, NL], F32R) for n in ("x_lead", "x_rest")]
        wd_part = [[ph.sb(f"wd_{n}{s}", [P, 2, DM], F32R) for n in ("lead", "rest")] for s in range(2)]
        a_part = [[ph.sb(f"a_{n}{s}", [P, 2, NL], F32R) for n in ("lead", "rest")] for s in range(2)]
        names = "gate_used x_lead_made x_rest_made w_lead_made w_rest_made wd_lead_made wd_rest_made a_lead_made a_rest_made".split()
        gate_used, x_lead_made, x_rest_made, w_lead_made, w_rest_made, wd_lead_made, wd_rest_made, a_lead_made, a_rest_made = [ph.sem(n) for n in names]
        names = "loads gu_done conv_done silu_done a_made down_done steps added".split()
        loads, gu_done, conv_done, silu_done, a_made, down_done, steps, added = [ph.sem(n) for n in names]
        wd_landed = [ph.sem(f"wd_landed{s}") for s in range(2)]
        NU = FT // 2
        used = list(core.used)
        raw = lambda s, m: core.ring[:, s, :].rearrange("p (m k n) -> p m k n", m=2, k=KT)[:, m]
        HU = (NU - 3) // 2
        weights = d[f"ffn_gu{layer}"]
        down = d[f"ffn_down{layer}"]
        with ph.block() as block:
            @block.sync
            def _(sp):
                for s in range(2):
                    sp.dma_start(wd[s][:], down[s]).then_inc(wd_landed[s], 16)
                sp.dma_start(cw[:], d["ffn_conv_w"][layer]).then_inc(loads, 16)
                sp.dma_start(cb[:], d["ffn_conv_b"][layer]).then_inc(loads, 16)

                def turn(u, s):
                    sp.wait_ge(w_rest_made, u * 2 + 2)
                    core.load(sp, s, weights[u + 2])
                    sp.wait_ge(wd_rest_made, u + 1)
                    sp.dma_start(wd[s][:], down[u + 2]).then_inc(wd_landed[s], 16)
                with sp.Fori(0, (NU - 2) // 2) as i:
                    for s in range(2):
                        turn(i * 2 + s, s)
                for u in range((NU - 2) // 2 * 2, NU - 2):
                    turn(u, u % 2)
                sp.wait_ge(w_rest_made, 2 * NU)
                if following:
                    prefetch(core, sp, d[following])

            @block.tensor
            def _(pe):
                prime(pe, down_done, 2)

                passes = ((0, 0), (0, 1), (1, 0))
                pe.wait_ge(x_rest_made, 2)

                def gate_up(u, s):
                    pe.wait_ge(a_made, u + 1)
                    for m in range(2):
                        pe.wait_ge(w_rest_made, u * 2 + m + 1)
                        for f in range(2):
                            for k in range(KT):
                                for w, x in passes:
                                    last = nc.tensor.matmul(ps[s][f][:, m, :], w_part[w][:, m, k, f * P:(f + 1) * P], x_part[x][:, k, :],
                                                            start=(k, w, x) == (0, 0, 0), stop=(k, w) == (KT - 1, 1))
                        last.then_inc(gu_done if m else gate_used, 1)

                def down_product(u, s, first=False, final=False):
                    pe.wait_ge(a_rest_made, u + 1)
                    pe.wait_ge(wd_rest_made, u + 1)
                    for f in range(2):
                        for t in range(LT):
                            for x, w in passes:
                                for n in range(2):
                                    last = nc.tensor.matmul(acc[t][n][:], a_part[s][x][:, f, t * P:(t + 1) * P], wd_part[s][w][:, f, n * NW:(n + 1) * NW],
                                                            start=first and (f, x, w) == (0, 0, 0), stop=final and (f, x) == (1, 1))
                    last.then_inc(down_done, 1)
                gate_up(0, 0)
                gate_up(1, 1)
                down_product(0, 0, first=True)
                with pe.Fori(0, HU) as i:
                    gate_up(i * 2 + 2, 0)
                    down_product(i * 2 + 1, 1)
                    gate_up(i * 2 + 3, 1)
                    down_product(i * 2 + 2, 0)
                gate_up(NU - 1, 0)
                down_product(NU - 2, 1)
                down_product(NU - 1, 0, final=True)
                core.used[0] += NU // 2 + 1
                core.used[1] += NU // 2

            @block.scalar
            def _(act):
                def lead_w(u, s, m, first=False):
                    act.wait_ge(core.landed[s], u * 8 + (16 * (used[s] + 1) - 8 * s))
                    if not first:
                        act.wait_ge(gu_done if m else gate_used, u)
                    nc.scalar.activation(w_part[0][:, m], raw(s, m), ACT.Copy).then_inc(w_lead_made, 1)

                def unit(u, s, turn, final=False):
                    if not final:
                        for m in range(2):
                            lead_w(u + 1, 1 - s, m)
                    act.wait_ge(wd_landed[s], turn * 16 + 16)
                    act.wait_ge(down_done, u + 1)
                    nc.scalar.activation(wd_part[s][0][:], wd[s][:], ACT.Copy).then_inc(wd_lead_made, 1)
                    for f in range(2):
                        act.wait_ge(conv_done, u * 2 + f + 1)
                        nc.scalar.activation(c[s][:, f, :], c[s][:, f, :], ACT.Silu).then_inc(silu_done, 1)
                    act.wait_ge(a_made, u + 3)
                    nc.scalar.activation(a_part[s][0][:], a[s][:], ACT.Copy).then_inc(a_lead_made, 1)
                for h in range(2):
                    lead_w(0, 0, h, first=True)
                    ks = slice(h * HK, (h + 1) * HK)
                    nc.scalar.activation(x_part[0][:, ks], hT[:, ks], ACT.Copy).then_inc(x_lead_made, 1)
                with act.Fori(0, NU // 2) as i:
                    for s in range(2):
                        unit(i * 2 + s, s, i)
                unit(NU - 1, 0, NU // 2, final=True)

            @block.vector
            def _(dve):
                chain = Chain(dve, steps)
                v = nc.vector
                prime(dve, a_made, 2)

                def rest_w(u, s, m):
                    dve.wait_ge(w_lead_made, u * 2 + m + 1)
                    v.tensor_tensor(w_part[1][:, m], raw(s, m), w_part[0][:, m].bitcast(F32), ALU.subtract).then_inc(w_rest_made, 1)
                for h in range(2):
                    rest_w(0, 0, h)
                    ks = slice(h * HK, (h + 1) * HK)
                    dve.wait_ge(x_lead_made, h + 1)
                    v.tensor_tensor(x_part[1][:, ks], hT[:, ks], x_part[0][:, ks].bitcast(F32), ALU.subtract).then_inc(x_rest_made, 1)
                dve.wait_ge(loads, 32)

                def unit(u, s, final=False):
                    if not final:
                        for m in range(2):
                            rest_w(u + 1, 1 - s, m)
                    dve.wait_ge(wd_lead_made, u + 1)
                    v.tensor_tensor(wd_part[s][1][:], wd[s][:], wd_part[s][0][:].bitcast(F32), ALU.subtract).then_inc(wd_rest_made, 1)
                    dve.wait_ge(gu_done, u + 1)
                    dve.wait_ge(a_made, u + 1)
                    for f in range(2):
                        g, cf = ps[s][f][:, 0, :], c[s][:, f, :]
                        wk = lambda k: cw[:, bass.ds(u * 2 + f, 1), k]
                        chain.run(v.tensor_scalar(cf, g, wk(2), cb[:, bass.ds(u * 2 + f, 1)], ALU.mult, ALU.add))
                        chain.run(v.scalar_tensor_tensor(out=cf[:, 1:NL], in0=g[:, 0:NL - 1], scalar=wk(1), in1=cf[:, 1:NL], op0=ALU.mult, op1=ALU.add))
                        v.scalar_tensor_tensor(out=cf[:, 2:NL], in0=g[:, 0:NL - 2], scalar=wk(0), in1=cf[:, 2:NL], op0=ALU.mult, op1=ALU.add).then_inc(conv_done, 1)
                    dve.wait_ge(down_done, u + 1)
                    for f in range(2):
                        dve.wait_ge(silu_done, u * 2 + f + 1)
                        last = v.tensor_tensor(a[s][:, f, :], c[s][:, f, :], ps[s][f][:, 1, :], ALU.mult)
                    last.then_inc(a_made, 1)
                    dve.wait_ge(a_lead_made, u + 1)
                    v.tensor_tensor(a_part[s][1][:], a[s][:], a_part[s][0][:].bitcast(F32), ALU.subtract).then_inc(a_rest_made, 1)
                with chain.loop(NU // 2, 8) as i:
                    for s in range(2):
                        unit(i * 2 + s, s)
                unit(NU - 1, 0, final=True)
                dve.wait_ge(down_done, NU + 2)
                for t in range(LT):
                    for n in range(2):
                        x = core.x[:, t, n * NW:(n + 1) * NW]
                        v.tensor_tensor(x, x, acc[t][n][:], ALU.add).then_inc(added, 1)


def store(core, out):
    nc = core.nc
    with phase(core, "store") as ph:
        stored = ph.sem("stored")
        with ph.block() as block:
            @block.sync
            def _(sp):
                sp.dma_start(out.rearrange("a (t p) n -> p (a t) n", p=P), core.x[:]).then_inc(stored, 16)
                sp.wait_ge(stored, 16)


def build(nc, d, out, start=0):
    for name, shape in (("mod", [2, 2, 3 * DM]), ("u", [NTOK, E]), ("y", [NL, E]), ("z", [NL, E]), ("ptab", [P, GD, 2, CH + 1]),
                        ("qtab", [P, GD, 2 * CH]), ("a8", [P, 2, GD]), ("lags", [2, SG, BG, (2 * CH - 1) * SG])):
        d[name] = nc.dram_tensor(name + "_scratch", shape, F32, kind="Internal").ap()
    with ExitStack() as ctx:
        core = Core(nc, ctx, d)

        def within(stack, n, shape, dt=F32, side="left"):
            return stack.enter_context(nc.sbuf_tensor(n, shape, dt, side=side))
        latent = [(core.x[:, t, :], 0) for t in range(LT)]
        with ExitStack() as first:
            with ExitStack() as mem:
                xc = within(mem, "xc", [P, LT, DM])
                modulation(core, xc)
                context = [(xc[:, t, :], 1) for t in range(LT)]
                with ExitStack() as heads, ExitStack() as outputs:
                    q, z = [within(heads, n, [P, TT, E], side="right") for n in "qz"]
                    kn, v = [within(heads, n, [P, TT, KVW], side="right") for n in ("kn", "v")]
                    with ExitStack() as inner:
                        hparts = [within(inner, n, [P, KT, NTOK], F32R) for n in ("h_lead", "h_rest")]
                        modulated_transposes(core, "h0", 0, None, xc, hparts)
                        attention_projection(core, hparts, q, kn, v, z)
                    yzT = within(outputs, "yzT", [P, ET, NTOK])
                    with ExitStack() as inner:
                        kT, work = within(inner, "kT", [P, KVH, NTOK]), within(inner, "work", [P, KT, NTOK])
                        attention(core, q, kn, v, z, kT, work, yzT)
                    heads.close()
                    residual_norm(core, "out0", 0, "w_out0", TT, latent + context, yzT, "s5_w_in")
                hT = within(first, "hT", [P, KT, NTOK], side="right")
                modulated_transposes(core, "h1", 1, hT, xc)
            ptab, qtab = within(first, "ptab", [P, GD, 2, CH + 1]), within(first, "qtab", [P, GD, 2 * CH])
            a8 = within(first, "a8", [P, 2, GD])
            s5_projection(core, hT, ptab, qtab, a8)
            S, u8 = within(first, "S", [P, LC + CC, GD]), within(first, "u8", [P, SN, LC])
            s5_chunk_inputs(core, qtab, S, u8)
            s5_carry(core, a8, S, hT)
            s5_outputs(core, ptab, qtab, S, u8, hT[0:SG, 0:E // NTOK, :].rearrange("m k (g n) -> m (k g) n", n=SG))
        with ExitStack() as second:
            yzT = within(second, "yzT1", [P, ET, NL])
            s5_gate(core, yzT)
            residual_norm(core, "out1", 1, "w_out1", LT, latent, yzT, "ev_w_in")
        with ExitStack() as third:
            hT = within(third, "hT2", [P, KT, NL])
            mixT = within(third, "mixT", [P, KT, NL])
            with ExitStack() as mem:
                rms_transposes(core, "hm0", d["norm_mix_g"][0], hT)
                zz = within(mem, "zz0", [P, LT, EV_IN])
                project(core, "evin", "ev_w_in", EV_IN // NW, hT, zz, [(ACT.Gelu, 2), (ACT.Copy, 3)], "ev_w_out")
                gated_mlp(core, zz, mixT)
                dilated_attention(core, zz, mixT)
            project_residual(core, "evout", "ev_w_out", mixT, "ffn_gu0")
            rms_transposes(core, "hf0", d["norm_ffn_g"][0], hT)
            conv_ffn(core, "ffn0", 0, hT, "od_w_in")
            with ExitStack() as mem:
                rms_transposes(core, "hm1", d["norm_mix_g"][1], hT)
                zz, gaT = within(mem, "zz1", [P, LT, 2 * CK + 2 * CV]), within(mem, "gaT", [CR, NL])
                project(core, "odin", "od_w_in", (2 * CK + 2 * CV) // NW, hT, zz, [(ACT.Copy, 4), (ACT.Silu, 2)], "od_w_out",
                        extra=(d["od_w_ga"], gaT))
                gla(core, zz, gaT, mixT)
            project_residual(core, "odout", "od_w_out", mixT, "ffn_gu1")
            rms_transposes(core, "hf1", d["norm_ffn_g"][1], hT)
            conv_ffn(core, "ffn1", 1, hT, None)
            store(core, out)


def tiles_of(w, halves=1):
    k, n = w.shape
    a = w.reshape(halves, KT, P, n // NW, NW).transpose(3, 0, 2, 1, 4)
    return np.ascontiguousarray(a).reshape(n // NW * halves, P, KT * NW)


def constants():
    c = {"ident": np.eye(P, dtype=np.float32)}
    n = np.arange(NL, dtype=np.float32)
    row, col = np.floor(n / 64).astype(np.float32), (n % 64).astype(np.float32)
    inv = np.power(np.float32(10000.0), -np.arange(32, dtype=np.float32) / np.float32(32)).astype(np.float32)
    ar, ac = row[:, None] * inv, col[:, None] * inv
    cos = np.concatenate([np.cos(ar), np.cos(ar), np.cos(ac), np.cos(ac)], 1)
    sin = np.concatenate([-np.sin(ar), np.sin(ar), -np.sin(ac), np.sin(ac)], 1)
    lay = lambda a: np.ascontiguousarray(a.reshape(LT, P, P).transpose(1, 0, 2)).astype(np.float32)
    c["rope_cos"], c["rope_sin"] = lay(cos), lay(sin)
    i = np.arange(NL)
    m = np.where(np.abs(i[:, None] - i[None, :]) <= 128, 0.0, NEG).astype(np.float32)
    c["attn_mask"] = np.ascontiguousarray(m.reshape(LT, P, NL).transpose(1, 0, 2))
    t, s = i[:, None], i[None, :]
    seen = ((t - s >= 0) & (t - s <= 128)).astype(np.float32)
    for dilation in (4, 16):
        seen += (t >= s) & ((t - s) % dilation == 0)
    lay2 = lambda m: np.ascontiguousarray(m.reshape(LT, P, NL).transpose(1, 0, 2)).astype(np.float32)
    c["branch_count"], c["branch_bar"] = lay2(seen), lay2(np.where(seen > 0, 0.0, NEG))
    r = np.arange(P)
    c["causal"] = (r[:, None] <= r[None, :]).astype(np.float32)
    same = (r[:, None] // CCH == r[None, :] // CCH).astype(np.float32)
    c["chunk_sums"], c["chunk_ones"] = c["causal"] * same, same
    c["chunk_ends"] = np.ascontiguousarray(same[:, ::CCH])
    return c


def laid_out(i):
    a = {k: np.asarray(v) for k, v in i.items()}
    o = constants()
    o["x"], o["ctx"] = a["x"][0], a["ctx"][0]
    o["cc"] = np.ascontiguousarray(np.stack([a["c"][0], a["c_ctx"]]).reshape(2, KT, P).transpose(2, 1, 0))
    o["ada_w"] = np.concatenate([tiles_of(a["ada_w"][l]) for l in range(2)])
    o["ada_b"], o["ln_g"], o["ln_b"] = a["ada_b"], a["ln_g"], a["ln_b"]
    o["attn_w_in"] = tiles_of(a["attn_w_in"][0])
    o["attn_sink"] = a["attn_sink"]
    o["w_out0"], o["w_out1"] = tiles_of(a["w_out"][0], 2), tiles_of(a["w_out"][1], 2)
    s5 = {k: a["s5_" + k][0] for k in ("lam_re", "lam_im", "log_step", "b_re", "b_im", "c_re", "c_im")}
    o["s5_w_in"], o["s5_w_z"] = tiles_of(a["s5_w_in"][0][:, :E]), tiles_of(a["s5_w_in"][0][:, E:])
    twice = lambda m: np.concatenate([m, m])
    for k in ("lam_re", "lam_im"):
        o["s5_" + k] = twice(s5[k].transpose(2, 1, 0).reshape(SS, GD))
    o["s5_log_step"] = np.ascontiguousarray(s5["log_step"].T).reshape(1, GD)
    batched = lambda m: m.reshape(SS, NB, BD, SG).transpose(1, 0, 2, 3)
    b = {k: batched(s5[k].transpose(2, 1, 0, 3)) for k in ("b_re", "b_im")}
    c = {k: batched(s5[k].transpose(3, 1, 0, 2)) for k in ("c_re", "c_im")}
    both = lambda m, n: np.stack([np.concatenate([m, n], 1), np.concatenate([n, m], 1)], 2)
    o["s5_bab"], o["s5_cab"] = both(b["b_re"], b["b_im"]), both(c["c_re"], c["c_im"])
    o["s5_d"], o["s5_glu_b"] = a["s5_d"], a["s5_glu_b"]
    o["s5_glu_w"] = tiles_of(a["s5_glu_w"][0], 2)
    cols = lambda m: np.ascontiguousarray(m.reshape(m.shape[0], -1, P).transpose(0, 2, 1))
    o["norm_mix_g"], o["norm_ffn_g"] = cols(a["norm_mix_g_2"]), cols(a["norm_ffn_g_2"])
    o["ev_w_in"], o["ev_w_out"] = tiles_of(a["ev_w_in_2"][0]), tiles_of(a["ev_w_out_2"][0])
    o["ev_a_ln_g"], o["ev_a_ln_b"], o["ev_q_g"], o["ev_k_g"] = (a[f"ev_{k}_2"] for k in ("a_ln_g", "a_ln_b", "q_g", "k_g"))
    o["ev_a_wsT"] = np.ascontiguousarray(a["ev_a_ws_2"][0].transpose(2, 0, 1))
    o["ev_a_bsT"] = np.ascontiguousarray(a["ev_a_bs_2"][0].T)
    w = a["od_w_in_2"][0]
    wide = 2 * CK + 2 * CV
    o["od_w_in"], o["od_w_out"] = tiles_of(w[:, :wide]), tiles_of(a["od_w_out_2"][0])
    o["od_w_ga"] = np.ascontiguousarray(w[:, wide:].reshape(KT, P, CR).transpose(1, 0, 2))
    o["od_w_a2"], o["od_b_a"], o["od_head_g"] = a["od_w_a2_2"][0], a["od_b_a_2"], a["od_head_g_2"]
    for l in range(2):
        gu = np.stack([a["ffn_w_gate_2"][l], a["ffn_w_up_2"][l]])
        gu = gu.reshape(2, KT, P, FT // 2, 2 * P).transpose(3, 2, 0, 1, 4)
        o[f"ffn_gu{l}"] = np.ascontiguousarray(gu).reshape(FT // 2, P, KT * NW)
        o[f"ffn_down{l}"] = np.ascontiguousarray(a["ffn_w_down_2"][l].reshape(FT // 2, 2, P, DM).transpose(0, 2, 1, 3))
    cw = a["ffn_conv_w_2"].reshape(2, CONV, FT, P).transpose(0, 3, 2, 1)
    o["ffn_conv_w"], o["ffn_conv_b"] = np.ascontiguousarray(cw), cols(a["ffn_conv_b_2"])
    return o


def kernel(**inputs):
    import concourse.bacc as bacc
    from concourse.bass_utils import run_bass_kernel_spmd

    nc = bacc.Bacc("TRN2", target_bir_lowering=False, num_devices=1)
    arrays, d = {}, {}
    for name, a in laid_out(inputs).items():
        a = np.ascontiguousarray(a)
        arrays[f"in_{name}"] = a
        d[name] = nc.dram_tensor(f"in_{name}", a.shape, mybir.dt.from_np(a.dtype), kind="ExternalInput").ap()
    out = nc.dram_tensor("out_x", [1, NL, DM], F32, kind="ExternalOutput").ap()
    build(nc, d, out)
    r = run_bass_kernel_spmd(nc, [arrays], core_ids=[0])
    return r.results[0]["out_x"]
```
